# Optimizing a Trainium2 kernel written in Bass

```python
import jax
import jax.numpy as jnp
from jax import lax
import numpy as np

D_MODEL = 1024
BATCH = 1
SEQ = 256
DEPTH = 1

GRID_W = 64
CTX_LEN = 256
RMS_EPS = 1e-6
N_MOD = 6

NA_HEADS = 8
NA_HEAD_DIM = 64
NA_WIDTH = NA_HEADS * NA_HEAD_DIM
WIN_ROWS = 8
WIN_COLS = 16
NA_QCB = 16
NA_KCB = 32

HG_HEADS = 4
HG_DK = 128
HG_DV = 128
HG_KEY_WIDTH = HG_HEADS * HG_DK
HG_WIDTH = HG_HEADS * HG_DV
HG_CHUNK = 64

GQA_Q_HEADS = 8
GQA_KV_HEADS = 2
GQA_HEAD_DIM = 64
GQA_Q_WIDTH = GQA_Q_HEADS * GQA_HEAD_DIM
GQA_KV_WIDTH = GQA_KV_HEADS * GQA_HEAD_DIM
GQA_BLOCK = 128
ROPE_THETA = 10000.0

N_BRANCHES = 3
BRANCH_W = 512

N_GROUPS = 4
EXPERTS_PER_GROUP = 4
N_EXPERTS = N_GROUPS * EXPERTS_PER_GROUP
TOP_K = 2
EXPERT_HIDDEN = 512

IN_SPLITS = (NA_WIDTH, NA_WIDTH, NA_WIDTH,
             HG_KEY_WIDTH, HG_KEY_WIDTH, HG_KEY_WIDTH, HG_WIDTH, HG_WIDTH,
             GQA_Q_WIDTH, GQA_KV_WIDTH, GQA_KV_WIDTH,
             D_MODEL, D_MODEL, D_MODEL)
IN_COLS = 3 * NA_WIDTH + 3 * HG_KEY_WIDTH + 2 * HG_WIDTH + GQA_Q_WIDTH + 2 * GQA_KV_WIDTH + N_BRANCHES * D_MODEL

kernel_name = 'hybrid_na_hgrn2_gqa_hmoe_dit'

def rmsnorm(x, g):
    xf = x.astype(jnp.float32)
    y = xf * lax.rsqrt(jnp.mean(xf * xf, axis=-1, keepdims=True) + RMS_EPS)
    return (y * g.astype(jnp.float32)).astype(x.dtype)

def modulate(h, shift, scale):
    return h * (1 + scale) + shift

def split_heads(z, dh):
    return z.reshape(z.shape[:-1] + (z.shape[-1] // dh, dh))

def split_in(z):
    return jnp.split(z, np.cumsum(IN_SPLITS)[:-1].tolist(), axis=-1)

def axial_rope_tables(n_tokens, dtype):
    t = jnp.arange(n_tokens)
    pos = jnp.stack([t // GRID_W, t % GRID_W], axis=-1).astype(jnp.float32)
    n_freq = GQA_HEAD_DIM // 4
    inv_freq = jnp.power(ROPE_THETA, -jnp.arange(n_freq, dtype=jnp.float32) / n_freq)
    ang = pos[:, :, None] * inv_freq
    ang = jnp.concatenate([ang, ang], axis=-1)
    return jnp.cos(ang).astype(dtype), jnp.sin(ang).astype(dtype)

def apply_axial_rope(x, cos, sin):
    xa = x.reshape(x.shape[:-1] + (2, GQA_HEAD_DIM // 2))
    x1, x2 = jnp.split(xa, 2, axis=-1)
    rot = jnp.concatenate([-x2, x1], axis=-1)
    out = xa * cos[None, :, None] + rot * sin[None, :, None]
    return out.reshape(x.shape)

def grouped_attention(q, k, v):
    scale = q.shape[-1] ** -0.5
    s = jnp.einsum('bqgrd,bkgd->bgrqk', q, k).astype(jnp.float32) * scale
    p = jax.nn.softmax(s, axis=-1).astype(v.dtype)
    return jnp.einsum('bgrqk,bkgd->bqgrd', p, v)

def blocked_grouped_attention(q, k, v):
    B, L, G, R, hd = q.shape
    nb = L // GQA_BLOCK
    qb = q.reshape(B, nb, GQA_BLOCK, G, R, hd).transpose(1, 0, 2, 3, 4, 5)
    ob = lax.map(lambda qq: grouped_attention(qq, k, v), qb)
    return ob.transpose(1, 0, 2, 3, 4, 5).reshape(B, L, G, R, hd)

def neighbourhood_attention(q, k, v, k_ctx, v_ctx, rpb):
    B, L, H, hd = q.shape
    rows = L // GRID_W
    wr = min(WIN_ROWS, rows)
    ncb = GRID_W // NA_QCB
    n_loc = wr * NA_KCB
    scale = hd ** -0.5
    qg = q.reshape(B, rows, GRID_W, H, hd)
    kg = k.reshape(B, rows, GRID_W, H, hd)
    vg = v.reshape(B, rows, GRID_W, H, hd)
    qcol = np.arange(GRID_W).reshape(ncb, NA_QCB)
    kc0 = np.clip(np.arange(ncb) * NA_QCB - WIN_COLS // 2, 0, GRID_W - NA_KCB)
    kcol = kc0[:, None] + np.arange(NA_KCB)[None, :]
    c0 = np.clip(qcol - WIN_COLS // 2, 0, GRID_W - WIN_COLS)
    col_ok = (kcol[:, None, :] >= c0[:, :, None]) & (kcol[:, None, :] < c0[:, :, None] + WIN_COLS)
    dcol = kcol[:, None, :] - qcol[:, :, None] + WIN_COLS - 1
    mask = np.broadcast_to(col_ok[:, :, None, :], (ncb, NA_QCB, wr, NA_KCB)).reshape(ncb, NA_QCB, n_loc)
    rpb = rpb.astype(jnp.float32)

    def one_row(r):
        r0 = jnp.clip(r - wr // 2, 0, rows - wr)
        q_r = lax.dynamic_index_in_dim(qg, r, axis=1, keepdims=False)
        k_r = lax.dynamic_slice_in_dim(kg, r0, wr, axis=1)[:, :, kcol]
        v_r = lax.dynamic_slice_in_dim(vg, r0, wr, axis=1)[:, :, kcol]
        k_r = k_r.transpose(0, 2, 1, 3, 4, 5).reshape(B, ncb, n_loc, H, hd)
        v_r = v_r.transpose(0, 2, 1, 3, 4, 5).reshape(B, ncb, n_loc, H, hd)
        q_b = q_r.reshape(B, ncb, NA_QCB, H, hd)
        drow = r0 + jnp.arange(wr) - r + WIN_ROWS - 1
        bias = rpb[:, drow][:, :, dcol]
        bias = bias.transpose(0, 2, 3, 1, 4).reshape(H, ncb, NA_QCB, n_loc)
        s_loc = jnp.einsum('bjqhd,bjkhd->bhjqk', q_b, k_r).astype(jnp.float32) * scale + bias
        s_loc = jnp.where(mask, s_loc, -jnp.inf)
        s_ctx = jnp.einsum('bjqhd,bkhd->bhjqk', q_b, k_ctx).astype(jnp.float32) * scale
        p = jax.nn.softmax(jnp.concatenate([s_loc, s_ctx], axis=-1), axis=-1).astype(v.dtype)
        o = (jnp.einsum('bhjqk,bjkhd->bjqhd', p[..., :n_loc], v_r)
             + jnp.einsum('bhjqk,bkhd->bjqhd', p[..., n_loc:], v_ctx))
        return o.reshape(B, GRID_W, H, hd)

    o = lax.map(one_row, jnp.arange(rows))
    return o.transpose(1, 0, 2, 3, 4).reshape(B, L, H * hd)

def chunked_gated_scan(q, k, v, log_f, s0):
    B, L, H, _ = q.shape
    dv = v.shape[-1]
    n = L // HG_CHUNK

    def chunks(a):
        return a.reshape(B, n, HG_CHUNK, H, a.shape[-1]).transpose(1, 0, 3, 2, 4)

    tri = np.tril(np.ones((HG_CHUNK, HG_CHUNK), dtype=bool))[:, :, None]

    def step(S, inp):
        qc, kc, vc, gc = inp
        b = jnp.cumsum(gc, axis=2)
        decay = jnp.exp(jnp.where(tri, b[:, :, :, None, :] - b[:, :, None, :, :], -jnp.inf))
        a = jnp.einsum('bhtd,bhsd,bhtsd->bhts', qc, kc, decay)
        o = jnp.einsum('bhts,bhsv->bhtv', a, vc) + jnp.einsum('bhtd,bhdv->bhtv', qc * jnp.exp(b), S)
        b_last = b[:, :, -1:, :]
        S = jnp.exp(b_last)[:, :, 0, :, None] * S + jnp.einsum('bhsd,bhsv->bhdv', kc * jnp.exp(b_last - b), vc)
        return S, o

    s_fin, o = lax.scan(step, s0, (chunks(q), chunks(k), chunks(v), chunks(log_f)))
    return o.transpose(1, 0, 3, 2, 4).reshape(B, L, H, dv), s_fin

def hgrn2_scans(q_raw, ff_raw, fb_raw, i_raw, lb, s_fwd, s_bwd):
    q = split_heads(jax.nn.silu(q_raw.astype(jnp.float32)), HG_DK)
    v = split_heads(i_raw.astype(jnp.float32), HG_DV)

    def forget(f_raw, lower):
        f = lower + (1.0 - lower) * jax.nn.sigmoid(f_raw.astype(jnp.float32))
        return split_heads(1.0 - f, HG_DK), split_heads(jnp.log(f), HG_DK)

    k_f, g_f = forget(ff_raw, lb[0])
    k_b, g_b = forget(fb_raw, lb[1])
    rev = lambda a: jnp.flip(a, axis=1)
    o_f, s_fwd = chunked_gated_scan(q, k_f, v, g_f, s_fwd)
    o_b, s_bwd = chunked_gated_scan(rev(q), rev(k_b), rev(v), rev(g_b), s_bwd)
    return o_f + rev(o_b), s_fwd, s_bwd

def hgrn2_readout(o, g_raw, norm_g):
    y = rmsnorm(o, norm_g) * jax.nn.silu(split_heads(g_raw, HG_DV).astype(jnp.float32))
    return y.reshape(o.shape[:2] + (HG_WIDTH,)).astype(g_raw.dtype)

def group_queries(q):
    return q.reshape(q.shape[:2] + (GQA_KV_HEADS, GQA_Q_HEADS // GQA_KV_HEADS, GQA_HEAD_DIM))

def branch_merge(branches, gate_logits, w_branch, w_out):
    y = 0
    for i in range(N_BRANCHES):
        y = y + jax.nn.sigmoid(gate_logits[i]) * (branches[i] @ w_branch[i])
    return y @ w_out

def token_mixer(h_lat, h_ctx, w_in, rpb, lb, hg_norm_g, q_norm_g, k_norm_g, w_branch, w_out, cos, sin, with_ctx):
    B, L, _ = h_lat.shape
    n_ctx = h_ctx.shape[1]
    zl = split_in(h_lat @ w_in)
    zc = split_in(h_ctx @ w_in)
    na_q, na_k, na_v = [split_heads(z, NA_HEAD_DIM) for z in zl[0:3]]
    na_qc, na_kc, na_vc = [split_heads(z, NA_HEAD_DIM) for z in zc[0:3]]
    a_lat = neighbourhood_attention(na_q, na_k, na_v, na_kc, na_vc, rpb)
    s0 = jnp.zeros((B, HG_HEADS, HG_DK, HG_DV), jnp.float32)
    o_ctx, s_fwd, s_bwd = hgrn2_scans(zc[3], zc[4], zc[5], zc[6], lb, s0, s0)
    o_lat, _, _ = hgrn2_scans(zl[3], zl[4], zl[5], zl[6], lb, s_fwd, s_bwd)
    b_lat = hgrn2_readout(o_lat, zl[7], hg_norm_g)
    q_lat = apply_axial_rope(rmsnorm(split_heads(zl[8], GQA_HEAD_DIM), q_norm_g), cos, sin)
    k_lat = apply_axial_rope(rmsnorm(split_heads(zl[9], GQA_HEAD_DIM), k_norm_g), cos, sin)
    q_ctx = rmsnorm(split_heads(zc[8], GQA_HEAD_DIM), q_norm_g)
    k_ctx = rmsnorm(split_heads(zc[9], GQA_HEAD_DIM), k_norm_g)
    v_lat = split_heads(zl[10], GQA_HEAD_DIM)
    v_ctx = split_heads(zc[10], GQA_HEAD_DIM)
    k_all = jnp.concatenate([k_ctx, k_lat], axis=1)
    v_all = jnp.concatenate([v_ctx, v_lat], axis=1)
    c_lat = blocked_grouped_attention(group_queries(q_lat), k_all, v_all).reshape(B, L, GQA_Q_WIDTH)
    y_lat = branch_merge((a_lat, b_lat, c_lat), zl[11:14], w_branch, w_out)
    if not with_ctx:
        return y_lat, None
    a_ctx = grouped_attention(na_qc[:, :, :, None, :], na_kc, na_vc).reshape(B, n_ctx, NA_WIDTH)
    b_ctx = hgrn2_readout(o_ctx, zc[7], hg_norm_g)
    c_ctx_out = grouped_attention(group_queries(q_ctx), k_ctx, v_ctx).reshape(B, n_ctx, GQA_Q_WIDTH)
    y_ctx = branch_merge((a_ctx, b_ctx, c_ctx_out), zc[11:14], w_branch, w_out)
    return y_lat, y_ctx

def hierarchical_moe(h, w_gr, b_gr, w_er, b_er, w_gate, w_up, w_down):
    n = h.shape[0]
    g_logits = (h @ w_gr + b_gr).astype(jnp.float32)
    g_val, g_idx = lax.top_k(g_logits, 1)
    p_group = jnp.exp(g_val - jax.nn.logsumexp(g_logits, axis=-1, keepdims=True))
    e_logits = (h @ w_er + b_er).astype(jnp.float32).reshape(n, N_GROUPS, EXPERTS_PER_GROUP)
    e_in = jnp.take_along_axis(e_logits, g_idx[:, :, None], axis=1)[:, 0]
    e_val, e_idx = lax.top_k(e_in, TOP_K)
    w_sel = jax.nn.softmax(e_val, axis=-1) * p_group
    expert_id = g_idx * EXPERTS_PER_GROUP + e_idx
    combine = jnp.einsum('nk,nke->ne', w_sel, jax.nn.one_hot(expert_id, N_EXPERTS, dtype=jnp.float32)).astype(h.dtype)
    y = jnp.zeros_like(h)
    for e in range(N_EXPERTS):
        he = jax.nn.silu(h @ w_gate[e]) * (h @ w_up[e])
        y = y + combine[:, e:e + 1] * (he @ w_down[e])
    return y

def setup_inputs(seed: int = 0) -> dict:
    key = jax.random.key(seed)
    ks = iter(jax.random.split(key, 32))
    d = D_MODEL

    def nrm(shape, s):
        return jax.random.normal(next(ks), shape, jnp.float32) * s

    return {
        'x': nrm((BATCH, SEQ, d), 1.0),
        'c': nrm((BATCH, d), 1.0),
        'ctx': nrm((BATCH, CTX_LEN, d), 1.0),
        'c_ctx': nrm((d,), 1.0),
        'w_ada': nrm((DEPTH, d, N_MOD * d), 0.5 * d ** -0.5),
        'b_ada': nrm((DEPTH, N_MOD * d), 0.02),
        'g_mix': 1.0 + nrm((DEPTH, d), 0.1),
        'g_ffn': 1.0 + nrm((DEPTH, d), 0.1),
        'w_in': nrm((DEPTH, d, IN_COLS), d ** -0.5),
        'na_rpb': nrm((DEPTH, NA_HEADS, 2 * WIN_ROWS - 1, 2 * WIN_COLS - 1), 0.1),
        'hg_lb_logits': nrm((DEPTH, 2, HG_KEY_WIDTH), 1.0),
        'hg_norm_g': 1.0 + nrm((DEPTH, HG_DV), 0.1),
        'gqa_qnorm_g': 1.0 + nrm((DEPTH, GQA_HEAD_DIM), 0.1),
        'gqa_knorm_g': 1.0 + nrm((DEPTH, GQA_HEAD_DIM), 0.1),
        'w_branch': nrm((DEPTH, N_BRANCHES, BRANCH_W, d), BRANCH_W ** -0.5),
        'w_out': nrm((DEPTH, d, d), d ** -0.5),
        'w_group_router': nrm((DEPTH, d, N_GROUPS), d ** -0.5),
        'b_group_router': nrm((DEPTH, N_GROUPS), 0.01),
        'w_expert_router': nrm((DEPTH, d, N_EXPERTS), d ** -0.5),
        'b_expert_router': nrm((DEPTH, N_EXPERTS), 0.01),
        'w_exp_gate': nrm((DEPTH, N_EXPERTS, d, EXPERT_HIDDEN), d ** -0.5),
        'w_exp_up': nrm((DEPTH, N_EXPERTS, d, EXPERT_HIDDEN), d ** -0.5),
        'w_exp_down': nrm((DEPTH, N_EXPERTS, EXPERT_HIDDEN, d), EXPERT_HIDDEN ** -0.5),
        'g_final': 1.0 + nrm((d,), 0.1),
    }

def reference(x, c, ctx, c_ctx, w_ada, b_ada, g_mix, g_ffn, w_in, na_rpb, hg_lb_logits, hg_norm_g,
              gqa_qnorm_g, gqa_knorm_g, w_branch, w_out, w_group_router, b_group_router,
              w_expert_router, b_expert_router, w_exp_gate, w_exp_up, w_exp_down, g_final):
    B, L, d = x.shape
    cos, sin = axial_rope_tables(L, x.dtype)
    p_lb = jax.nn.softmax(hg_lb_logits.astype(jnp.float32), axis=0)
    lower_bounds = jnp.cumsum(p_lb, axis=0) - p_lb[0:1]
    silu_c = jax.nn.silu(c)
    silu_cc = jax.nn.silu(c_ctx)[None, :]
    for l in range(DEPTH):
        last = l == DEPTH - 1
        mod = jnp.split((silu_c @ w_ada[l] + b_ada[l])[:, None, :], N_MOD, axis=-1)
        mod_c = jnp.split((silu_cc @ w_ada[l] + b_ada[l])[:, None, :], N_MOD, axis=-1)
        h_lat = modulate(rmsnorm(x, g_mix[l]), mod[0], mod[1])
        h_ctx = modulate(rmsnorm(ctx, g_mix[l]), mod_c[0], mod_c[1])
        y_lat, y_ctx = token_mixer(h_lat, h_ctx, w_in[l], na_rpb[l], lower_bounds[l], hg_norm_g[l],
                                   gqa_qnorm_g[l], gqa_knorm_g[l], w_branch[l], w_out[l], cos, sin, not last)
        x = x + mod[2] * y_lat
        f_lat = modulate(rmsnorm(x, g_ffn[l]), mod[3], mod[4]).reshape(-1, d)
        if last:
            y = hierarchical_moe(f_lat, w_group_router[l], b_group_router[l], w_expert_router[l],
                                 b_expert_router[l], w_exp_gate[l], w_exp_up[l], w_exp_down[l])
            x = x + mod[5] * y.reshape(x.shape)
        else:
            ctx = ctx + mod_c[2] * y_ctx
            f_ctx = modulate(rmsnorm(ctx, g_ffn[l]), mod_c[3], mod_c[4]).reshape(-1, d)
            n_lat = f_lat.shape[0]
            y = hierarchical_moe(jnp.concatenate([f_lat, f_ctx], axis=0), w_group_router[l], b_group_router[l],
                                 w_expert_router[l], b_expert_router[l], w_exp_gate[l], w_exp_up[l], w_exp_down[l])
            x = x + mod[5] * y[:n_lat].reshape(x.shape)
            ctx = ctx + mod_c[5] * y[n_lat:].reshape(ctx.shape)
    return rmsnorm(x, g_final)


_drawn_inputs = setup_inputs


def setup_inputs(seed=0):
    import zlib

    import numpy as np

    out = dict(_drawn_inputs(seed))
    spreads = {}
    factors = {'b_ada': 3.642,
     'g_mix': 2.972,
     'na_rpb': 8.0,
     'hg_norm_g': 4.031,
     'gqa_qnorm_g': 8.0,
     'gqa_knorm_g': 8.0,
     'b_group_router': 53.874,
     'b_expert_router': 64.0,
     'g_ffn': 4.481}
    for name, (base, spread) in spreads.items():
        noise = np.random.default_rng([zlib.crc32(name.encode()), seed]).standard_normal(out[name].shape)
        drawn = base * np.exp(spread * noise) if base else spread * noise
        out[name] = jnp.asarray(drawn.astype(out[name].dtype))
    for name, factor in factors.items():
        out[name] = (out[name] * factor).astype(out[name].dtype)
    return out
```

```python
import numpy as np
import concourse.bass as bass
from concourse import mybir
from concourse.alu_op_type import AluOpType as ALU
from contextlib import ExitStack

F32 = mybir.dt.float32
I32 = mybir.dt.int32
I8 = mybir.dt.int8
ACT = mybir.ActivationFunctionType
AX = mybir.AxisListType

P = 128
D = 1024
KD = D // P
L = 256
NT = L // P
GRID = 64
ROWS = L // GRID
WR, WC = 8, 16
HD = 64
NH = 8
HGH = 4
NE = 16
NG = 4
EPG = NE // NG
EH = 512
KH = EH // P
CAP = 64
PAIRS = NE // 2
MAXPASS = L // CAP
EPS = 1e-6
QSCALE = HD ** -0.5
NEG = -1e30
RB = ROWS + 2
ROUTES = NG + NE

FRONT = ["ada0", "ada1", "ada2", "ada3", "ff", "fb", "hq", "hg", "hi", "nk", "nq", "nv", "gq", "gkv"]
FRONT += [f"gate{i}" for i in range(6)] + [f"ada{i}" for i in range(4, 12)]
FRONT += ["br0", "br1", "br2", "out0", "out1"]
FSLOTS = 3
SLOTS = 6
SLOT = 4096
FUSES = len(FRONT) // FSLOTS
assert FUSES * FSLOTS == len(FRONT)



def group_fills(name):
    if name[:3] == "ada":
        n = 1
    elif name in ("ff", "fb", "hi", "nk", "nv"):
        n = 4
    elif name[:2] in ("br",):
        n = 4
    else:
        n = 2
    return [(name, i, "dve" if name[:2] in ("br", "ou") else "act") for i in range(n)]


FILLS = [f for g in FRONT[:28] for f in group_fills(g)]
FILLS += [("row2", i, "act") for i in range(2)] + [("row5", i, "act") for i in range(2)]
FILLS += [f for g in FRONT[28:] for f in group_fills(g)]
PBANKS = 3


def fill_no(name, i=0):
    return [f[:2] for f in FILLS].index((name, i))


def emptied(n):
    who = FILLS[n][2]
    return who, sum(f[2] == who for f in FILLS[:n + 1])


LEVELS = 8
UNITS = [(k, t, h) for k in ("na", "gq") for t in range(NT) for h in range(NH)]
SHARED = [("kc", i) for i in range(4)]
SHARED += [(f"lev{v}", i) for v in range(LEVELS) for i in range(4)] + [("s0", i) for i in range(2)]
SHARED += [("lev8", i) for i in range(2)] + [("o", i) for i in range(2)] + [("osq", i) for i in range(2)]
SHARED += [("gqT", i) for i in range(2)] + [("gkT", 0)]
STEPS = len(UNITS) + 3
AT_STEP = 2 * NH * NT // 2 + 5


def step_shared(i):
    out = [("pT", i - 1)] if 1 <= i <= len(UNITS) else []
    if i == AT_STEP:
        out += [("aT", 0), ("aT", 1)]
    return out


SHARED += [f for i in range(STEPS) for f in step_shared(i)]
SHARED += [("cT", 0), ("cT", 1)] + [("fT", i) for i in range(4)] + [("sT", i) for i in range(4)]


def shared_no(name, i=0):
    return SHARED.index((name, i))


FILLER = [n for n, f in enumerate(FILLS) if f[0][:4] == "gate" or (f[0][:3] == "ada" and int(f[0][3:]) >= 4)]
FILLER_AT = {i: [] for i in range(STEPS)}
for _j, _n in enumerate(FILLER):
    FILLER_AT[_j * STEPS // len(FILLER)].append(_n)
GATE_FILLS = fill_no("gate5", 1)


def build(nc, d):
    ctx = ExitStack()
    with ctx:
        TOTAL = 52740
        sb = ctx.enter_context(nc.sbuf_tensor("sb", [P, TOTAL], F32))
        banks = [ctx.enter_context(nc.psum_tensor(f"bank{i}", [P, 512], F32)) for i in range(8)]
        proj = banks[0:3]
        shared = banks[3:5]
        score = banks[5:7]
        pv_bank = banks[7]

        def at(start, *dims):
            n = int(np.prod(dims))
            v = sb[:, start:start + n]
            if len(dims) == 2:
                v = v.rearrange("p (a b) -> p a b", b=dims[1])
            if len(dims) == 3:
                v = v.rearrange("p (a b c) -> p a b c", b=dims[1], c=dims[2])
            return v

        slot = [at(i * SLOT, SLOT) for i in range(SLOTS)]
        A0 = FSLOTS * SLOT
        na_k = at(A0, 4, 2 * L)
        na_v = at(A0 + 2048, 4, 512)
        sig_q, sig_g = at(A0 + 2048, 4, L), at(A0 + 3072, 4, L)
        na_bias = at(A0 + 4096, NH, RB * GRID)
        X = at(A0 + 7168, 8, L)
        Y = at(A0 + 9216, 8, L)
        sq = at(A0 + 7168, KD, 512)
        probs = at(A0 + 7168, 2, 512)
        probsT = at(A0 + 8192, 2, 512)
        a_nat = at(A0 + 9216, NT, 512)
        gkv = at(A0 + 11264, 4, 256)
        B0 = A0 + (SLOTS - FSLOTS) * SLOT
        hT = at(B0, KD, 2 * L)
        xn, fT = at(B0, NT, D), at(B0 + 2048, KD, L)
        F0 = B0 + 4096
        T_lat = at(F0, 8, L)
        masks_wide = at(F0, 2 * (LEVELS - 1), P)
        forget = at(F0, 2, 8, L)
        F_ctx = at(F0 + 2048, 8, L)
        Kc = at(F0 + 4096, 8, L)
        kcn = at(F0 + 6144, 8, L)
        g_sq = at(F0 + 4096, 1536)
        g_rot = at(F0 + 4096, NT, 512)
        k_rot = at(F0 + 5120, NT, 128)
        gates = at(F0 + 2048, 3 * KD, L)
        o_sb, o_tmp = at(F0, 4, L), at(F0 + 1024, 4, L)
        SW = at(F0, NT, NE * CAP)
        yacc = at(F0 + 2048, NT, D)
        S_all = at(F0 + 4096, NT, NE * CAP)
        ST_all = at(F0 + 6144, PAIRS, NT * P)
        C0 = F0 + 8192
        T_alt = at(C0, 1024)
        rstd_row = at(C0, 512)
        QR = at(C0 + 1024, 4, L)
        row5 = at(C0 + 1024, D)
        v_hg = at(C0 + 2048, 4, 512)
        x_nat = at(C0 + 2048, NT, D)
        AT = at(C0 + 4096, 6, 512)
        yT = at(C0 + 4096, KD, L)
        diag = at(C0 + 6144, KD, P)
        h_sb = at(C0 + 4096, KD, P)
        y_sb = at(C0 + 5120, D)
        he = at(C0 + 6144, 2, KH * CAP)
        sl = at(C0 + 6656, 2, KH * CAP)
        S0 = at(C0 + 7168, 8, P)
        row2 = at(C0 + 7168, D)
        bT = at(C0 + 8192, 4, L)
        na_q = at(C0 + 9216, 4, L)
        aT = na_q
        S_now, ST_now = at(C0 + 9216, NT, P), at(C0 + 9472, NT, P)
        gq = at(C0 + 10240, NT, 512)
        c_nat = gq
        gqT = at(C0 + 11264, 4, L)
        cT = gqT
        g_last = at(C0 + 11264, D)
        gkT = at(C0 + 12288, 512)
        E0 = C0 + 12800
        consts = {}
        pos = [E0]

        def keep(n, *dims):
            v = at(pos[0], *dims) if dims else at(pos[0], n)
            pos[0] += n
            assert pos[0] <= TOTAL, pos[0]
            return v

        small = keep(SMALL)
        def sm(name):
            o, dims = SM[name]
            return small[:, o:o + int(np.prod(dims))] if len(dims) == 1 else at(E0 + o, *dims)
        ident, ones, below, slots_iota = sm("ident"), sm("ones"), sm("below"), sm("iota")
        cvec = keep(16, KD, 2)
        mod = keep(96, 48, 2)
        A_mix, A_ffn = keep(16, KD, 2), keep(8)
        lower, span = keep(8), keep(8)
        lb_e, lb_p = keep(8), keep(8)
        g_ms = keep(24)
        qcos, qsin = keep(128, NT, HD), keep(128, NT, HD)
        kcos, ksin = keep(128, NT, HD), keep(128, NT, HD)
        nmax = keep(32)
        psum_ = keep(32)
        stat = keep(8)
        zeros = keep(256)
        r_g, r_e = keep(8, NT, NG), keep(32, NT, NE)
        r_gm, r_gs, r_sm = keep(2), keep(2), keep(2)
        r_m1, r_m2, r_w1, r_w2, r_d = keep(2), keep(2), keep(2), keep(2), keep(2)
        r_t, r_sel, r_eg = keep(8, NT, NG), keep(8, NT, NG), keep(8, NT, NG)
        r_em, r_et = keep(32, NT, NE), keep(32, NT, NE)
        oh1, oh2 = keep(32, NT, NE), keep(32, NT, NE)
        member, comb, posm = keep(32, NT, NE), keep(32, NT, NE), keep(32, NT, NE)
        counts, count, over = keep(16), keep(1), keep(3)
        passes_f = keep(1)
        masks = ctx.enter_context(nc.sbuf_tensor("masks", [P, 2 * (LEVELS - 1), P], I8))
        passes = ctx.enter_context(nc.sbuf_tensor("passes", [1, 1], I32))

        def sem(name):
            return ctx.enter_context(nc.semaphore(name))

        x_in = [sem("x_in0"), sem("x_in1")]
        c_in, small_in, bias_in, masks_in, xnat_in, glast_in = [sem(n) for n in (
            "c_in", "small_in", "bias_in", "masks_in", "xnat_in", "glast_in")]
        w_in_ = [sem(f"weights_in{i}") for i in range(SLOTS)]
        w_used = sem("weights_used")
        fill_ready = sem("fill_ready")
        out_by = {"act": sem("fill_out_act"), "dve": sem("fill_out_dve")}
        shared_ready, shared_out = sem("shared_ready"), sem("shared_out")
        masks_ready = sem("masks_ready")
        sq_ready, rms_ready, rms_root, c_ready = sem("sq_ready"), sem("rms_ready"), sem("rms_root"), sem("c_ready")
        h_ready = sem("h_ready")
        lb_in, lb_ready = sem("lb_in"), sem("lb_ready")
        silu_hg = sem("silu_hg")
        kc_ready = sem("kc_ready")
        xy_ready = sem("xy_ready")
        hg_read = sem("hg_read")
        o_sq, o_root, b_ready = sem("o_sq"), sem("o_root"), sem("b_ready")
        g_sum, g_root, g_rec, gqa_ready = sem("g_sum"), sem("g_root"), sem("g_rec"), sem("gqa_ready")
        g_tab = sem("g_tab")
        scores_ready, max_ready, exp_ready = sem("scores_ready"), sem("max_ready"), sem("exp_ready")
        pv_ready, pv_out = sem("pv_ready"), sem("pv_out")
        sig_gates = sem("sig_gates")
        modb_ready, diag_ready, diag_used = sem("modb_ready"), sem("diag_ready"), sem("diag_used")
        x1_ready, x1_sum, x1_root, xn_ready = sem("x1_ready"), sem("x1_sum"), sem("x1_root"), sem("xn_ready")
        logits_ready, gexp_in, gexp_out = sem("logits_ready"), sem("gexp_in"), sem("gexp_out")
        member_ready, pos_ready, passes_ready = sem("member_ready"), sem("pos_ready"), sem("passes_ready")
        slots_ready = sem("slots_ready")
        cut_ready, cut_used = sem("cut_ready"), sem("cut_used")
        gather_ready, h_out = sem("gather_ready"), sem("h_out")
        gu_ready, silu_ready, he_ready = sem("gu_ready"), sem("silu_ready"), sem("he_ready")
        down_ready, y_out = sem("down_ready"), sem("y_out")
        scat_ready, scat_out = sem("scat_ready"), sem("scat_out")
        fin_sum, fin_root, fin_ready, stored = sem("fin_sum"), sem("fin_root"), sem("fin_ready"), sem("stored")
        v_step, p_step, a_step = sem("vector_step"), sem("pool_step"), sem("scalar_step")

        block = ctx.enter_context(nc.Block())

        def wait_emptied(eng, n):
            who, count_ = emptied(n)
            eng.wait_ge(out_by[who], count_)

        def slot_value(s):
            return 16 * FUSES if s < FSLOTS else 0

        @block.sync
        def _(sp):
            for i in range(2):
                sp.dma_start(hT[:, 4 * i:4 * i + 4, :], d["xcT"][:, 4 * i:4 * i + 4, :]).then_inc(x_in[i], 16)
            for n, name in enumerate(FRONT):
                if n >= FSLOTS:
                    sp.wait_ge(w_used, n - FSLOTS + 1)
                cols = SLOT // 2 if name == "gkv" else SLOT
                sp.dma_start(slot[n % FSLOTS][:, 0:cols], d["front_w"][n, :, 0:cols]).then_inc(w_in_[n % FSLOTS], 16)
                if name == "nq":
                    sp.dma_start(na_bias, d["na_bias"]).then_inc(bias_in, 16)
                if name == "gate4":
                    sp.wait_ge(shared_out, shared_no("o", 1) + 1)
                    sp.dma_start(x_nat, d["x_nat"]).then_inc(xnat_in, 16)

            def load(s, row):
                sp.dma_start(slot[s], d["expert_w"][bass.ds(row, 1), :, :].rearrange("a p n -> p (a n)")
                             if not isinstance(row, int) else d["expert_w"][row, :, :]).then_inc(w_in_[s], 16)

            def load_pair(before, j, first=False):
                for q, (s, part) in enumerate(((0, 0), (1, 1), (3, 3), (4, 4), (2, 2), (5, 5))):
                    if first and s < FSLOTS:
                        sp.wait_ge(w_used, len(FRONT) - FSLOTS + s + 1)
                    elif first:
                        sp.wait_ge(shared_out, shared_no("cT", 1) + 1)
                    else:
                        sp.wait_ge(gu_ready if part % 3 < 2 else down_ready, before * 2 + 1 + s // 3)
                    load(s, j * 6 + part)

            load_pair(0, 0, first=True)
            with sp.Fori(0, PAIRS - 1) as j:
                load_pair(j, j + 1)
            sp.wait_ge(passes_ready, 2)
            n_pass = sp.value_load(passes[0:1, 0:1], min_val=1, max_val=MAXPASS)
            with sp.If(n_pass > 1):
                with sp.Fori(0, n_pass - 1) as p:
                    with sp.Fori(0, PAIRS) as j:
                        load_pair(p * PAIRS + j + (PAIRS - 1), j)
            sp.wait_ge(fin_ready, 1)
            for t in range(NT):
                if t:
                    sp.wait_ge(fin_ready, t + 1)
                sp.dma_start(d["out"][t * P:(t + 1) * P, :], yacc[:, t, :]).then_inc(stored, 16)
            sp.wait_ge(stored, 16 * NT)

        @block.gpsimd
        def _(pool):
            steps = [0]

            def link(ins):
                steps[0] += 1
                ins.then_inc(p_step, 1)
                pool.wait_ge(p_step, steps[0])

            pool.wait_ge(masks_in, 16)
            pool.tensor_copy(masks[:, :, :], masks_wide).then_inc(masks_ready, 1)
            pool.wait_ge(small_in, 16)
            for c_, s_, g in ((qcos, qsin, "gqn"), (kcos, ksin, "gkn")):
                gn = sm(g).unsqueeze(1).broadcast_to([P, NT, HD])
                gs = sm(g + "_swapped").unsqueeze(1).broadcast_to([P, NT, HD])
                pool.tensor_tensor(c_, sm("cos"), gn, ALU.mult)
                last = pool.tensor_tensor(s_, sm("sin"), gs, ALU.mult)
            last.then_inc(g_tab, 1)

            pool.wait_ge(g_tab, 1)
            pool.wait_ge(g_rec, 1)
            rq = g_ms[:, 0:16].unsqueeze(2).broadcast_to([P, 16, HD])
            rk = g_ms[:, 16:24].rearrange("p (a b) -> p a b", b=2).unsqueeze(3).broadcast_to([P, 4, 2, HD])
            q16 = gq.rearrange("p t (h c) -> p (t h) c", c=HD)
            k4 = gkv[:, :, 0:128].rearrange("p t (h c) -> p t h c", c=HD)
            link(pool.tensor_tensor(q16, q16, rq, ALU.mult))
            link(pool.tensor_tensor(k4, k4, rk, ALU.mult))
            for x, rot, c_, s_, nh in ((gq, g_rot, qcos, qsin, NH), (gkv, k_rot, kcos, ksin, 2)):
                for t in range(NT):
                    xv = x[:, t, 0:nh * HD].rearrange("p (h a f c) -> p h a f c", a=2, f=2, c=16)
                    rv = rot[:, t, :].rearrange("p (h a f c) -> p h a f c", a=2, f=2, c=16)
                    sv = s_[:, t, :].rearrange("p (a f c) -> p a f c", a=2, f=2)
                    for f in range(2):
                        ins = pool.tensor_tensor(rv[:, :, :, f, :], xv[:, :, :, 1 - f, :],
                                                 sv[:, :, f, :].unsqueeze(1).broadcast_to([P, nh, 2, 16]), ALU.mult)
                    link(ins)
                    xh = x[:, t, 0:nh * HD].rearrange("p (h c) -> p h c", c=HD)
                    link(pool.tensor_tensor(xh, xh, c_[:, t, :].unsqueeze(1).broadcast_to([P, nh, HD]), ALU.mult))
                    link(pool.tensor_tensor(x[:, t, 0:nh * HD], x[:, t, 0:nh * HD], rot[:, t, :], ALU.add))
            kx = gkv[:, NT:4, 0:128].rearrange("p t (h c) -> p t h c", c=HD)
            gk = sm("gkn").unsqueeze(1).unsqueeze(1).broadcast_to([P, 2, 2, HD])
            pool.tensor_tensor(kx, kx, gk, ALU.mult).then_inc(gqa_ready, 1)

            pool.wait_ge(modb_ready, 1)
            pool.wait_ge(shared_out, shared_no("o", 1) + 1)
            for r, m in enumerate((2, 5)):
                if r:
                    pool.wait_ge(diag_used, 1)
                for k in range(KD):
                    last = pool.tensor_scalar(diag[:, k, :], ident, mod[:, m * KD + k, 0:1], None, ALU.mult)
                last.then_inc(diag_ready, 1)

            def cut(n, j, first):
                if not first:
                    pool.wait_ge(gather_ready, n)
                src = S_all[:, :, bass.ds(j * P, P)]
                pool.tensor_copy(S_now, src).then_inc(cut_ready, 1)
                if not first:
                    pool.wait_ge(scat_ready, 4 * n)
                srcT = ST_all[:, bass.ds(j, 1), :].rearrange("p a (t c) -> p (a t) c", t=NT)
                pool.tensor_copy(ST_now, srcT).then_inc(cut_ready, 1)

            pool.wait_ge(slots_ready, 2)
            cut(0, 0, True)
            with pool.Fori(1, PAIRS) as j:
                cut(j, j, False)
            pool.wait_ge(passes_ready, 2)
            n_pass = pool.value_load(passes[0:1, 0:1], min_val=1, max_val=MAXPASS)
            with pool.If(n_pass > 1):
                with pool.Fori(1, n_pass) as p:
                    with pool.Fori(0, PAIRS) as j:
                        pool.wait_ge(slots_ready, 2 * p + 2)
                        cut(p * PAIRS + j, j, False)
            pool.nop()

        @block.scalar
        def _(act):
            act.dma_start(cvec, d["cvec"]).then_inc(c_in, 16)
            act.dma_start(small, d["small_w"]).then_inc(small_in, 16)
            act.dma_start(masks_wide, d["level_masks"]).then_inc(masks_in, 16)
            act.wait_ge(c_in, 16)
            act.activation(cvec, cvec, ACT.Silu).then_inc(c_ready, 1)
            for k in range(KD):
                if k % 4 == 0:
                    act.wait_ge(x_in[k // 4], 16)
                act.activation(sq[:, k, :], hT[:, k, :], ACT.Square).then_inc(sq_ready, 1)
            act.wait_ge(rms_ready, 1)
            act.wait_ge(small_in, 16)
            act.activation(rstd_row, pv_bank[:, :], ACT.Sqrt, bias=sm("eps"), scale=1.0 / D).then_inc(rms_root, 1)

            act.wait_ge(lb_in, 1)
            act.activation(lb_e, lb_e, ACT.Exp).then_inc(lb_ready, 1)

            def fill(n):
                name, i, who = FILLS[n]
                assert who == "act"
                ps = proj[n % PBANKS]
                act.wait_ge(fill_ready, n + 1)
                two = ps[:, :].rearrange("p (a b) -> p a b", a=2)
                done = out_by["act"]
                if name[:3] == "ada":
                    g = int(name[3:])
                    act.activation(mod[:, 4 * g:4 * g + 4, :], ps[:, 0:8].rearrange("p (a b) -> p a b", b=2),
                                   ACT.Copy).then_inc(done, 1)
                elif name in ("ff", "fb"):
                    if (name, i) == ("ff", 0):
                        act.wait_ge(masks_ready, 1)
                    act.activation(forget[:, :, 4 * (name == "fb") + i, :], two, ACT.Sigmoid).then_inc(done, 1)
                elif name in ("hq", "hg"):
                    raw, sig = (QR, sig_q) if name == "hq" else (bT, sig_g)
                    act.activation(raw[:, 2 * i:2 * i + 2, :], two, ACT.Copy)
                    act.activation(sig[:, 2 * i:2 * i + 2, :], two, ACT.Sigmoid).then_inc(done, 1)
                elif name == "hi":
                    act.activation(v_hg[:, i, :], ps[:, :], ACT.Copy).then_inc(done, 1)
                elif name == "nk":
                    act.activation(na_k[:, i, :], ps[:, :], ACT.Copy).then_inc(done, 1)
                elif name == "nq":
                    act.activation(na_q[:, 2 * i:2 * i + 2, :], two, ACT.Copy, scale=QSCALE).then_inc(done, 1)
                elif name == "nv":
                    if i == 0:
                        act.wait_ge(silu_hg, 2)
                    act.activation(na_v[:, i, :], ps[:, :], ACT.Copy).then_inc(done, 1)
                elif name == "gq":
                    act.activation(gq[:, i, :], ps[:, :], ACT.Copy).then_inc(done, 1)
                elif name == "gkv":
                    act.activation(gkv[:, 2 * i:2 * i + 2, :], two, ACT.Copy).then_inc(done, 1)
                elif name[:4] == "gate":
                    c = 4 * int(name[4:]) + 2 * i
                    if c == 0:
                        act.wait_ge(gqa_ready, 1)
                        act.wait_ge(shared_out, shared_no("s0", 1) + 1)
                    act.activation(gates[:, c:c + 2, :], two, ACT.Copy).then_inc(done, 1)
                elif name in ("row2", "row5"):
                    act.activation((row2 if name == "row2" else row5)[:, 512 * i:512 * i + 512], ps[:, :],
                                   ACT.Copy).then_inc(done, 1)

            for n in range(fill_no("gq", 1) + 1):
                fill(n)
            act.wait_ge(shared_out, shared_no("o", 1) + 1)
            act.activation(o_tmp, o_sb, ACT.Square).then_inc(o_sq, 1)
            for i in range(2):
                act.wait_ge(shared_ready, shared_no("osq", i) + 1)
                act.activation(o_tmp[:, 2 * i:2 * i + 2, :],
                               shared[shared_no("osq", i) % 2][:, :].rearrange("p (a b) -> p a b", a=2),
                               ACT.Sqrt, bias=sm("eps"), scale=1.0 / P).then_inc(o_root, 1)
            fill(fill_no("gkv", 0))
            fill(fill_no("gkv", 1))
            act.wait_ge(g_sum, 1)
            act.activation(g_ms, g_ms, ACT.Sqrt, bias=sm("eps"), scale=1.0 / HD).then_inc(g_root, 1)
            for i in range(STEPS):
                if i < len(UNITS):
                    act.wait_ge(max_ready, i + 1)
                    if i >= 2:
                        act.wait_ge(shared_ready, shared_no("pT", i - 2) + 1)
                    act.activation(probs[:, i % 2, :], score[i % 2][:, :], ACT.Exp, bias=nmax[:, i:i + 1],
                                   accum_out=psum_[:, i:i + 1]).then_inc(exp_ready, 1)
                for n in FILLER_AT[i]:
                    fill(n)
            act.wait_ge(out_by["act"], emptied(GATE_FILLS)[1])
            for b in range(3):
                act.activation(gates[:, b * KD:(b + 1) * KD, :], gates[:, b * KD:(b + 1) * KD, :],
                               ACT.Sigmoid).then_inc(sig_gates, 1)
            for name in ("row2", "row5"):
                for i in range(2):
                    fill(fill_no(name, i))
            for t in range(NT):
                act.wait_ge(x1_ready, 2 * NT - NT + t + 1)
                act.activation(xn[:, t, :], x_nat[:, t, :], ACT.Square, accum_out=stat[:, t:t + 1]).then_inc(x1_sum, 1)
            act.wait_ge(x1_sum, NT)
            act.activation(stat[:, 0:NT], stat[:, 0:NT], ACT.Sqrt, bias=sm("eps"), scale=1.0 / D).then_inc(x1_root, 1)
            act.dma_start(g_last, d["g_last"]).then_inc(glast_in, 16)
            act.wait_ge(gexp_in, 1)
            act.activation(r_eg, r_eg, ACT.Exp).then_inc(gexp_out, 1)
            act.wait_ge(gexp_in, 2)
            act.activation(r_d, r_d, ACT.Exp).then_inc(gexp_out, 1)

            def pair(before, first=False):
                n = before + 1
                for e in range(2):
                    act.wait_ge(gu_ready, 2 * n + e + 1)
                    if not first:
                        act.wait_ge(he_ready, 2 * before + e + 1)
                    act.activation(sl[:, e, :], banks[2 + e][:, 0:KH * CAP], ACT.Silu).then_inc(silu_ready, 1)
                act.wait_ge(down_ready, 2 * n + 2)
                if not first:
                    act.wait_ge(scat_ready, 4 * n)
                for i in range(2):
                    act.activation(y_sb[:, 512 * i:512 * i + 512], banks[4 + i][:, :], ACT.Copy).then_inc(y_out, 1)

            pair(-1, True)
            with act.Fori(0, PAIRS - 1) as j:
                pair(j)
            act.wait_ge(passes_ready, 2)
            n_pass = act.value_load(passes[0:1, 0:1], min_val=1, max_val=MAXPASS)
            with act.If(n_pass > 1):
                with act.Fori(PAIRS - 1, n_pass * PAIRS - 1) as j:
                    pair(j)
            for t in range(NT):
                act.wait_ge(fin_sum, t + 1)
                act.activation(SW[:, t, :], x_nat[:, t, :], ACT.Square, accum_out=stat[:, 2 + t:3 + t]).then_inc(a_step, 1)
            act.wait_ge(a_step, NT)
            act.activation(stat[:, 2:4], stat[:, 2:4], ACT.Sqrt, bias=sm("eps"), scale=1.0 / D).then_inc(fin_root, 1)

        @block.tensor
        def _(pe):
            def take_slot(n):
                pe.wait_ge(w_in_[n % FSLOTS], 16 * (n // FSLOTS + 1))

            def lhs(w, k, c, width=512):
                return w[:, k * width + c:k * width + c + P]

            def fill(n):
                name, i, _ = FILLS[n]
                ps = proj[n % PBANKS]
                if n >= PBANKS:
                    wait_emptied(pe, n - PBANKS)
                if name[:3] == "row":
                    if i == 0:
                        pe.wait_ge(diag_ready, 1 + (name == "row5"))
                    ins = pe.matmul(ps[:, :], ones, diag[:, 4 * i:4 * i + 4, :].rearrange("p a b -> p (a b)"),
                                    start=True, stop=True)
                    ins.then_inc(fill_ready, 1)
                    return
                g = FRONT.index(name)
                w = slot[g % FSLOTS]
                if i == 0:
                    take_slot(g)
                if name[:3] == "ada":
                    for c in range(4):
                        for k in range(KD):
                            ins = pe.matmul(ps[:, 2 * c:2 * c + 2], lhs(w, k, c * P), cvec[:, k, :],
                                            start=(k == 0), stop=(k == KD - 1))
                elif name in ("ff", "fb", "nk"):
                    for k in range(KD):
                        if name == "ff" and i == 0:
                            pe.wait_ge(h_ready, k + 1)
                        ins = pe.matmul(ps[:, :], lhs(w, k, i * P), hT[:, k, :], start=(k == 0), stop=(k == KD - 1))
                elif name in ("hq", "hg", "nq") or name[:4] == "gate":
                    for c in range(2):
                        for k in range(KD):
                            ins = pe.matmul(ps[:, c * L:(c + 1) * L], lhs(w, k, (2 * i + c) * P), hT[:, k, 0:L],
                                            start=(k == 0), stop=(k == KD - 1))
                elif name in ("hi", "nv", "gq"):
                    for k in range(KD):
                        ins = pe.matmul(ps[:, :], hT[:, k, i * P:(i + 1) * P], w[:, k * 512:(k + 1) * 512],
                                        start=(k == 0), stop=(k == KD - 1))
                elif name == "gkv":
                    for c in range(2):
                        for k in range(KD):
                            t = 2 * i + c
                            ins = pe.matmul(ps[:, c * 256:(c + 1) * 256], hT[:, k, t * P:(t + 1) * P],
                                            w[:, k * 256:(k + 1) * 256], start=(k == 0), stop=(k == KD - 1))
                elif name[:2] == "br":
                    b = int(name[2])
                    src = (aT, bT, cT)[b]
                    for c in range(2):
                        for k in range(4):
                            ins = pe.matmul(ps[:, c * L:(c + 1) * L], lhs(w, k, (2 * i + c) * P, D), src[:, k, :],
                                            start=(k == 0), stop=(k == 3))
                elif name[:3] == "out":
                    for k in range(KD):
                        if name == "out0" and i == 0 and k % 2 == 0:
                            pe.wait_ge(out_by["dve"], 8 + k // 2 + 1)
                        ins = pe.matmul(ps[:, :], yT[:, k, i * P:(i + 1) * P], w[:, k * 512:(k + 1) * 512],
                                        start=(k == 0), stop=(k == KD - 1))
                ins.then_inc(fill_ready, 1)
                if n + 1 == len(FILLS) or FILLS[n + 1][0] != name:
                    pe.wait_ge(fill_ready, n + 1)
                    pe.sem_inc(w_used, 1)

            def take_shared(n):
                if n >= 2:
                    pe.wait_ge(shared_out, n - 1)
                return shared[n % 2]

            def level(v):
                pe.wait_ge(xy_ready, v + 1)
                for q in range(4):
                    dr, t = q // 2, q % 2
                    ps = take_shared(shared_no(f"lev{v}", q))
                    for h in range(HGH):
                        j = dr * 4 + h
                        kk = (X if dr else Y)[:, j, t * P:(t + 1) * P]
                        qq = (QR[:, h] if v == 0 else (Y if dr else X)[:, j])[:, t * P:(t + 1) * P]
                        ins = pe.matmul(ps[:, h * P:(h + 1) * P], kk, qq, start=True, stop=True)
                    ins.then_inc(shared_ready, 1)

            def across():
                pe.wait_ge(xy_ready, LEVELS + 1)
                for dr in range(2):
                    ps = take_shared(shared_no("lev8", dr))
                    for h in range(HGH):
                        kk = (X if dr else Y)[:, dr * 4 + h, dr * P:(dr + 1) * P]
                        qq = (Y if dr else X)[:, dr * 4 + h, (1 - dr) * P:(2 - dr) * P]
                        ins = pe.matmul(ps[:, h * P:(h + 1) * P], kk, qq, start=True, stop=True)
                    ins.then_inc(shared_ready, 1)

            def ctx_keys():
                pe.wait_ge(kc_ready, 1)
                for q in range(4):
                    dr, t = q // 2, q % 2
                    ps = take_shared(shared_no("kc", q))
                    for h in range(HGH):
                        ins = pe.transpose(ps[:, h * P:(h + 1) * P], Kc[:, dr * 4 + h, t * P:(t + 1) * P], ident)
                    ins.then_inc(shared_ready, 1)

            def ctx_state():
                pe.wait_ge(shared_out, shared_no("kc", 3) + 1)
                wait_emptied(pe, fill_no("hi", 3))
                for dr in range(2):
                    ps = take_shared(shared_no("s0", dr))
                    for h in range(HGH):
                        for t in range(NT):
                            ins = pe.matmul(ps[:, h * P:(h + 1) * P], kc_tile(dr, t, h), v_hg[:, NT + t, h * P:(h + 1) * P],
                                            start=(t == 0), stop=(t == NT - 1))
                    ins.then_inc(shared_ready, 1)

            def kc_tile(dr, t, h):
                o = F0 + 6144 + ((dr * 2 + t) * HGH + h) * P
                return sb[:, o:o + P]

            def outputs():
                pe.wait_ge(xy_ready, LEVELS + 2)
                pe.wait_ge(shared_out, shared_no("lev8", 1) + 1)
                for i in range(2):
                    ps = take_shared(shared_no("o", i))
                    for hh in range(2):
                        h = 2 * i + hh
                        for t in range(NT):
                            o = ps[:, hh * L + t * P:hh * L + (t + 1) * P]
                            for dr in range(2):
                                cols = slice(h * P, (h + 1) * P)
                                pe.matmul(o, v_hg[:, t, cols], AT[:, dr * 3 + t, cols], start=(dr == 0), stop=False)
                                if t != dr:
                                    pe.matmul(o, v_hg[:, dr, cols], AT[:, dr * 3 + 2, cols], start=False, stop=False)
                                qq = (Y if dr else X)[:, dr * 4 + h, t * P:(t + 1) * P]
                                ins = pe.matmul(o, S0[:, dr * 4 + h, :], qq, start=False, stop=(dr == 1))
                    ins.then_inc(shared_ready, 1)

            def square_sums():
                pe.wait_ge(o_sq, 1)
                for i in range(2):
                    ps = take_shared(shared_no("osq", i))
                    pe.matmul(ps[:, :], ones, o_tmp[:, 2 * i:2 * i + 2, :].rearrange("p a b -> p (a b)"),
                              start=True, stop=True).then_inc(shared_ready, 1)

            def turn_gqa():
                pe.wait_ge(gqa_ready, 1)
                for i in range(2):
                    ps = take_shared(shared_no("gqT", i))
                    for r in range(2):
                        for t in range(NT):
                            src = gq[:, t, (2 * i + r) * P:(2 * i + r + 1) * P]
                            ins = pe.transpose(ps[:, r * L + t * P:r * L + (t + 1) * P], src, ident)
                    ins.then_inc(shared_ready, 1)
                ps = take_shared(shared_no("gkT"))
                for t in range(4):
                    ins = pe.transpose(ps[:, t * P:(t + 1) * P], gkv[:, t, 0:P], ident)
                ins.then_inc(shared_ready, 1)

            def scores(u):
                kind, t, h = UNITS[u]
                if u >= 2:
                    pe.wait_ge(exp_ready, u - 1)
                if kind == "na":
                    b, q, k = (h % 2) * HD, na_q[:, h // 2, :], na_k[:, h // 2, :]
                else:
                    if u == 2 * NH:
                        pe.wait_ge(shared_out, shared_no("gkT") + 1)
                    b, q, k = (h // 4) * HD, gqT[:, h % 4, :], gkT
                pe.matmul(score[u % 2][:, :], q[b:b + HD, t * P:(t + 1) * P], k[b:b + HD, :],
                          start=True, stop=True).then_inc(scores_ready, 1)

            def turn_probs(u):
                pe.wait_ge(exp_ready, u + 1)
                ps = take_shared(shared_no("pT", u))
                for c in range(4):
                    ins = pe.transpose(ps[:, c * P:(c + 1) * P], probs[:, u % 2, c * P:(c + 1) * P], ident)
                ins.then_inc(shared_ready, 1)

            def values(u):
                kind, t, h = UNITS[u]
                pe.wait_ge(shared_out, shared_no("pT", u) + 1)
                if u >= NH and h == 0:
                    pe.wait_ge(pv_out, u // NH)
                for c in range(4):
                    v = na_v[:, c, h * HD:(h + 1) * HD] if kind == "na" else \
                        gkv[:, c, P + (h // 4) * HD:P + (h // 4 + 1) * HD]
                    ins = pe.matmul(pv_bank[:, h * HD:(h + 1) * HD], probsT[:, u % 2, c * P:(c + 1) * P], v,
                                    start=(c == 0), stop=(c == 3))
                ins.then_inc(pv_ready, 1)

            def turn_branch(name, src, k_out):
                pe.wait_ge(pv_out, k_out)
                for i in range(2):
                    ps = take_shared(shared_no(name, i))
                    for c in range(2):
                        for t in range(NT):
                            ins = pe.transpose(ps[:, c * L + t * P:c * L + (t + 1) * P],
                                               src[:, t, (2 * i + c) * P:(2 * i + c + 1) * P], ident)
                    ins.then_inc(shared_ready, 1)

            pe.wait_ge(small_in, 16)
            for k in range(KD):
                pe.wait_ge(sq_ready, k + 1)
                ins = pe.matmul(pv_bank[:, :], ones, sq[:, k, :], start=(k == 0), stop=(k == KD - 1))
            ins.then_inc(rms_ready, 1)
            pe.wait_ge(c_ready, 1)
            for n in range(fill_no("hg", 1) + 1):
                fill(n)
            ctx_keys()
            for v in range(4):
                level(v)
                fill(fill_no("hi", v))
            for v in range(4, 8):
                level(v)
                fill(fill_no("nk", v - 4))
            ctx_state()
            fill(fill_no("nq", 0))
            across()
            fill(fill_no("nq", 1))
            fill(fill_no("nv", 0))
            outputs()
            for n in range(fill_no("nv", 1), fill_no("gq", 1) + 1):
                fill(n)
            square_sums()
            fill(fill_no("gkv", 0))
            fill(fill_no("gkv", 1))
            turn_gqa()
            wait_emptied(pe, fill_no("nv", 3))
            for i in range(STEPS):
                if i < len(UNITS):
                    scores(i)
                if i % 2 == 0:
                    for n in FILLER_AT[i]:
                        fill(n)
                if 1 <= i <= len(UNITS):
                    turn_probs(i - 1)
                if i % 2 == 1:
                    for n in FILLER_AT[i]:
                        fill(n)
                if 2 <= i < len(UNITS) + 2:
                    values(i - 2)
                if i == AT_STEP:
                    turn_branch("aT", a_nat, 2)
            turn_branch("cT", c_nat, 4)
            for i in range(2):
                fill(fill_no("row2", i))
            pe.wait_ge(fill_ready, fill_no("row2", 1) + 1)
            pe.sem_inc(diag_used, 1)
            for i in range(2):
                fill(fill_no("row5", i))
            pe.wait_ge(shared_out, shared_no("aT", 1) + 1)
            for n in range(fill_no("br0"), fill_no("br1")):
                fill(n)
            pe.wait_ge(b_ready, 1)
            for n in range(fill_no("br1"), fill_no("br2")):
                fill(n)
            pe.wait_ge(shared_out, shared_no("cT", 1) + 1)
            for n in range(fill_no("br2"), len(FILLS)):
                fill(n)
            for q in range(4):
                if q == 0:
                    pe.wait_ge(xn_ready, NT)
                ps = take_shared(shared_no("fT", q))
                for c in range(2):
                    for t in range(NT):
                        k = 2 * q + c
                        ins = pe.transpose(ps[:, c * L + t * P:c * L + (t + 1) * P], xn[:, t, k * P:(k + 1) * P], ident)
                ins.then_inc(shared_ready, 1)
            pe.wait_ge(shared_out, shared_no("fT", 3) + 1)
            pe.wait_ge(pv_out, 4)
            for t in range(NT):
                for k in range(KD):
                    ins = pe.matmul(pv_bank[:, t * 32:t * 32 + ROUTES], fT[:, k, t * P:(t + 1) * P], sm("router")[:, k, :],
                                    start=(k == 0), stop=(k == KD - 1))
            ins.then_inc(logits_ready, 1)
            pe.wait_ge(member_ready, 1)
            pe.matmul(pv_bank[:, 64:80], below, member[:, 0, :], start=True, stop=True)
            pe.matmul(pv_bank[:, 80:96], ones, member[:, 0, :], start=True, stop=False)
            pe.matmul(pv_bank[:, 80:96], below, member[:, 1, :], start=False, stop=True)
            pe.matmul(pv_bank[:, 96:112], ones, member[:, 0, :], start=True, stop=False)
            pe.matmul(pv_bank[:, 96:112], ones, member[:, 1, :], start=False, stop=True).then_inc(pos_ready, 1)

            def turn_slots(p):
                for q in range(4):
                    n = p * 4 + q
                    if q == 0:
                        pe.wait_ge(slots_ready, p * 2 + 1)
                    if isinstance(p, int) and q < 2:
                        take_shared(shared_no("sT", q))
                    else:
                        pe.wait_ge(shared_out, shared_no("sT") + n - 1)
                    ps = shared[(shared_no("sT") + q) % 2]
                    for c in range(4):
                        pr, t = 2 * q + c // 2, c % 2
                        ins = pe.transpose(ps[:, c * P:(c + 1) * P], SW[:, t, pr * P:(pr + 1) * P], ident)
                    ins.then_inc(shared_ready, 1)

            def gather(n):
                pe.wait_ge(cut_ready, 2 * n + 1)
                if not isinstance(n, int) or n:
                    pe.wait_ge(h_out, 2 * n)
                for i in range(2):
                    for c in range(4):
                        for t in range(NT):
                            ins = pe.matmul(banks[i][:, c * P:(c + 1) * P], xn[:, t, (4 * i + c) * P:(4 * i + c + 1) * P],
                                            S_now[:, t, :], start=(t == 0), stop=(t == NT - 1))
                    if i == 1:
                        ins.then_inc(gather_ready, 1)

            def weights(n, s):
                pe.wait_ge(w_in_[s], slot_value(s) + 16 * (n + 1))

            def gate_up(before, e, first=False):
                n = before + 1
                if e == 0:
                    pe.wait_ge(h_out, 2 * n + 2)
                weights(n, 3 * e)
                weights(n, 3 * e + 1)
                if not first:
                    pe.wait_ge(he_ready, 2 * before + e + 1)
                for g in range(2):
                    for c in range(KH):
                        o = (g * KH + c) * CAP
                        for k in range(KD):
                            ins = pe.matmul(banks[2 + e][:, o:o + CAP], lhs(slot[3 * e + g], k, c * P),
                                            h_sb[:, k, e * CAP:(e + 1) * CAP], start=(k == 0), stop=(k == KD - 1))
                ins.then_inc(gu_ready, 1)

            def down(n, e, first=False):
                weights(n, 3 * e + 2)
                pe.wait_ge(he_ready, 2 * n + e + 1)
                if e == 0 and not first:
                    pe.wait_ge(y_out, 2 * n)
                for i in range(2):
                    for k in range(KH):
                        ins = pe.matmul(banks[4 + i][e * CAP:(e + 1) * CAP, :], he[:, e, k * CAP:(k + 1) * CAP],
                                        slot[3 * e + 2][:, k * D + i * 512:k * D + (i + 1) * 512],
                                        start=(k == 0), stop=(k == KH - 1))
                ins.then_inc(down_ready, 1)

            def scatter(n):
                pe.wait_ge(y_out, 2 * n + 2)
                pe.wait_ge(cut_ready, 2 * n + 2)
                for q in range(4):
                    t, i = q // 2, q % 2
                    if q > 1:
                        pe.wait_ge(scat_out, 4 * n + q - 1)
                    elif not isinstance(n, int) or n:
                        pe.wait_ge(scat_out, 4 * n)
                    pe.matmul(banks[6 + i][:, :], ST_now[:, t, :], y_sb[:, i * 512:(i + 1) * 512],
                              start=True, stop=True).then_inc(scat_ready, 1)

            def one_pass(p):
                turn_slots(p)
                n0 = p * PAIRS
                first = isinstance(p, int)
                if first:
                    pe.wait_ge(pos_ready, 1)
                gather(n0)
                gate_up(n0 - 1, 0, first)
                gate_up(n0 - 1, 1, first)
                gather(n0 + 1)
                down(n0, 0, first)
                down(n0, 1, first)
                with pe.Fori(0, PAIRS - 2) as j:
                    before = n0 + j
                    gate_up(before, 0)
                    scatter(before)
                    gate_up(before, 1)
                    gather(before + 2)
                    down(before + 1, 0)
                    down(before + 1, 1)
                before = n0 + PAIRS - 2
                gate_up(before, 0)
                scatter(before)
                gate_up(before, 1)
                down(before + 1, 0)
                down(before + 1, 1)
                scatter(before + 1)

            pe.wait_ge(passes_ready, 2)
            one_pass(0)
            n_pass = pe.value_load(passes[0:1, 0:1], min_val=1, max_val=MAXPASS)
            with pe.If(n_pass > 1):
                with pe.Fori(1, n_pass) as p:
                    one_pass(p)
            pe.nop()

        @block.vector
        def _(dve):
            steps = [0]

            def link(ins):
                steps[0] += 1
                ins.then_inc(v_step, 1)
                dve.wait_ge(v_step, steps[0])

            dve.memset(zeros, 0.0)
            dve.wait_ge(small_in, 16)
            lg = sm("lb")
            dve.tensor_tensor(lb_e, lg, lg, ALU.subtract).then_inc(lb_in, 1)
            dve.wait_ge(rms_root, 1)
            link(dve.reciprocal(rstd_row, rstd_row))
            for k in range(KD):
                ins = dve.tensor_tensor(hT[:, k, :], hT[:, k, :], rstd_row, ALU.mult)
            link(ins)
            dve.wait_ge(out_by["act"], emptied(fill_no("ada3"))[1])
            b_ada = sm("b_ada")
            link(dve.tensor_tensor(mod[:, 0:16, :], mod[:, 0:16, :],
                                   b_ada[:, 0:16].unsqueeze(2).broadcast_to([P, 16, 2]), ALU.add))
            link(dve.tensor_scalar(A_mix, mod[:, 8:16, :], 1.0, None, ALU.add))
            link(dve.tensor_tensor(A_mix, A_mix, sm("g_mix").unsqueeze(2).broadcast_to([P, KD, 2]), ALU.mult))
            for k in range(KD):
                for s in range(2):
                    ins = dve.tensor_scalar(hT[:, k, s * L:(s + 1) * L], hT[:, k, s * L:(s + 1) * L],
                                            A_mix[:, k, s:s + 1], mod[:, k, s:s + 1], ALU.mult, ALU.add)
                ins.then_inc(h_ready, 1)
            dve.wait_ge(lb_ready, 1)
            link(dve.reciprocal(lb_p, lb_e))
            link(dve.tensor_tensor(lb_p, lb_e, lb_p, ALU.mult))
            link(dve.tensor_tensor(lower, lb_p, lb_p, ALU.subtract))
            link(dve.tensor_scalar(span, lower, -1.0, 1.0, ALU.mult, ALU.add))

            for dr in range(2):
                name = ("ff", "fb")[dr]
                for h in range(HGH):
                    j = dr * 4 + h
                    dve.wait_ge(out_by["act"], emptied(fill_no(name, h))[1])
                    ins = dve.tensor_scalar(forget[:, :, j, :], forget[:, :, j, :], span[:, j:j + 1],
                                            lower[:, j:j + 1], ALU.mult, ALU.add)
                link(ins)
                keys = (X if dr else Y)[:, dr * 4:dr * 4 + 4, :]
                link(dve.tensor_scalar(keys, T_lat[:, dr * 4:dr * 4 + 4, :], -1.0, 1.0, ALU.mult, ALU.add))
                dve.tensor_scalar(Kc[:, dr * 4:dr * 4 + 4, :], F_ctx[:, dr * 4:dr * 4 + 4, :], -1.0, 1.0,
                                  ALU.mult, ALU.add)
                for h in range(HGH):
                    j = dr * 4 + h
                    dst = kcn[:, j, :]
                    if dr == 0:
                        dve.memset(dst[:, L - 1:L], 1.0)
                        ins = dve.tensor_tensor_scan(dst[:, 0:L - 1][:, ::-1], F_ctx[:, j, 1:L][:, ::-1],
                                                     zeros[:, 0:L - 1], 1.0, ALU.mult, ALU.add)
                    else:
                        dve.memset(dst[:, 0:1], 1.0)
                        ins = dve.tensor_tensor_scan(dst[:, 1:L], F_ctx[:, j, 0:L - 1],
                                                     zeros[:, 0:L - 1], 1.0, ALU.mult, ALU.add)
                link(ins)
            link(dve.tensor_tensor(Kc, Kc, kcn, ALU.mult))
            dve.sem_inc(kc_ready, 1)
            dve.wait_ge(out_by["act"], emptied(fill_no("hq", 1))[1])
            dve.tensor_tensor(QR, QR, sig_q, ALU.mult).then_inc(silu_hg, 1)
            dve.wait_ge(silu_hg, 1)
            dve.tensor_tensor(X[:, 0:4, :], QR, T_lat[:, 0:4, :], ALU.mult)
            dve.tensor_tensor(Y[:, 4:8, :], QR, T_lat[:, 4:8, :], ALU.mult).then_inc(xy_ready, 2)
            dve.wait_ge(out_by["act"], emptied(fill_no("hg", 1))[1])
            dve.tensor_tensor(bT, bT, sig_g, ALU.mult).then_inc(silu_hg, 1)

            def shared_wait(n):
                dve.wait_ge(shared_ready, n + 1)
                return shared[n % 2]

            def shared_copy(n, dst):
                dve.tensor_copy(dst, shared_wait(n)[:, :]).then_inc(shared_out, 1)

            for q in range(4):
                o = F0 + 6144 + q * 512
                shared_copy(shared_no("kc", q), sb[:, o:o + 512])

            def products(v):
                for q in range(4):
                    dr, t = q // 2, q % 2
                    n = shared_no(f"lev{v}", q)
                    ps = shared_wait(n)[:, :].rearrange("p (h t) -> p h t", h=HGH)
                    dst = AT[:, dr * 3 + t, :].rearrange("p (h t) -> p h t", h=HGH)
                    if v == 0:
                        m = ident.unsqueeze(1).broadcast_to([P, HGH, P])
                        dve.tensor_tensor(dst, ps, m, ALU.mult).then_inc(shared_out, 1)
                    else:
                        m = masks[:, dr * (LEVELS - 1) + v - 1, :].unsqueeze(1).broadcast_to([P, HGH, P])
                        dve.wait_ge(shared_out, n - 3)
                        dve.copy_predicated(dst, m, ps).then_inc(shared_out, 1)

            def join(v):
                m = 1 << (v - 1)
                t_ = T_of[v - 1]
                pairs = t_.rearrange("p (b s) -> p b s", s=2)
                xv = at(A0 + 7168, 2048).rearrange("p (b s m) -> p b s m", s=2, m=m)
                yv = at(A0 + 9216, 2048).rearrange("p (b s m) -> p b s m", s=2, m=m)
                nb = 2048 // (2 * m)
                left = pairs[:, :, 0:1].broadcast_to([P, nb, m])
                right = pairs[:, :, 1:2].broadcast_to([P, nb, m])
                dve.tensor_tensor(xv[:, :, 1, :], xv[:, :, 1, :], left, ALU.mult)
                ins = dve.tensor_tensor(yv[:, :, 0, :], yv[:, :, 0, :], right, ALU.mult)
                if v < LEVELS:
                    ins.then_inc(xy_ready, 1)
                    dve.tensor_tensor(T_of[v], pairs[:, :, 0], pairs[:, :, 1], ALU.mult).then_inc(v_step, 1)
                    steps[0] += 1
                else:
                    ins.then_inc(xy_ready, 1)

            T_of = [at(F0, 2048)]
            for v in range(1, LEVELS):
                size = 2048 >> v
                T_of.append(at(C0 if v % 2 else F0, size))
            T_of.append(at(C0, 2048 >> LEVELS))

            dve.wait_ge(masks_ready, 1)
            products(0)
            for v in range(1, LEVELS):
                products(v)
                dve.wait_ge(v_step, steps[0])
                dve.wait_ge(xy_ready, v + 1)
                join(v)
            for q in range(2):
                shared_copy(shared_no("s0", q), S0[:, 4 * q:4 * q + 4, :].rearrange("p a b -> p (a b)"))
            for dr in range(2):
                shared_copy(shared_no("lev8", dr), AT[:, dr * 3 + 2, :])
            dve.wait_ge(v_step, steps[0])
            dve.wait_ge(xy_ready, LEVELS + 1)
            join(LEVELS)
            for q in range(2):
                shared_copy(shared_no("o", q), o_sb[:, 2 * q:2 * q + 2, :].rearrange("p a b -> p (a b)"))

            for i in range(2):
                dve.wait_ge(o_root, i + 1)
                dve.reciprocal(o_tmp[:, 2 * i:2 * i + 2, :], o_tmp[:, 2 * i:2 * i + 2, :]).then_inc(shared_out, 1)
            dve.wait_ge(shared_out, shared_no("osq", 1) + 1)
            link(dve.tensor_tensor(o_sb, o_sb, o_tmp, ALU.mult))
            dve.scalar_tensor_tensor(out=bT, in0=o_sb, scalar=sm("hg_g"), in1=bT, op0=ALU.mult, op1=ALU.mult)\
               .then_inc(b_ready, 1)

            dve.wait_ge(out_by["act"], emptied(fill_no("gkv", 1))[1])
            dve.tensor_tensor(g_sq[:, 0:1024], gq.rearrange("p t n -> p (t n)"), gq.rearrange("p t n -> p (t n)"), ALU.mult)
            gkk = gkv[:, :, 0:P]
            link(dve.tensor_tensor(g_sq[:, 1024:1536].rearrange("p (a b) -> p a b", b=P), gkk, gkk, ALU.mult))
            dve.tensor_reduce(g_ms, g_sq.rearrange("p (a b) -> p a b", b=HD), AX.X, ALU.add).then_inc(g_sum, 1)
            dve.wait_ge(g_root, 1)
            link(dve.reciprocal(g_ms, g_ms))
            dve.tensor_scalar(g_ms[:, 0:16], g_ms[:, 0:16], QSCALE, None, ALU.mult).then_inc(g_rec, 1)

            for q in range(2):
                shared_copy(shared_no("gqT", q), gqT[:, 2 * q:2 * q + 2, :].rearrange("p a b -> p (a b)"))
            shared_copy(shared_no("gkT"), gkT)

            def maximum(u):
                kind, t, h = UNITS[u]
                dve.wait_ge(scores_ready, u + 1)
                s = score[u % 2]
                if kind == "na":
                    if u == 0:
                        dve.wait_ge(bias_in, 16)
                    i0 = 2 - 2 * t
                    link(dve.tensor_tensor(s[:, 0:L], s[:, 0:L], na_bias[:, h, i0 * GRID:(i0 + ROWS) * GRID], ALU.add))
                dve.tensor_reduce(nmax[:, u:u + 1], s[:, :], AX.X, ALU.max, negate=True).then_inc(max_ready, 1)

            def attention_out(k):
                dve.wait_ge(exp_ready, (k + 1) * NH)
                link(dve.reciprocal(psum_[:, k * NH:(k + 1) * NH], psum_[:, k * NH:(k + 1) * NH]))
                dve.wait_ge(pv_ready, (k + 1) * NH)
                dst = (a_nat if k < 2 else c_nat)[:, k % 2, :].rearrange("p (h c) -> p h c", c=HD)
                dve.tensor_tensor(dst, pv_bank[:, :].rearrange("p (h c) -> p h c", c=HD),
                                  psum_[:, k * NH:(k + 1) * NH].unsqueeze(2).broadcast_to([P, NH, HD]),
                                  ALU.mult).then_inc(pv_out, 1)

            for i in range(STEPS):
                if i < len(UNITS):
                    maximum(i)
                if 1 <= i <= len(UNITS):
                    u = i - 1
                    if u >= 2:
                        dve.wait_ge(pv_ready, u - 1)
                    shared_copy(shared_no("pT", u), probsT[:, u % 2, :])
                if i >= NH + 2 and (i - 2) % NH == 0:
                    attention_out((i - 2) // NH - 1)
                if i == AT_STEP:
                    for q in range(2):
                        shared_copy(shared_no("aT", q), aT[:, 2 * q:2 * q + 2, :].rearrange("p a b -> p (a b)"))
            for q in range(2):
                shared_copy(shared_no("cT", q), cT[:, 2 * q:2 * q + 2, :].rearrange("p a b -> p (a b)"))

            dve.wait_ge(out_by["act"], emptied(fill_no("ada11"))[1])
            link(dve.tensor_tensor(mod[:, 16:48, :], mod[:, 16:48, :],
                                   b_ada[:, 16:48].unsqueeze(2).broadcast_to([P, 32, 2]), ALU.add))
            link(dve.tensor_scalar(A_ffn, mod[:, 32:40, 0], 1.0, None, ALU.add))
            dve.tensor_tensor(A_ffn, A_ffn, sm("g_ffn"), ALU.mult).then_inc(modb_ready, 1)

            dve_out = out_by["dve"]
            for n in range(fill_no("br0"), fill_no("out0")):
                b, i = int(FILLS[n][0][2]), FILLS[n][1]
                dve.wait_ge(fill_ready, n + 1)
                if i == 0:
                    dve.wait_ge(sig_gates, b + 1)
                ps = proj[n % PBANKS][:, :].rearrange("p (a b) -> p a b", a=2)
                g = gates[:, b * KD + 2 * i:b * KD + 2 * i + 2, :]
                y = yT[:, 2 * i:2 * i + 2, :]
                if b == 0:
                    dve.tensor_tensor(y, ps, g, ALU.mult).then_inc(dve_out, 1)
                else:
                    link(dve.tensor_tensor(g, ps, g, ALU.mult))
                    dve.wait_ge(dve_out, 4 * (b - 1) + i + 1)
                    dve.tensor_tensor(y, y, g, ALU.add).then_inc(dve_out, 1)

            dve.wait_ge(xnat_in, 16)
            for n in range(fill_no("out0"), len(FILLS)):
                i, t = int(FILLS[n][0][3]), FILLS[n][1]
                cols = slice(512 * i, 512 * i + 512)
                if n == fill_no("out0"):
                    wait_emptied(dve, fill_no("row2", 1))
                dve.wait_ge(fill_ready, n + 1)
                dve.tensor_tensor(xn[:, t, cols], proj[n % PBANKS][:, :], row2[:, cols], ALU.mult).then_inc(dve_out, 1)
                dve.wait_ge(dve_out, emptied(n)[1])
                dve.tensor_tensor(x_nat[:, t, cols], x_nat[:, t, cols], xn[:, t, cols], ALU.add).then_inc(x1_ready, 1)
            dve.wait_ge(x1_root, 1)
            link(dve.reciprocal(stat[:, 0:NT], stat[:, 0:NT]))
            for t in range(NT):
                dve.tensor_scalar(xn[:, t, :], x_nat[:, t, :], stat[:, t:t + 1], None, ALU.mult).then_inc(xn_ready, 1)
            for q in range(4):
                n = shared_no("fT", q)
                ps = shared_wait(n)
                for c in range(2):
                    k = 2 * q + c
                    ins = dve.tensor_scalar(fT[:, k, :], ps[:, c * L:(c + 1) * L], A_ffn[:, k:k + 1],
                                            mod[:, 3 * KD + k, 0:1], ALU.mult, ALU.add)
                ins.then_inc(shared_out, 1)

            def wide(v, n):
                return v.unsqueeze(2).broadcast_to([P, NT, n])

            def first_best(dst, x, best, weight, tmp, tmp_max, n):
                link(dve.tensor_tensor(tmp, x, wide(best, n), ALU.is_equal))
                link(dve.tensor_tensor(tmp, tmp, weight.unsqueeze(1).broadcast_to([P, NT, n]), ALU.mult))
                link(dve.tensor_reduce(tmp_max, tmp, AX.X, ALU.max))
                link(dve.tensor_tensor(dst, tmp, wide(tmp_max, n), ALU.is_equal))

            dve.wait_ge(logits_ready, 1)
            lo = pv_bank[:, 0:64].rearrange("p (t n) -> p t n", t=NT)
            rb = sm("router_b")
            dve.tensor_tensor(r_g, lo[:, :, 0:NG], rb[:, 0:NG].unsqueeze(1).broadcast_to([P, NT, NG]), ALU.add)
            link(dve.tensor_tensor(r_e, lo[:, :, NG:ROUTES], rb[:, NG:ROUTES].unsqueeze(1).broadcast_to([P, NT, NE]), ALU.add))
            link(dve.tensor_reduce(r_gm, r_g, AX.X, ALU.max))
            dve.tensor_tensor(r_eg, r_g, wide(r_gm, NG), ALU.subtract).then_inc(gexp_in, 1)
            first_best(r_sel, r_g, r_gm, sm("rank")[:, NE - NG:NE], r_t, r_sm, NG)
            sel = r_sel.rearrange("p t g -> p (t g)").unsqueeze(2).broadcast_to([P, NT * NG, EPG])
            em = r_em.rearrange("p t (g e) -> p (t g) e", g=NG)
            link(dve.tensor_tensor(em, r_e.rearrange("p t (g e) -> p (t g) e", g=NG), sel, ALU.mult))
            link(dve.tensor_scalar(r_t, r_sel, -1.0, -NEG, ALU.add, ALU.mult))
            outside = r_t.rearrange("p t g -> p (t g)").unsqueeze(2).broadcast_to([P, NT * NG, EPG])
            link(dve.tensor_tensor(em, em, outside, ALU.add))
            link(dve.tensor_reduce(r_m1, r_em, AX.X, ALU.max))
            first_best(oh1, r_em, r_m1, sm("rank"), r_et, r_sm, NE)
            link(dve.scalar_tensor_tensor(out=r_em, in0=oh1, scalar=3 * NEG, in1=r_em, op0=ALU.mult, op1=ALU.add))
            link(dve.tensor_reduce(r_m2, r_em, AX.X, ALU.max))
            dve.tensor_tensor(r_d, r_m2, r_m1, ALU.subtract).then_inc(gexp_in, 1)
            first_best(oh2, r_em, r_m2, sm("rank"), r_et, r_sm, NE)
            dve.tensor_tensor(member, oh1, oh2, ALU.add).then_inc(member_ready, 1)
            dve.wait_ge(gexp_out, 2)
            link(dve.tensor_reduce(r_gs, r_eg, AX.X, ALU.add))
            link(dve.tensor_scalar(r_w1, r_d, 1.0, None, ALU.add))
            link(dve.tensor_tensor(r_w1, r_w1, r_gs, ALU.mult))
            link(dve.reciprocal(r_w1, r_w1))
            link(dve.tensor_tensor(r_w2, r_w1, r_d, ALU.mult))
            dve.tensor_tensor(oh1, oh1, wide(r_w1, NE), ALU.mult)
            link(dve.tensor_tensor(oh2, oh2, wide(r_w2, NE), ALU.mult))
            link(dve.tensor_tensor(comb, oh1, oh2, ALU.add))
            dve.wait_ge(pos_ready, 1)
            rank_ps = pv_bank[:, 64:96].rearrange("p (t n) -> p t n", t=NT)
            dve.wait_ge(member_ready, 1)
            link(dve.scalar_tensor_tensor(out=posm, in0=rank_ps, scalar=1.0, in1=member, op0=ALU.add, op1=ALU.mult))
            link(dve.tensor_scalar(posm, posm, -1.0, None, ALU.add))
            link(dve.tensor_reduce(count, pv_bank[:, 96:112], AX.X, ALU.max))
            link(dve.tensor_scalar(over, sm("limits"), count, None, ALU.is_lt))
            link(dve.tensor_reduce(passes_f, over, AX.X, ALU.add))
            dve.tensor_scalar(passes[0:1, 0:1], passes_f[0:1, :], 1.0, None, ALU.add).then_inc(passes_ready, 2)

            def build_slots(p):
                for t in range(NT):
                    s = S_all[:, t, :].rearrange("p (e c) -> p e c", c=CAP)
                    dve.tensor_tensor(s, slots_iota.unsqueeze(1).broadcast_to([P, NE, CAP]),
                                      posm[:, t, :].unsqueeze(2).broadcast_to([P, NE, CAP]), ALU.is_equal)
                link_now()
                for t in range(NT):
                    s = S_all[:, t, :].rearrange("p (e c) -> p e c", c=CAP)
                    w = SW[:, t, :].rearrange("p (e c) -> p e c", c=CAP)
                    ins = dve.tensor_tensor(w, s, comb[:, t, :].unsqueeze(2).broadcast_to([P, NE, CAP]), ALU.mult)
                return ins

            def link_now():
                dve.drain()

            build_slots(0).then_inc(slots_ready, 1)
            dve.memset(yacc, 0.0)
            for q in range(4):
                n = shared_no("sT", q)
                dst = ST_all[:, 2 * q:2 * q + 2, :].rearrange("p a b -> p (a b)")
                shared_copy(n, dst)

            def spread(v):
                return v.unsqueeze(2).broadcast_to([P, 4, P])

            def modulate(n):
                dve.wait_ge(gather_ready, n + 1)
                if not isinstance(n, int) or n:
                    dve.wait_ge(gu_ready, 2 * n)
                for i in range(2):
                    ps = banks[i][:, :].rearrange("p (a b) -> p a b", b=P)
                    dve.tensor_tensor(h_sb[:, 4 * i:4 * i + 4, :], ps, spread(A_ffn[:, 4 * i:4 * i + 4]), ALU.mult)
                dve.drain()
                for i in range(2):
                    hh = h_sb[:, 4 * i:4 * i + 4, :]
                    dve.tensor_tensor(hh, hh, spread(mod[:, 3 * KD + 4 * i:3 * KD + 4 * i + 4, 0]), ALU.add)\
                       .then_inc(h_out, 1)

            def gated(before, e, first=False):
                n = before + 1
                dve.wait_ge(silu_ready, 2 * n + e + 1)
                if not first:
                    dve.wait_ge(down_ready, 2 * before + e + 1)
                dve.tensor_tensor(he[:, e, :], sl[:, e, :], banks[2 + e][:, KH * CAP:2 * KH * CAP], ALU.mult)\
                   .then_inc(he_ready, 1)

            def scattered(n):
                for q in range(4):
                    t, i = q // 2, q % 2
                    dve.wait_ge(scat_ready, 4 * n + q + 1)
                    y = yacc[:, t, 512 * i:512 * i + 512]
                    dve.tensor_tensor(y, y, banks[6 + i][:, :], ALU.add).then_inc(scat_out, 1)

            def one_pass(p):
                n0 = p * PAIRS
                first = isinstance(p, int)
                modulate(n0)
                gated(n0 - 1, 0, first)
                gated(n0 - 1, 1, first)
                modulate(n0 + 1)
                with dve.Fori(0, PAIRS - 2) as j:
                    before = n0 + j
                    gated(before, 0)
                    scattered(before)
                    gated(before, 1)
                    modulate(before + 2)
                before = n0 + PAIRS - 2
                gated(before, 0)
                scattered(before)
                gated(before, 1)
                scattered(before + 1)

            dve.wait_ge(shared_out, shared_no("sT", 3) + 1)
            dve.sem_inc(slots_ready, 1)
            one_pass(0)
            n_pass = dve.value_load(passes[0:1, 0:1], min_val=1, max_val=MAXPASS)
            with dve.If(n_pass > 1):
                with dve.Fori(1, n_pass) as p:
                    dve.tensor_scalar(posm, posm, -float(CAP), None, ALU.add)
                    dve.drain()
                    build_slots(p).then_inc(slots_ready, 1)
                    for q in range(4):
                        dve.wait_ge(shared_ready, shared_no("sT") + p * 4 + q + 1)
                        dst = ST_all[:, 2 * q:2 * q + 2, :].rearrange("p a b -> p (a b)")
                        dve.tensor_copy(dst, shared[(shared_no("sT") + q) % 2][:, :]).then_inc(shared_out, 1)
                    dve.drain()
                    dve.sem_inc(slots_ready, 1)
                    one_pass(p)
            dve.drain()

            dve.wait_ge(glast_in, 16)
            wait_emptied(dve, fill_no("row5", 1))
            for t in range(NT):
                link(dve.tensor_tensor(yacc[:, t, :], yacc[:, t, :], row5, ALU.mult))
                dve.tensor_tensor(x_nat[:, t, :], x_nat[:, t, :], yacc[:, t, :], ALU.add).then_inc(fin_sum, 1)
            dve.wait_ge(fin_root, 1)
            link(dve.reciprocal(stat[:, 2:4], stat[:, 2:4]))
            for t in range(NT):
                dve.scalar_tensor_tensor(out=yacc[:, t, :], in0=x_nat[:, t, :], scalar=stat[:, 2 + t:3 + t],
                                         in1=g_last, op0=ALU.mult, op1=ALU.mult).then_inc(fin_ready, 1)


SM = {}
SMALL = 0
for _name, *_dims in (("ident", P), ("ones", P), ("below", P), ("iota", CAP), ("eps", 1), ("limits", MAXPASS - 1),
                      ("rank", NE), ("b_ada", 48), ("g_mix", KD), ("g_ffn", KD), ("lb", 8), ("hg_g", 1),
                      ("gqn", HD), ("gqn_swapped", HD), ("gkn", HD), ("gkn_swapped", HD),
                      ("router_b", ROUTES), ("router", KD, ROUTES), ("cos", NT, HD), ("sin", NT, HD)):
    SM[_name] = (SMALL, _dims)
    SMALL += int(np.prod(_dims))


def columns(v):
    return v.reshape(-1, P).T


def shape_constants():
    f = np.float32
    i = np.arange(P)
    rank = np.arange(NE, 0, -1, dtype=f)
    t = np.arange(L)
    pos = np.stack([t // GRID, t % GRID], axis=-1).astype(f)
    n_freq = HD // 4
    inv = np.power(f(10000.0), -np.arange(n_freq, dtype=f) / f(n_freq)).astype(f)
    ang = (pos[:, :, None] * inv).astype(f)
    cos = np.concatenate([np.cos(ang)] * 2, axis=-1).reshape(NT, P, HD).transpose(1, 0, 2)
    sin = np.concatenate([-np.sin(ang), np.sin(ang)], axis=-1).reshape(NT, P, HD).transpose(1, 0, 2)
    return {
        "ident": np.eye(P, dtype=f), "ones": np.ones((P, P), f),
        "below": (i[:, None] < i[None, :]).astype(f),
        "iota": np.tile(np.arange(CAP, dtype=f), (P, 1)),
        "eps": np.full((P, 1), EPS, f),
        "limits": np.tile(np.arange(1, MAXPASS, dtype=f) * CAP, (P, 1)),
        "rank": np.tile(rank, (P, 1)), "cos": cos.astype(f), "sin": sin.astype(f),
    }


def level_masks():
    i = np.arange(P)
    out = np.zeros((P, 2 * (LEVELS - 1), P), np.float32)
    for v in range(LEVELS - 1):
        m = 1 << v
        same = (i[:, None] // (2 * m)) == (i[None, :] // (2 * m))
        right = (i // m) % 2 == 1
        out[:, v, :] = same & ~right[:, None] & right[None, :]
        out[:, LEVELS - 1 + v, :] = same & right[:, None] & ~right[None, :]
    return out


def bias_layout(rpb):
    col = np.arange(GRID)
    c0 = np.clip(col - WC // 2, 0, GRID - WC)
    inside = (col[None, :] >= c0[:, None]) & (col[None, :] < c0[:, None] + WC)
    dc = np.where(inside, col[None, :] - col[:, None] + WC - 1, 0)
    out = np.full((P, NH, RB, GRID), NEG, np.float32)
    for half in range(2):
        for i in range(RB):
            dr = i - 2 - half + WR - 1
            rows = rpb[:, dr][:, dc]
            out[half * GRID:(half + 1) * GRID, :, i, :] = np.where(inside[:, None, :], rows.transpose(1, 0, 2), np.float32(NEG))
    return out.reshape(P, NH, RB * GRID)


def weight_slots(w, width=512):
    k, n = w.shape
    s = w.reshape(k // P, P, n // width, width).transpose(2, 1, 0, 3)
    return s.reshape(n // width, P, -1)


def kernel(**inputs):
    import concourse.bacc as bacc
    from concourse.bass_utils import run_bass_kernel_spmd

    a = {k: np.asarray(v) for k, v in inputs.items()}
    x, ctx_ = a["x"][0], a["ctx"][0]
    xc = np.concatenate([x, ctx_], axis=0)
    w_in = a["w_in"][0]
    part = {}
    at_ = 0
    for name, n in (("nq", 512), ("nk", 512), ("nv", 512), ("hq", 512), ("ff", 512), ("fb", 512), ("hi", 512),
                    ("hg", 512), ("gq", 512), ("gkv", 256), ("gate", 3 * D)):
        part[name] = w_in[:, at_:at_ + n]
        at_ += n
    part["gq"] = part["gq"].reshape(D, 2, NH // 2, HD).transpose(0, 2, 1, 3).reshape(D, NH * HD)
    ada = weight_slots(a["w_ada"][0])
    gate = weight_slots(part["gate"])
    front = []
    for name in FRONT:
        if name[:3] == "ada":
            s = ada[int(name[3:])]
        elif name[:4] == "gate":
            s = gate[int(name[4:])]
        elif name == "gkv":
            s = np.zeros((P, SLOT), np.float32)
            s[:, 0:SLOT // 2] = weight_slots(part["gkv"], 256)[0]
        elif name[:2] == "br":
            s = weight_slots(a["w_branch"][0, int(name[2])], D)[0]
        elif name[:3] == "out":
            s = weight_slots(a["w_out"][0])[int(name[3])]
        else:
            s = weight_slots(part[name])[0]
        front.append(s)
    experts = []
    for e in range(NE):
        experts += [weight_slots(a["w_exp_gate"][0, e])[0], weight_slots(a["w_exp_up"][0, e])[0],
                    weight_slots(a["w_exp_down"][0, e], D)[0]]
    small = dict(shape_constants())

    def swapped(g):
        return g.reshape(2, 2, HD // 4)[:, ::-1].reshape(HD)

    small.update({
        "b_ada": columns(a["b_ada"][0]), "g_mix": columns(a["g_mix"][0]), "g_ffn": columns(a["g_ffn"][0]),
        "lb": columns(a["hg_lb_logits"][0].reshape(-1)), "hg_g": columns(a["hg_norm_g"][0]),
        "gqn": np.tile(a["gqa_qnorm_g"][0], (P, 1)), "gqn_swapped": np.tile(swapped(a["gqa_qnorm_g"][0]), (P, 1)),
        "gkn": np.tile(a["gqa_knorm_g"][0], (P, 1)), "gkn_swapped": np.tile(swapped(a["gqa_knorm_g"][0]), (P, 1)),
        "router_b": np.tile(np.concatenate([a["b_group_router"][0], a["b_expert_router"][0]]), (P, 1)),
        "router": np.concatenate([a["w_group_router"][0], a["w_expert_router"][0]], axis=1)
                    .reshape(KD, P, ROUTES).transpose(1, 0, 2),
    })
    arrays = {
        "xcT": xc.T.reshape(KD, P, 2 * L).transpose(1, 0, 2),
        "x_nat": x.reshape(NT, P, D).transpose(1, 0, 2),
        "cvec": np.stack([a["c"][0], a["c_ctx"]], axis=-1).reshape(KD, P, 2).transpose(1, 0, 2),
        "front_w": np.stack(front), "expert_w": np.stack(experts),
        "na_bias": bias_layout(a["na_rpb"][0]),
        "small_w": np.concatenate([small[n].reshape(P, -1) for n in SM], axis=1),
        "level_masks": level_masks(),
        "g_last": np.tile(a["g_final"], (P, 1)),
    }
    arrays = {k: np.ascontiguousarray(v) for k, v in arrays.items()}
    nc = bacc.Bacc("TRN2", target_bir_lowering=False, num_devices=1)
    d = {n: nc.dram_tensor(n, v.shape, mybir.dt.from_np(v.dtype), kind="ExternalInput").ap() for n, v in arrays.items()}
    d["out"] = nc.dram_tensor("out", (L, D), F32, kind="ExternalOutput").ap()
    build(nc, d)
    r = run_bass_kernel_spmd(nc, [arrays], core_ids=[0])
    return r.results[0]["out"].reshape(1, L, D)
```

```python
import numpy as np
import concourse.bass as bass
from concourse import mybir
from concourse.alu_op_type import AluOpType as ALU
from contextlib import ExitStack

F32 = mybir.dt.float32
I32 = mybir.dt.int32
I8 = mybir.dt.int8
ACT = mybir.ActivationFunctionType
AX = mybir.AxisListType

P = 128
D = 1024
KD = D // P
L = 256
NT = L // P
GRID = 64
ROWS = L // GRID
WR, WC = 8, 16
HD = 64
NH = 8
HGH = 4
NE = 16
NG = 4
EPG = NE // NG
EH = 512
KH = EH // P
BW = NH * HD
CAP = 64
PAIRS = NE // 2
MAXPASS = L // CAP
EPS = 1e-6
QSCALE = HD ** -0.5
NEG = -1e30
RB = ROWS + 2
ROUTES = NG + NE

FRONT = ["ada0", "ada1", "ada2", "ada3", "ff", "fb", "hq", "hg", "hi", "nk", "nq", "nv", "gq", "gkv"]
FRONT += ["gate0", "ada4", "gate1", "ada5", "gate2", "ada6", "gate3", "ada7", "gate4", "ada8", "ada9", "gate5",
          "ada10", "ada11"]
FRONT += ["br0", "br1", "br2", "out0", "out1"]
FSLOTS = 3
SLOTS = 6
SLOT = 4096
FUSES = len(FRONT) // FSLOTS
assert FUSES * FSLOTS == len(FRONT)



def group_fills(name):
    if name[:3] == "ada":
        n = 1
    elif name in ("ff", "fb", "hi", "nk", "nv"):
        n = 4
    elif name[:2] in ("br",):
        n = 4
    else:
        n = 2
    return [(name, i, "dve" if name[:2] in ("br", "ou") else "act") for i in range(n)]


FILLS = [f for g in FRONT for f in group_fills(g)]
PBANKS = 3
ROW_GROUPS = (4, 5, 10, 11)


def fill_no(name, i=0):
    return [f[:2] for f in FILLS].index((name, i))


def emptied(n):
    who = FILLS[n][2]
    return who, sum(f[2] == who for f in FILLS[:n + 1])


UNITS = [(k, t, c) for k in ("na", "gq") for t in range(NT) for c in range(4)]
STEPS = len(UNITS)
FILLER = [n for n in range(fill_no("gq"), fill_no("br0"))]


def cost(n):
    return 1 if FILLS[n][0][:3] == "ada" else 4


FILLER_AT = {i: [] for i in range(STEPS)}
_spent = 0
for _n in FILLER:
    FILLER_AT[_spent * STEPS // sum(cost(n) for n in FILLER)].append(_n)
    _spent += cost(_n)
G_STEP = [i for i in range(STEPS) if fill_no("gkv", 1) in FILLER_AT[i]][0]
GATE_FILLS = fill_no("gate5", 1)

LEVELS = 8
SHARED = [("ada", g) for g in range(4)] + [("kc", i) for i in range(4)]
SHARED += [(f"lev{v}", i) for v in range(LEVELS) for i in range(4)] + [("s0", i) for i in range(2)]
SHARED += [("lev8", i) for i in range(2)] + [("o", i) for i in range(2)] + [("osq", i) for i in range(2)]


def ada_in_step(i):
    return [int(FILLS[n][0][3:]) for n in FILLER_AT.get(i, []) if FILLS[n][0][:3] == "ada"]


for _i in range(STEPS + 1):
    SHARED += [("ada", g) for g in ada_in_step(_i - 1)]
    if _i == 2 * 4:
        SHARED += [("gqT", 0), ("gqT", 1), ("gkT", 0)]
    if _i < STEPS:
        SHARED += [("pT", 2 * _i), ("pT", 2 * _i + 1)]
SHARED += [("fT", i) for i in range(4)] + [("rT", 0)] + [("sT", i) for i in range(4)]


def shared_no(name, i=0):
    return SHARED.index((name, i))


def build(nc, d):
    ctx = ExitStack()
    with ctx:
        TOTAL = 52740
        sb = ctx.enter_context(nc.sbuf_tensor("sb", [P, TOTAL], F32))
        banks = [ctx.enter_context(nc.psum_tensor(f"bank{i}", [P, 512], F32)) for i in range(8)]
        proj = banks[0:3]
        shared = banks[3:5]
        score = banks[5:7]
        pv_bank = banks[7]

        def at(start, *dims):
            n = int(np.prod(dims))
            v = sb[:, start:start + n]
            if len(dims) == 2:
                v = v.rearrange("p (a b) -> p a b", b=dims[1])
            if len(dims) == 3:
                v = v.rearrange("p (a b c) -> p a b c", b=dims[1], c=dims[2])
            return v

        slot = [at(i * SLOT, SLOT) for i in range(SLOTS)]
        A0 = FSLOTS * SLOT
        na_k = at(A0, 4, 2 * L)
        na_v = at(A0 + 2048, 4, 512)
        sig_q, sig_g = at(A0 + 2048, 4, L), at(A0 + 3072, 4, L)
        na_bias = at(A0 + 4096, NH, RB * GRID)
        X = at(A0 + 7168, 8, L)
        Y = at(A0 + 9216, 8, L)
        sq = at(A0 + 7168, KD, 512)
        probs = at(A0 + 7168, 2, 512)
        probsT = at(A0 + 8192, 2, 512)
        ada_late = at(A0 + 9216, 2, 512)
        ada_early = at(A0, 2, 512)
        gkv = at(A0 + 11264, 4, 256)
        B0 = A0 + (SLOTS - FSLOTS) * SLOT
        hT = at(B0, KD, 2 * L)
        xn, fT = at(B0, NT, D), at(B0 + 2048, KD, L)
        F0 = B0 + 4096
        T_lat = at(F0, 8, L)
        masks_wide = at(F0, 2 * (LEVELS - 1), P)
        forget = at(F0, 2, 8, L)
        F_ctx = at(F0 + 2048, 8, L)
        Kc = at(F0 + 4096, 8, L)
        kcn = at(F0 + 6144, 8, L)
        gates = at(F0 + 2048, 3 * KD, L)
        o_sb, o_tmp = at(F0, 4, L), at(F0 + 1024, 4, L)
        b_rows = at(F0, 4, 512)
        SW = at(F0, NT, NE * CAP)
        yacc = at(F0 + 2048, NT, D)
        S_all = at(F0 + 4096, NT, NE * CAP)
        ST_all = at(F0 + 6144, PAIRS, NT * P)
        C0 = F0 + 8192
        T_alt = at(C0, 1024)
        rstd_row = at(C0, 512)
        QR = at(C0 + 1024, 4, L)
        row5 = at(C0 + 1024, D)
        v_hg = at(C0 + 2048, 4, 512)
        x_nat = at(C0 + 2048, NT, D)
        AT = at(C0 + 4096, 6, 512)
        yT = at(C0 + 4096, KD, L)
        g_sq = at(C0 + 4096, 1536)
        g_rot = at(C0 + 5632, NT, 512)
        k_rot = at(C0 + 6656, NT, 128)
        h_sb = at(C0 + 4096, KD, P)
        y_sb = at(C0 + 5120, D)
        he = at(C0 + 6144, EH)
        heT = at(C0 + 6656, KH, P)
        sl = at(C0 + 11264, EH)
        logits_sb = at(C0 + 6144, L)
        S0 = at(C0 + 7168, 8, P)
        row2 = at(C0 + 7168, D)
        bT = at(C0 + 8192, 4, L)
        na_q = at(C0 + 9216, 4, L)
        aT = na_q
        S_now, ST_now = at(C0 + 9216, NT, P), at(C0 + 9472, NT, P)
        gq = at(C0 + 10240, NT, 512)
        g_last = at(C0 + 10240, D)
        gqT = at(C0 + 11264, 4, L)
        cT = gqT
        gkT = at(C0 + 12288, 512)
        E0 = C0 + 12800
        consts = {}
        pos = [E0]

        def keep(n, *dims):
            v = at(pos[0], *dims) if dims else at(pos[0], n)
            pos[0] += n
            assert pos[0] <= TOTAL, pos[0]
            return v

        small = keep(SMALL)
        def sm(name):
            o, dims = SM[name]
            return small[:, o:o + int(np.prod(dims))] if len(dims) == 1 else at(E0 + o, *dims)
        ident, ones, below, slots_iota = sm("ident"), sm("ones"), sm("below"), sm("iota")
        cvec = keep(KD * 32, KD, 32)
        mod = keep(96, 48, 2)
        A_mix, A_ffn = keep(16, KD, 2), keep(8)
        lower, span = keep(8), keep(8)
        lb_e, lb_p = keep(8), keep(8)
        g_ms = keep(24)
        qcos, qsin = keep(128, NT, HD), keep(128, NT, HD)
        kcos, ksin = keep(128, NT, HD), keep(128, NT, HD)
        nmax = keep(32)
        sums = keep(32)
        stat = keep(8)
        zeros = at(C0 + 512, 256)
        r_g, r_e = keep(8, NT, NG), keep(32, NT, NE)
        r_all = keep(2 * ROUTES, NT, ROUTES)
        first_sum = keep(16)
        r_gm, r_gs, r_sm = keep(2), keep(2), keep(2)
        r_m1, r_m2, r_w1, r_w2, r_d = keep(2), keep(2), keep(2), keep(2), keep(2)
        r_t, r_sel, r_eg = keep(8, NT, NG), keep(8, NT, NG), keep(8, NT, NG)
        r_em, r_et = keep(32, NT, NE), keep(32, NT, NE)
        oh1, oh2 = keep(32, NT, NE), keep(32, NT, NE)
        member, comb, posm = keep(32, NT, NE), keep(32, NT, NE), keep(32, NT, NE)
        count, over = keep(1), keep(3)
        passes_f = keep(1)
        masks = ctx.enter_context(nc.sbuf_tensor("masks", [P, 2 * (LEVELS - 1), P], I8))
        passes = ctx.enter_context(nc.sbuf_tensor("passes", [1, 1], I32))

        def sem(name):
            return ctx.enter_context(nc.semaphore(name))

        x_in = [sem("x_in0"), sem("x_in1")]
        c_in, small_in, bias_in, masks_in, xnat_in, glast_in = [sem(n) for n in (
            "c_in", "small_in", "bias_in", "masks_in", "xnat_in", "glast_in")]
        w_in_ = [sem(f"weights_in{i}") for i in range(SLOTS)]
        w_used = sem("weights_used")
        fill_ready = sem("fill_ready")
        out_by = {"act": sem("fill_out_act"), "dve": sem("fill_out_dve")}
        shared_ready, shared_out = sem("shared_ready"), sem("shared_out")
        masks_ready = sem("masks_ready")
        sq_ready, rms_ready, rms_root, c_ready = sem("sq_ready"), sem("rms_ready"), sem("rms_root"), sem("c_ready")
        h_ready = sem("h_ready")
        lb_in, lb_ready = sem("lb_in"), sem("lb_ready")
        silu_hg = sem("silu_hg")
        kc_ready = sem("kc_ready")
        xy_ready = sem("xy_ready")
        hg_read = sem("hg_read")
        o_sq, o_root, b_ready = sem("o_sq"), sem("o_root"), sem("b_ready")
        g_sum, g_root, g_rec, gqa_ready = sem("g_sum"), sem("g_root"), sem("g_rec"), sem("gqa_ready")
        g_tab = sem("g_tab")
        scores_ready, max_ready, exp_ready = sem("scores_ready"), sem("max_ready"), sem("exp_ready")
        norm_ready, pv_ready, pv_out = sem("norm_ready"), sem("pv_ready"), sem("pv_out")
        sig_gates = sem("sig_gates")
        brow_in = sem("brow_in")
        x1_ready, x1_sum, x1_root, xn_ready = sem("x1_ready"), sem("x1_sum"), sem("x1_root"), sem("xn_ready")
        router_ready, logits_ready, gexp_in, gexp_out = sem("router_ready"), sem("logits_ready"), sem("gexp_in"), sem("gexp_out")
        member_ready, pos_ready, passes_ready = sem("member_ready"), sem("pos_ready"), sem("passes_ready")
        slots_ready, weighted, turned_slots = sem("slots_ready"), sem("weighted_slots"), sem("turned_slots")
        cut_ready, cutT_ready = sem("cut_for_gather"), sem("cut_for_scatter")
        gather_ready, h_out = sem("gather_ready"), sem("h_out")
        gate_ready, up_ready, silu_ready = sem("gate_ready"), sem("up_ready"), sem("silu_ready")
        he_ready, turned, heT_ready = sem("he_ready"), sem("hidden_turned"), sem("heT_ready")
        down_ready, y_out = sem("down_ready"), sem("y_out")
        scat_ready, scat_out = sem("scat_ready"), sem("scat_out")
        fin_sum, fin_root, fin_ready, stored = sem("fin_sum"), sem("fin_root"), sem("fin_ready"), sem("stored")
        v_step, p_step, a_step = sem("vector_step"), sem("pool_step"), sem("scalar_step")

        block = ctx.enter_context(nc.Block())

        def wait_emptied(eng, n):
            who, count_ = emptied(n)
            eng.wait_ge(out_by[who], count_)

        def ada_place(g):
            return (ada_early if g < 4 else ada_late)[:, g % 2, :]

        def slot_value(s):
            return 16 * FUSES if s < FSLOTS else 0

        @block.sync
        def _(sp):
            for i in range(2):
                sp.dma_start(hT[:, 4 * i:4 * i + 4, :], d["xcT"][:, 4 * i:4 * i + 4, :]).then_inc(x_in[i], 16)
            for n, name in enumerate(FRONT):
                if n >= FSLOTS:
                    sp.wait_ge(w_used, n - FSLOTS + 1)
                cols = SLOT // 2 if name == "gkv" else SLOT
                sp.dma_start(slot[n % FSLOTS][:, 0:cols], d["front_w"][n, :, 0:cols]).then_inc(w_in_[n % FSLOTS], 16)
                if name == "nq":
                    sp.dma_start(na_bias, d["na_bias"]).then_inc(bias_in, 16)
                if name == "ff":
                    sp.dma_start(masks_wide, d["level_masks"]).then_inc(masks_in, 16)
                if name == "gate2":
                    sp.wait_ge(b_ready, 1)
                    sp.dma_start(b_rows, d["b_rows"]).then_inc(brow_in, 16)
                    sp.dma_start(x_nat, d["x_nat"]).then_inc(xnat_in, 16)

            def load(s, row):
                sp.dma_start(slot[s], d["expert_w"][bass.ds(row, 1), :, :].rearrange("a p n -> p (a n)")
                             if not isinstance(row, int) else d["expert_w"][row, :, :]).then_inc(w_in_[s], 16)

            def load_pair(before, j, first=False):
                for s in range(SLOTS):
                    part = (s % 2) * 3 + s // 2
                    if first and s < FSLOTS:
                        sp.wait_ge(w_used, len(FRONT) - FSLOTS + s + 1)
                    elif first:
                        sp.wait_ge(shared_out, shared_no("pT", 2 * STEPS - 1) + 1)
                        sp.wait_ge(pv_out, 4)
                    else:
                        sp.wait_ge((gate_ready, up_ready, down_ready)[s // 2], before + 1)
                    load(s, j * 6 + part)

            load_pair(0, 0, first=True)
            with sp.Fori(0, PAIRS - 1) as j:
                load_pair(j, j + 1)
            sp.wait_ge(passes_ready, 2)
            n_pass = sp.value_load(passes[0:1, 0:1], min_val=1, max_val=MAXPASS)
            with sp.If(n_pass > 1):
                with sp.Fori(0, n_pass - 1) as p:
                    with sp.Fori(0, PAIRS) as j:
                        load_pair(p * PAIRS + j + (PAIRS - 1), j)
            sp.wait_ge(fin_ready, 1)
            for t in range(NT):
                if t:
                    sp.wait_ge(fin_ready, t + 1)
                sp.dma_start(d["out"][t * P:(t + 1) * P, :], yacc[:, t, :]).then_inc(stored, 16)
            sp.wait_ge(stored, 16 * NT)

        @block.gpsimd
        def _(pool):
            steps = [0]

            def link(ins):
                steps[0] += 1
                ins.then_inc(p_step, 1)
                pool.wait_ge(p_step, steps[0])

            pool.wait_ge(masks_in, 16)
            pool.tensor_copy(masks[:, :, :], masks_wide).then_inc(masks_ready, 1)
            pool.wait_ge(small_in, 16)
            for c_, s_, g in ((qcos, qsin, "gqn"), (kcos, ksin, "gkn")):
                gn = sm(g).unsqueeze(1).broadcast_to([P, NT, HD])
                gs = sm(g + "_swapped").unsqueeze(1).broadcast_to([P, NT, HD])
                pool.tensor_tensor(c_, sm("cos"), gn, ALU.mult)
                last = pool.tensor_tensor(s_, sm("sin"), gs, ALU.mult)
            last.then_inc(g_tab, 1)

            pool.wait_ge(g_tab, 1)
            pool.wait_ge(g_rec, 1)
            rq = g_ms[:, 0:16].unsqueeze(2).broadcast_to([P, 16, HD])
            rk = g_ms[:, 16:24].rearrange("p (a b) -> p a b", b=2).unsqueeze(3).broadcast_to([P, 4, 2, HD])
            q16 = gq.rearrange("p t (h c) -> p (t h) c", c=HD)
            k4 = gkv[:, :, 0:128].rearrange("p t (h c) -> p t h c", c=HD)
            link(pool.tensor_tensor(q16, q16, rq, ALU.mult))
            link(pool.tensor_tensor(k4, k4, rk, ALU.mult))
            for x, rot, c_, s_, nh in ((gq, g_rot, qcos, qsin, NH), (gkv, k_rot, kcos, ksin, 2)):
                for t in range(NT):
                    xv = x[:, t, 0:nh * HD].rearrange("p (h a f c) -> p h a f c", a=2, f=2, c=16)
                    rv = rot[:, t, :].rearrange("p (h a f c) -> p h a f c", a=2, f=2, c=16)
                    sv = s_[:, t, :].rearrange("p (a f c) -> p a f c", a=2, f=2)
                    for f in range(2):
                        ins = pool.tensor_tensor(rv[:, :, :, f, :], xv[:, :, :, 1 - f, :],
                                                 sv[:, :, f, :].unsqueeze(1).broadcast_to([P, nh, 2, 16]), ALU.mult)
                    link(ins)
                    xh = x[:, t, 0:nh * HD].rearrange("p (h c) -> p h c", c=HD)
                    link(pool.tensor_tensor(xh, xh, c_[:, t, :].unsqueeze(1).broadcast_to([P, nh, HD]), ALU.mult))
                    link(pool.tensor_tensor(x[:, t, 0:nh * HD], x[:, t, 0:nh * HD], rot[:, t, :], ALU.add))
            kx = gkv[:, NT:4, 0:128].rearrange("p t (h c) -> p t h c", c=HD)
            gk = sm("gkn").unsqueeze(1).unsqueeze(1).broadcast_to([P, 2, 2, HD])
            pool.tensor_tensor(kx, kx, gk, ALU.mult).then_inc(gqa_ready, 1)

            def cut_gather(n, j, first=False):
                if not first:
                    pool.wait_ge(gather_ready, n)
                pool.tensor_copy(S_now, S_all[:, :, bass.ds(j * P, P)]).then_inc(cut_ready, 1)

            def cut_scatter(n, j, p, first=False):
                pool.wait_ge(turned_slots, p + 1)
                if not first:
                    pool.wait_ge(scat_ready, 4 * n)
                srcT = ST_all[:, bass.ds(j, 1), :].rearrange("p a (t c) -> p (a t) c", t=NT)
                pool.tensor_copy(ST_now, srcT).then_inc(cutT_ready, 1)

            pool.wait_ge(slots_ready, 1)
            cut_gather(0, 0, True)
            cut_gather(1, 1)
            cut_scatter(0, 0, 0, True)
            with pool.Fori(1, PAIRS - 1) as j:
                cut_gather(j + 1, j + 1)
                cut_scatter(j, j, 0)
            cut_scatter(PAIRS - 1, PAIRS - 1, 0)
            pool.wait_ge(passes_ready, 2)
            n_pass = pool.value_load(passes[0:1, 0:1], min_val=1, max_val=MAXPASS)
            with pool.If(n_pass > 1):
                with pool.Fori(1, n_pass) as p:
                    n0 = p * PAIRS
                    with pool.Fori(0, PAIRS) as j:
                        pool.wait_ge(slots_ready, p + 1)
                        cut_gather(n0 + j, j)
                        cut_scatter(n0 + j, j, p)
            pool.nop()

        @block.scalar
        def _(act):
            act.dma_start(cvec, d["cvec"]).then_inc(c_in, 16)
            act.dma_start(small, d["small_w"]).then_inc(small_in, 16)
            act.wait_ge(c_in, 16)
            act.activation(cvec, cvec, ACT.Silu).then_inc(c_ready, 1)
            for k in range(KD):
                if k % 4 == 0:
                    act.wait_ge(x_in[k // 4], 16)
                act.activation(sq[:, k, :], hT[:, k, :], ACT.Square).then_inc(sq_ready, 1)
            act.wait_ge(rms_ready, 1)
            act.wait_ge(small_in, 16)
            act.activation(rstd_row, pv_bank[:, :], ACT.Sqrt, bias=sm("eps"), scale=1.0 / D).then_inc(rms_root, 1)

            act.wait_ge(lb_in, 1)
            act.activation(lb_e, lb_e, ACT.Exp).then_inc(lb_ready, 1)

            def fill(n):
                name, i, who = FILLS[n]
                assert who == "act"
                ps = proj[n % PBANKS]
                act.wait_ge(fill_ready, n + 1)
                two = ps[:, :].rearrange("p (a b) -> p a b", a=2)
                done = out_by["act"]
                if name[:3] == "ada":
                    g = int(name[3:])
                    if g % 4 >= 2 or g > 4:
                        act.wait_ge(shared_ready, shared_no("ada", g - 2) + 1)
                    act.activation(ada_place(g), ps[:, :], ACT.Copy).then_inc(done, 1)
                elif name in ("ff", "fb"):
                    if (name, i) == ("ff", 0):
                        act.wait_ge(masks_ready, 1)
                    act.activation(forget[:, :, 4 * (name == "fb") + i, :], two, ACT.Sigmoid).then_inc(done, 1)
                elif name in ("hq", "hg"):
                    raw, sig = (QR, sig_q) if name == "hq" else (bT, sig_g)
                    act.activation(raw[:, 2 * i:2 * i + 2, :], two, ACT.Copy)
                    act.activation(sig[:, 2 * i:2 * i + 2, :], two, ACT.Sigmoid).then_inc(done, 1)
                elif name == "hi":
                    act.activation(v_hg[:, i, :], ps[:, :], ACT.Copy).then_inc(done, 1)
                elif name == "nk":
                    act.activation(na_k[:, i, :], ps[:, :], ACT.Copy).then_inc(done, 1)
                elif name == "nq":
                    act.activation(na_q[:, 2 * i:2 * i + 2, :], two, ACT.Copy, scale=QSCALE).then_inc(done, 1)
                elif name == "nv":
                    if i == 0:
                        act.wait_ge(silu_hg, 2)
                    act.activation(na_v[:, i, :], ps[:, :], ACT.Copy).then_inc(done, 1)
                elif name == "gq":
                    act.activation(gq[:, i, :], ps[:, :], ACT.Copy).then_inc(done, 1)
                elif name == "gkv":
                    act.activation(gkv[:, 2 * i:2 * i + 2, :], two, ACT.Copy).then_inc(done, 1)
                elif name[:4] == "gate":
                    c = 4 * int(name[4:]) + 2 * i
                    if c == 0:
                        act.wait_ge(shared_out, shared_no("s0", 1) + 1)
                    act.activation(gates[:, c:c + 2, :], two, ACT.Copy).then_inc(done, 1)

            for n in range(fill_no("nv", 2) + 1):
                fill(n)
            act.wait_ge(shared_out, shared_no("o", 1) + 1)
            act.activation(o_tmp, o_sb, ACT.Square).then_inc(o_sq, 1)
            fill(fill_no("nv", 3))
            for i in range(2):
                act.wait_ge(shared_ready, shared_no("osq", i) + 1)
                act.activation(o_tmp[:, 2 * i:2 * i + 2, :],
                               shared[shared_no("osq", i) % 2][:, :].rearrange("p (a b) -> p a b", a=2),
                               ACT.Sqrt, bias=sm("eps"), scale=1.0 / P).then_inc(o_root, 1)
            for i in range(STEPS):
                for e in range(2):
                    act.wait_ge(max_ready, 2 * i + e + 1)
                    if i:
                        act.wait_ge(shared_ready, shared_no("pT", 2 * i - 2 + e) + 1)
                    act.activation(probs[:, e, :], score[e][:, :], ACT.Exp, bias=nmax[:, 2 * i + e:2 * i + e + 1],
                                   accum_out=sums[:, 2 * i + e:2 * i + e + 1]).then_inc(exp_ready, 1)
                for n in FILLER_AT[i]:
                    fill(n)
                if i == G_STEP:
                    act.wait_ge(g_sum, 1)
                    act.activation(g_ms, g_ms, ACT.Sqrt, bias=sm("eps"), scale=1.0 / HD).then_inc(g_root, 1)
            act.wait_ge(out_by["act"], emptied(GATE_FILLS)[1])
            for b in range(3):
                act.activation(gates[:, b * KD:(b + 1) * KD, :], gates[:, b * KD:(b + 1) * KD, :],
                               ACT.Sigmoid).then_inc(sig_gates, 1)
            for t in range(NT):
                act.wait_ge(x1_ready, 2 * NT - NT + t + 1)
                act.activation(xn[:, t, :], x_nat[:, t, :], ACT.Square, accum_out=stat[:, t:t + 1]).then_inc(x1_sum, 1)
            act.wait_ge(x1_sum, NT)
            act.activation(stat[:, 0:NT], stat[:, 0:NT], ACT.Sqrt, bias=sm("eps"), scale=1.0 / D).then_inc(x1_root, 1)
            act.dma_start(g_last, d["g_last"]).then_inc(glast_in, 16)
            act.wait_ge(router_ready, 1)
            act.activation(logits_sb, pv_bank[:, 0:L], ACT.Copy).then_inc(a_step, 1)
            act.wait_ge(gexp_in, 1)
            act.activation(r_eg, r_eg, ACT.Exp).then_inc(gexp_out, 1)
            act.wait_ge(gexp_in, 2)
            act.activation(r_d, r_d, ACT.Exp).then_inc(gexp_out, 1)

            def pair(before, first=False):
                n = before + 1
                act.wait_ge(gate_ready, n + 1)
                if not first:
                    act.wait_ge(he_ready, before + 1)
                act.activation(sl, banks[2][:, :], ACT.Silu).then_inc(silu_ready, 1)
                act.wait_ge(turned, n + 1)
                if not first:
                    act.wait_ge(down_ready, before + 1)
                act.activation(heT, banks[6][:, :].rearrange("p (a b) -> p a b", b=P), ACT.Copy).then_inc(heT_ready, 1)
                act.wait_ge(down_ready, n + 1)
                if not first:
                    act.wait_ge(scat_ready, 4 * before + 4)
                for i in range(2):
                    act.activation(y_sb[:, 512 * i:512 * i + 512], banks[4 + i][:, :], ACT.Copy).then_inc(y_out, 1)

            pair(-1, True)
            with act.Fori(0, PAIRS - 1) as j:
                pair(j)
            act.wait_ge(passes_ready, 2)
            n_pass = act.value_load(passes[0:1, 0:1], min_val=1, max_val=MAXPASS)
            with act.If(n_pass > 1):
                with act.Fori(PAIRS - 1, n_pass * PAIRS - 1) as j:
                    pair(j)
            for t in range(NT):
                act.wait_ge(fin_sum, t + 1)
                act.activation(SW[:, t, :], x_nat[:, t, :], ACT.Square, accum_out=stat[:, 2 + t:3 + t]).then_inc(a_step, 1)
            act.wait_ge(a_step, NT + 1)
            act.activation(stat[:, 2:4], stat[:, 2:4], ACT.Sqrt, bias=sm("eps"), scale=1.0 / D).then_inc(fin_root, 1)

        @block.tensor
        def _(pe):
            def take_slot(n):
                pe.wait_ge(w_in_[n % FSLOTS], 16 * (n // FSLOTS + 1))

            def lhs(w, k, c, width=512):
                return w[:, k * width + c:k * width + c + P]

            def fill(n):
                name, i, _ = FILLS[n]
                ps = proj[n % PBANKS]
                if n >= PBANKS:
                    wait_emptied(pe, n - PBANKS)
                g = FRONT.index(name)
                w = slot[g % FSLOTS]
                if i == 0:
                    take_slot(g)
                if name[:3] == "ada":
                    for k in range(KD):
                        q = 32 * (k % 4)
                        ins = pe.matmul(ps[q:q + 32, :], cvec[:, k, :], w[:, k * 512:(k + 1) * 512],
                                        start=(k < 4), stop=(k >= KD - 4))
                elif name in ("ff", "fb", "nk"):
                    for k in range(KD):
                        if name == "ff" and i == 0:
                            pe.wait_ge(h_ready, k + 1)
                        ins = pe.matmul(ps[:, :], lhs(w, k, i * P), hT[:, k, :], start=(k == 0), stop=(k == KD - 1))
                elif name in ("hq", "hg", "nq") or name[:4] == "gate":
                    for c in range(2):
                        for k in range(KD):
                            ins = pe.matmul(ps[:, c * L:(c + 1) * L], lhs(w, k, (2 * i + c) * P), hT[:, k, 0:L],
                                            start=(k == 0), stop=(k == KD - 1))
                elif name in ("hi", "nv", "gq"):
                    for k in range(KD):
                        ins = pe.matmul(ps[:, :], hT[:, k, i * P:(i + 1) * P], w[:, k * 512:(k + 1) * 512],
                                        start=(k == 0), stop=(k == KD - 1))
                elif name == "gkv":
                    for c in range(2):
                        for k in range(KD):
                            t = 2 * i + c
                            ins = pe.matmul(ps[:, c * 256:(c + 1) * 256], hT[:, k, t * P:(t + 1) * P],
                                            w[:, k * 256:(k + 1) * 256], start=(k == 0), stop=(k == KD - 1))
                elif name[:2] == "br":
                    b = int(name[2])
                    src = (aT, bT, cT)[b]
                    for c in range(2):
                        for k in range(4):
                            ins = pe.matmul(ps[:, c * L:(c + 1) * L], lhs(w, k, (2 * i + c) * P, D), src[:, k, :],
                                            start=(k == 0), stop=(k == 3))
                elif name[:3] == "out":
                    for k in range(KD):
                        if name == "out0" and i == 0 and k % 2 == 0:
                            pe.wait_ge(out_by["dve"], 8 + k // 2 + 1)
                        ins = pe.matmul(ps[:, :], yT[:, k, i * P:(i + 1) * P], w[:, k * 512:(k + 1) * 512],
                                        start=(k == 0), stop=(k == KD - 1))
                ins.then_inc(fill_ready, 1)
                if n + 1 == len(FILLS) or FILLS[n + 1][0] != name:
                    pe.wait_ge(fill_ready, n + 1)
                    pe.sem_inc(w_used, 1)

            def take_shared(n):
                if n >= 2:
                    pe.wait_ge(shared_out, n - 1)
                return shared[n % 2]

            def level(v):
                pe.wait_ge(xy_ready, v + 1)
                for q in range(4):
                    dr, t = q // 2, q % 2
                    ps = take_shared(shared_no(f"lev{v}", q))
                    for h in range(HGH):
                        j = dr * 4 + h
                        kk = (X if dr else Y)[:, j, t * P:(t + 1) * P]
                        qq = (QR[:, h] if v == 0 else (Y if dr else X)[:, j])[:, t * P:(t + 1) * P]
                        ins = pe.matmul(ps[:, h * P:(h + 1) * P], kk, qq, start=True, stop=True)
                    ins.then_inc(shared_ready, 1)

            def across():
                pe.wait_ge(xy_ready, LEVELS + 1)
                for dr in range(2):
                    ps = take_shared(shared_no("lev8", dr))
                    for h in range(HGH):
                        kk = (X if dr else Y)[:, dr * 4 + h, dr * P:(dr + 1) * P]
                        qq = (Y if dr else X)[:, dr * 4 + h, (1 - dr) * P:(2 - dr) * P]
                        ins = pe.matmul(ps[:, h * P:(h + 1) * P], kk, qq, start=True, stop=True)
                    ins.then_inc(shared_ready, 1)

            def ctx_keys():
                pe.wait_ge(kc_ready, 1)
                for q in range(4):
                    dr, t = q // 2, q % 2
                    ps = take_shared(shared_no("kc", q))
                    for h in range(HGH):
                        ins = pe.transpose(ps[:, h * P:(h + 1) * P], Kc[:, dr * 4 + h, t * P:(t + 1) * P], ident)
                    ins.then_inc(shared_ready, 1)

            def ctx_state():
                pe.wait_ge(shared_out, shared_no("kc", 3) + 1)
                wait_emptied(pe, fill_no("hi", 3))
                for dr in range(2):
                    ps = take_shared(shared_no("s0", dr))
                    for h in range(HGH):
                        for t in range(NT):
                            ins = pe.matmul(ps[:, h * P:(h + 1) * P], kc_tile(dr, t, h), v_hg[:, NT + t, h * P:(h + 1) * P],
                                            start=(t == 0), stop=(t == NT - 1))
                    ins.then_inc(shared_ready, 1)

            def kc_tile(dr, t, h):
                o = F0 + 6144 + ((dr * 2 + t) * HGH + h) * P
                return sb[:, o:o + P]

            def outputs():
                pe.wait_ge(xy_ready, LEVELS + 2)
                pe.wait_ge(shared_out, shared_no("lev8", 1) + 1)
                for i in range(2):
                    ps = take_shared(shared_no("o", i))
                    for hh in range(2):
                        h = 2 * i + hh
                        for t in range(NT):
                            o = ps[:, hh * L + t * P:hh * L + (t + 1) * P]
                            for dr in range(2):
                                cols = slice(h * P, (h + 1) * P)
                                pe.matmul(o, v_hg[:, t, cols], AT[:, dr * 3 + t, cols], start=(dr == 0), stop=False)
                                if t != dr:
                                    pe.matmul(o, v_hg[:, dr, cols], AT[:, dr * 3 + 2, cols], start=False, stop=False)
                                qq = (Y if dr else X)[:, dr * 4 + h, t * P:(t + 1) * P]
                                ins = pe.matmul(o, S0[:, dr * 4 + h, :], qq, start=False, stop=(dr == 1))
                    ins.then_inc(shared_ready, 1)

            def square_sums():
                pe.wait_ge(o_sq, 1)
                for i in range(2):
                    ps = take_shared(shared_no("osq", i))
                    pe.matmul(ps[:, :], ones, o_tmp[:, 2 * i:2 * i + 2, :].rearrange("p a b -> p (a b)"),
                              start=True, stop=True).then_inc(shared_ready, 1)

            def turn_gqa():
                pe.wait_ge(gqa_ready, 1)
                for i in range(2):
                    ps = take_shared(shared_no("gqT", i))
                    for r in range(2):
                        for t in range(NT):
                            src = gq[:, t, (2 * i + r) * P:(2 * i + r + 1) * P]
                            ins = pe.transpose(ps[:, r * L + t * P:r * L + (t + 1) * P], src, ident)
                    ins.then_inc(shared_ready, 1)
                ps = take_shared(shared_no("gkT"))
                for t in range(4):
                    ins = pe.transpose(ps[:, t * P:(t + 1) * P], gkv[:, t, 0:P], ident)
                ins.then_inc(shared_ready, 1)

            def ada_turn(g):
                wait_emptied(pe, fill_no(f"ada{g}"))
                ps = take_shared(shared_no("ada", g))
                src = ada_place(g)
                if g in ROW_GROUPS:
                    ins = pe.matmul(ps[:, :], sm("stream0"), src, start=True, stop=True)
                else:
                    for c in range(4):
                        ins = pe.transpose(ps[:, c * P:(c + 1) * P], src[:, c * P:(c + 1) * P], ident)
                ins.then_inc(shared_ready, 1)

            def scores(i):
                kind, t, c = UNITS[i]
                if i:
                    pe.wait_ge(exp_ready, 2 * i)
                q, k = (na_q[:, c, :], na_k[:, c, :]) if kind == "na" else (gqT[:, c, :], gkT)
                for e in range(2):
                    b = e * HD
                    pe.matmul(score[e][:, :], q[b:b + HD, t * P:(t + 1) * P], k[b:b + HD, :],
                              start=True, stop=True).then_inc(scores_ready, 1)

            def turn_probs(i):
                for e in range(2):
                    pe.wait_ge(norm_ready, 2 * i + e + 1)
                    ps = take_shared(shared_no("pT", 2 * i + e))
                    for c in range(4):
                        ins = pe.transpose(ps[:, c * P:(c + 1) * P], probs[:, e, c * P:(c + 1) * P], ident)
                    ins.then_inc(shared_ready, 1)

            def values(i):
                kind, t, c = UNITS[i]
                pe.wait_ge(shared_out, shared_no("pT", 2 * i + 1) + 1)
                if i >= 4 and c == 0:
                    pe.wait_ge(pv_out, i // 4)
                for j in range(4):
                    for e in range(2):
                        v = na_v[:, j, (2 * c + e) * HD:(2 * c + e + 1) * HD] if kind == "na" else \
                            gkv[:, j, P + e * HD:P + (e + 1) * HD]
                        ins = pe.matmul(pv_bank[e * HD:(e + 1) * HD, c * P:(c + 1) * P], v,
                                        probsT[:, e, j * P:(j + 1) * P], start=(j == 0), stop=(j == 3))
                ins.then_inc(pv_ready, 1)

            pe.wait_ge(small_in, 16)
            for k in range(KD):
                pe.wait_ge(sq_ready, k + 1)
                ins = pe.matmul(pv_bank[:, :], ones, sq[:, k, :], start=(k == 0), stop=(k == KD - 1))
            ins.then_inc(rms_ready, 1)
            pe.wait_ge(c_ready, 1)
            for g in range(4):
                fill(fill_no(f"ada{g}"))
                if g:
                    ada_turn(g - 1)
            ada_turn(3)
            for n in range(fill_no("ff"), fill_no("hg", 1) + 1):
                fill(n)
            ctx_keys()
            for v in range(4):
                level(v)
                fill(fill_no("hi", v))
            for v in range(4, 8):
                level(v)
                fill(fill_no("nk", v - 4))
            ctx_state()
            fill(fill_no("nq", 0))
            across()
            fill(fill_no("nq", 1))
            fill(fill_no("nv", 0))
            outputs()
            for n in range(fill_no("nv", 1), fill_no("nv", 3) + 1):
                fill(n)
            square_sums()
            wait_emptied(pe, fill_no("nv", 3))
            for i in range(STEPS):
                for g in ada_in_step(i - 1):
                    ada_turn(g)
                if i == 2 * 4:
                    turn_gqa()
                    pe.wait_ge(shared_out, shared_no("gkT") + 1)
                scores(i)
                if i:
                    values(i - 1)
                for n in FILLER_AT[i]:
                    fill(n)
                turn_probs(i)
            for g in ada_in_step(STEPS - 1):
                ada_turn(g)
            values(STEPS - 1)
            for b in range(3):
                if b == 0:
                    pe.wait_ge(pv_out, 2)
                elif b == 1:
                    pe.wait_ge(b_ready, 1)
                else:
                    pe.wait_ge(pv_out, 4)
                for i in range(4):
                    fill(fill_no(f"br{b}", i))
            for n in range(fill_no("out0"), len(FILLS)):
                fill(n)
            for q in range(4):
                if q == 0:
                    pe.wait_ge(xn_ready, NT)
                ps = take_shared(shared_no("fT", q))
                for c in range(2):
                    for t in range(NT):
                        k = 2 * q + c
                        ins = pe.transpose(ps[:, c * L + t * P:c * L + (t + 1) * P], xn[:, t, k * P:(k + 1) * P], ident)
                ins.then_inc(shared_ready, 1)
            pe.wait_ge(shared_out, shared_no("fT", 3) + 1)
            pe.wait_ge(pv_out, 4)
            for k in range(KD):
                q = 32 * (k % 4)
                ins = pe.matmul(pv_bank[q:q + 32, 0:L], sm("router")[:, k, :], fT[:, k, :],
                                start=(k < 4), stop=(k >= KD - 4))
            ins.then_inc(router_ready, 1)
            pe.wait_ge(a_step, 1)
            ps = take_shared(shared_no("rT"))
            for t in range(NT):
                ins = pe.transpose(ps[:, t * P:(t + 1) * P], logits_sb[:, t * P:(t + 1) * P], ident)
            ins.then_inc(shared_ready, 1)
            pe.wait_ge(member_ready, 1)
            both = member.rearrange("p t n -> p (t n)")
            pe.matmul(pv_bank[:, 0:32], below, both, start=True, stop=True)
            pe.matmul(pv_bank[:, 32:64], ones, both, start=True, stop=True).then_inc(pos_ready, 1)

            def turn_slots(p):
                for q in range(4):
                    n = p * 4 + q
                    if q == 0:
                        pe.wait_ge(weighted, p + 1)
                    if isinstance(p, int) and q < 2:
                        take_shared(shared_no("sT", q))
                    else:
                        pe.wait_ge(shared_out, shared_no("sT") + n - 1)
                    ps = shared[(shared_no("sT") + q) % 2]
                    for c in range(4):
                        pr, t = 2 * q + c // 2, c % 2
                        ins = pe.transpose(ps[:, c * P:(c + 1) * P], SW[:, t, pr * P:(pr + 1) * P], ident)
                    ins.then_inc(shared_ready, 1)

            def gather(n):
                pe.wait_ge(cut_ready, n + 1)
                if not isinstance(n, int) or n:
                    pe.wait_ge(h_out, 2 * n)
                for i in range(2):
                    for c in range(4):
                        for t in range(NT):
                            ins = pe.matmul(banks[i][:, c * P:(c + 1) * P], xn[:, t, (4 * i + c) * P:(4 * i + c + 1) * P],
                                            S_now[:, t, :], start=(t == 0), stop=(t == NT - 1))
                    if i == 1:
                        ins.then_inc(gather_ready, 1)

            def two_experts(bank, n, s, parts, lhsT, cols):
                for e in range(2):
                    pe.wait_ge(w_in_[s + e], slot_value(s + e) + 16 * (n + 1))
                for k in range(parts):
                    for e in range(2):
                        ins = pe.matmul(bank[e * CAP:(e + 1) * CAP, :], lhsT[:, k, e * CAP:(e + 1) * CAP],
                                        slot[s + e][:, k * cols[0] + cols[1]:k * cols[0] + cols[1] + 512],
                                        start=(k == 0), stop=(k == parts - 1))
                return ins

            def gate_up(before, first=False):
                n = before + 1
                pe.wait_ge(h_out, 2 * n + 2)
                if not first:
                    pe.wait_ge(he_ready, before + 1)
                two_experts(banks[2], n, 0, KD, h_sb, (512, 0)).then_inc(gate_ready, 1)
                two_experts(banks[3], n, 2, KD, h_sb, (512, 0)).then_inc(up_ready, 1)

            def turn_hidden(n):
                pe.wait_ge(he_ready, n + 1)
                if not isinstance(n, int) or n > 1:
                    pe.wait_ge(scat_out, 4 * n - 4)
                for k in range(KH):
                    ins = pe.transpose(banks[6][:, k * P:(k + 1) * P], he[:, k * P:(k + 1) * P], ident)
                ins.then_inc(turned, 1)

            def down(n, first=False):
                pe.wait_ge(heT_ready, n + 1)
                if not first:
                    pe.wait_ge(y_out, 2 * n)
                for i in range(2):
                    ins = two_experts(banks[4 + i], n, 4, KH, heT, (D, 512 * i))
                ins.then_inc(down_ready, 1)

            def scatter(n, last=False):
                pe.wait_ge(y_out, 2 * n + 2)
                pe.wait_ge(cutT_ready, n + 1)
                for q in range(4):
                    t, i = q // 2, q % 2
                    if q == 0:
                        pe.wait_ge(heT_ready, n + (1 if last else 2))
                    if q > 1:
                        pe.wait_ge(scat_out, 4 * n + q - 1)
                    elif not isinstance(n, int) or n:
                        pe.wait_ge(scat_out, 4 * n)
                    pe.matmul(banks[6 + i][:, :], ST_now[:, t, :], y_sb[:, i * 512:(i + 1) * 512],
                              start=True, stop=True).then_inc(scat_ready, 1)

            def one_pass(p):
                first = isinstance(p, int)
                n0 = p * PAIRS
                gather(n0)
                turn_slots(p)
                pe.wait_ge(shared_out, shared_no("sT") + p * 4 + 4)
                gate_up(n0 - 1, first)
                gather(n0 + 1)
                turn_hidden(n0)
                down(n0, first)
                with pe.Fori(0, PAIRS - 2) as j:
                    before = n0 + j
                    gate_up(before)
                    gather(before + 2)
                    turn_hidden(before + 1)
                    scatter(before)
                    down(before + 1)
                before = n0 + PAIRS - 2
                gate_up(before)
                turn_hidden(before + 1)
                scatter(before)
                down(before + 1)
                scatter(before + 1, last=True)

            pe.wait_ge(passes_ready, 2)
            one_pass(0)
            n_pass = pe.value_load(passes[0:1, 0:1], min_val=1, max_val=MAXPASS)
            with pe.If(n_pass > 1):
                with pe.Fori(1, n_pass) as p:
                    one_pass(p)
            pe.nop()

        @block.vector
        def _(dve):
            steps = [0]

            def link(ins):
                steps[0] += 1
                ins.then_inc(v_step, 1)
                dve.wait_ge(v_step, steps[0])

            def shared_wait(n):
                dve.wait_ge(shared_ready, n + 1)
                return shared[n % 2]

            dve.memset(zeros, 0.0)
            dve.wait_ge(small_in, 16)
            lg = sm("lb")
            dve.tensor_tensor(lb_e, lg, lg, ALU.subtract).then_inc(lb_in, 1)
            dve.wait_ge(rms_root, 1)
            link(dve.reciprocal(rstd_row, rstd_row))
            for k in range(KD):
                ins = dve.tensor_tensor(hT[:, k, :], hT[:, k, :], rstd_row, ALU.mult)
            link(ins)
            def add_ada(g):
                n = shared_no("ada", g)
                ps = shared_wait(n)
                if g in ROW_GROUPS:
                    r = ROW_GROUPS.index(g)
                    if r == 0:
                        dve.wait_ge(brow_in, 16)
                    dst = (row2, row5)[r // 2][:, 512 * (r % 2):512 * (r % 2) + 512]
                    dve.tensor_tensor(dst, ps[:, :], b_rows[:, r, :], ALU.add).then_inc(shared_out, 1)
                else:
                    parts = ps[:, :].rearrange("p (c q s) -> p c s q", c=4, q=4)[:, :, 0:2, :]
                    dve.tensor_reduce(mod[:, 4 * g:4 * g + 4, :], parts, AX.X, ALU.add).then_inc(shared_out, 1)

            for g in range(4):
                add_ada(g)
            dve.wait_ge(shared_out, 4)
            b_ada = sm("b_ada")
            link(dve.tensor_tensor(mod[:, 0:16, :], mod[:, 0:16, :],
                                   b_ada[:, 0:16].unsqueeze(2).broadcast_to([P, 16, 2]), ALU.add))
            link(dve.tensor_scalar(A_mix, mod[:, 8:16, :], 1.0, None, ALU.add))
            link(dve.tensor_tensor(A_mix, A_mix, sm("g_mix").unsqueeze(2).broadcast_to([P, KD, 2]), ALU.mult))
            for k in range(KD):
                for s in range(2):
                    ins = dve.tensor_scalar(hT[:, k, s * L:(s + 1) * L], hT[:, k, s * L:(s + 1) * L],
                                            A_mix[:, k, s:s + 1], mod[:, k, s:s + 1], ALU.mult, ALU.add)
                ins.then_inc(h_ready, 1)
            dve.wait_ge(lb_ready, 1)
            link(dve.reciprocal(lb_p, lb_e))
            link(dve.tensor_tensor(lb_p, lb_e, lb_p, ALU.mult))
            link(dve.tensor_tensor(lower, lb_p, lb_p, ALU.subtract))
            link(dve.tensor_scalar(span, lower, -1.0, 1.0, ALU.mult, ALU.add))

            for dr in range(2):
                name = ("ff", "fb")[dr]
                for h in range(HGH):
                    j = dr * 4 + h
                    dve.wait_ge(out_by["act"], emptied(fill_no(name, h))[1])
                    ins = dve.tensor_scalar(forget[:, :, j, :], forget[:, :, j, :], span[:, j:j + 1],
                                            lower[:, j:j + 1], ALU.mult, ALU.add)
                link(ins)
                keys = (X if dr else Y)[:, dr * 4:dr * 4 + 4, :]
                link(dve.tensor_scalar(keys, T_lat[:, dr * 4:dr * 4 + 4, :], -1.0, 1.0, ALU.mult, ALU.add))
                dve.tensor_scalar(Kc[:, dr * 4:dr * 4 + 4, :], F_ctx[:, dr * 4:dr * 4 + 4, :], -1.0, 1.0,
                                  ALU.mult, ALU.add)
                for h in range(HGH):
                    j = dr * 4 + h
                    dst = kcn[:, j, :]
                    if dr == 0:
                        dve.memset(dst[:, L - 1:L], 1.0)
                        ins = dve.tensor_tensor_scan(dst[:, 0:L - 1][:, ::-1], F_ctx[:, j, 1:L][:, ::-1],
                                                     zeros[:, 0:L - 1], 1.0, ALU.mult, ALU.add)
                    else:
                        dve.memset(dst[:, 0:1], 1.0)
                        ins = dve.tensor_tensor_scan(dst[:, 1:L], F_ctx[:, j, 0:L - 1],
                                                     zeros[:, 0:L - 1], 1.0, ALU.mult, ALU.add)
                link(ins)
            link(dve.tensor_tensor(Kc, Kc, kcn, ALU.mult))
            dve.sem_inc(kc_ready, 1)
            dve.wait_ge(out_by["act"], emptied(fill_no("hq", 1))[1])
            dve.tensor_tensor(QR, QR, sig_q, ALU.mult).then_inc(silu_hg, 1)
            dve.wait_ge(silu_hg, 1)
            dve.tensor_tensor(X[:, 0:4, :], QR, T_lat[:, 0:4, :], ALU.mult)
            dve.tensor_tensor(Y[:, 4:8, :], QR, T_lat[:, 4:8, :], ALU.mult).then_inc(xy_ready, 2)
            dve.wait_ge(out_by["act"], emptied(fill_no("hg", 1))[1])
            dve.tensor_tensor(bT, bT, sig_g, ALU.mult).then_inc(silu_hg, 1)

            def shared_copy(n, dst):
                dve.tensor_copy(dst, shared_wait(n)[:, :]).then_inc(shared_out, 1)

            for q in range(4):
                o = F0 + 6144 + q * 512
                shared_copy(shared_no("kc", q), sb[:, o:o + 512])

            def products(v):
                for q in range(4):
                    dr, t = q // 2, q % 2
                    n = shared_no(f"lev{v}", q)
                    ps = shared_wait(n)[:, :].rearrange("p (h t) -> p h t", h=HGH)
                    dst = AT[:, dr * 3 + t, :].rearrange("p (h t) -> p h t", h=HGH)
                    if v == 0:
                        m = ident.unsqueeze(1).broadcast_to([P, HGH, P])
                        dve.tensor_tensor(dst, ps, m, ALU.mult).then_inc(shared_out, 1)
                    else:
                        m = masks[:, dr * (LEVELS - 1) + v - 1, :].unsqueeze(1).broadcast_to([P, HGH, P])
                        dve.wait_ge(shared_out, n - 3)
                        dve.copy_predicated(dst, m, ps).then_inc(shared_out, 1)

            def join(v):
                m = 1 << (v - 1)
                t_ = T_of[v - 1]
                pairs = t_.rearrange("p (b s) -> p b s", s=2)
                xv = at(A0 + 7168, 2048).rearrange("p (b s m) -> p b s m", s=2, m=m)
                yv = at(A0 + 9216, 2048).rearrange("p (b s m) -> p b s m", s=2, m=m)
                nb = 2048 // (2 * m)
                left = pairs[:, :, 0:1].broadcast_to([P, nb, m])
                right = pairs[:, :, 1:2].broadcast_to([P, nb, m])
                dve.tensor_tensor(xv[:, :, 1, :], xv[:, :, 1, :], left, ALU.mult)
                ins = dve.tensor_tensor(yv[:, :, 0, :], yv[:, :, 0, :], right, ALU.mult)
                if v < LEVELS:
                    ins.then_inc(xy_ready, 1)
                    dve.tensor_tensor(T_of[v], pairs[:, :, 0], pairs[:, :, 1], ALU.mult).then_inc(v_step, 1)
                    steps[0] += 1
                else:
                    ins.then_inc(xy_ready, 1)

            T_of = [at(F0, 2048)]
            for v in range(1, LEVELS):
                size = 2048 >> v
                T_of.append(at(C0 if v % 2 else F0, size))
            T_of.append(at(C0, 2048 >> LEVELS))

            dve.wait_ge(masks_ready, 1)
            products(0)
            for v in range(1, LEVELS):
                products(v)
                dve.wait_ge(v_step, steps[0])
                dve.wait_ge(xy_ready, v + 1)
                join(v)
            for q in range(2):
                shared_copy(shared_no("s0", q), S0[:, 4 * q:4 * q + 4, :].rearrange("p a b -> p (a b)"))
            for dr in range(2):
                shared_copy(shared_no("lev8", dr), AT[:, dr * 3 + 2, :])
            dve.wait_ge(v_step, steps[0])
            dve.wait_ge(xy_ready, LEVELS + 1)
            join(LEVELS)
            for q in range(2):
                shared_copy(shared_no("o", q), o_sb[:, 2 * q:2 * q + 2, :].rearrange("p a b -> p (a b)"))

            for i in range(2):
                dve.wait_ge(o_root, i + 1)
                dve.reciprocal(o_tmp[:, 2 * i:2 * i + 2, :], o_tmp[:, 2 * i:2 * i + 2, :]).then_inc(shared_out, 1)
            dve.wait_ge(shared_out, shared_no("osq", 1) + 1)
            link(dve.tensor_tensor(o_sb, o_sb, o_tmp, ALU.mult))
            dve.scalar_tensor_tensor(out=bT, in0=o_sb, scalar=sm("hg_g"), in1=bT, op0=ALU.mult, op1=ALU.mult)\
               .then_inc(b_ready, 1)

            def gqa_squares():
                wait_emptied(dve, fill_no("gkv", 1))
                q = gq.rearrange("p t n -> p (t n)")
                dve.tensor_tensor(g_sq[:, 0:1024], q, q, ALU.mult)
                k = gkv[:, :, 0:P]
                link(dve.tensor_tensor(g_sq[:, 1024:1536].rearrange("p (a b) -> p a b", b=P), k, k, ALU.mult))
                dve.tensor_reduce(g_ms, g_sq.rearrange("p (a b) -> p a b", b=HD), AX.X, ALU.add).then_inc(g_sum, 1)

            def gqa_norms():
                dve.wait_ge(g_root, 1)
                link(dve.reciprocal(g_ms, g_ms))
                dve.tensor_scalar(g_ms[:, 0:16], g_ms[:, 0:16], QSCALE, None, ALU.mult).then_inc(g_rec, 1)

            def maxima(i):
                kind, t, c = UNITS[i]
                if i == 0:
                    dve.wait_ge(bias_in, 16)
                for e in range(2):
                    dve.wait_ge(scores_ready, 2 * i + e + 1)
                    s = score[e]
                    if kind == "na":
                        i0 = 2 - 2 * t
                        link(dve.tensor_tensor(s[:, 0:L], s[:, 0:L],
                                               na_bias[:, 2 * c + e, i0 * GRID:(i0 + ROWS) * GRID], ALU.add))
                    u = 2 * i + e
                    dve.tensor_reduce(nmax[:, u:u + 1], s[:, :], AX.X, ALU.max, negate=True).then_inc(max_ready, 1)

            def normalise(i):
                dve.wait_ge(exp_ready, 2 * i + 2)
                r = sums[:, 2 * i:2 * i + 2]
                link(dve.reciprocal(r, r))
                for e in range(2):
                    dve.tensor_scalar(probs[:, e, :], probs[:, e, :], r[:, e:e + 1], None, ALU.mult).then_inc(norm_ready, 1)

            def values_out(k):
                dve.wait_ge(pv_ready, 4 * (k + 1))
                dst = (aT if k < 2 else cT)[:, :, (k % 2) * P:(k % 2 + 1) * P]
                dve.tensor_copy(dst, pv_bank[:, :].rearrange("p (c q) -> p c q", c=4)).then_inc(pv_out, 1)

            for i in range(STEPS):
                for g in ada_in_step(i - 1):
                    add_ada(g)
                if i == G_STEP + 1:
                    gqa_norms()
                if i == 2 * 4:
                    for q in range(2):
                        shared_copy(shared_no("gqT", q), gqT[:, 2 * q:2 * q + 2, :].rearrange("p a b -> p (a b)"))
                    shared_copy(shared_no("gkT"), gkT)
                maxima(i)
                normalise(i)
                if i:
                    if i % 4 == 0:
                        values_out(i // 4 - 1)
                    dve.wait_ge(pv_ready, i)
                for e in range(2):
                    shared_copy(shared_no("pT", 2 * i + e), probsT[:, e, :])
                if i == G_STEP:
                    gqa_squares()
            for g in ada_in_step(STEPS - 1):
                add_ada(g)
            values_out(3)

            dve.wait_ge(shared_out, shared_no("ada", 11) + 1)
            link(dve.tensor_tensor(mod[:, 24:40, 0], mod[:, 24:40, 0], b_ada[:, 24:40], ALU.add))
            link(dve.tensor_scalar(A_ffn, mod[:, 32:40, 0], 1.0, None, ALU.add))
            link(dve.tensor_tensor(A_ffn, A_ffn, sm("g_ffn"), ALU.mult))

            dve_out = out_by["dve"]
            for n in range(fill_no("br0"), fill_no("out0")):
                b, i = int(FILLS[n][0][2]), FILLS[n][1]
                dve.wait_ge(fill_ready, n + 1)
                if i == 0:
                    dve.wait_ge(sig_gates, b + 1)
                ps = proj[n % PBANKS][:, :].rearrange("p (a b) -> p a b", a=2)
                g = gates[:, b * KD + 2 * i:b * KD + 2 * i + 2, :]
                y = yT[:, 2 * i:2 * i + 2, :]
                if b == 0:
                    dve.tensor_tensor(y, ps, g, ALU.mult).then_inc(dve_out, 1)
                else:
                    link(dve.tensor_tensor(g, ps, g, ALU.mult))
                    dve.wait_ge(dve_out, 4 * (b - 1) + i + 1)
                    dve.tensor_tensor(y, y, g, ALU.add).then_inc(dve_out, 1)

            dve.wait_ge(xnat_in, 16)
            for n in range(fill_no("out0"), len(FILLS)):
                i, t = int(FILLS[n][0][3]), FILLS[n][1]
                cols = slice(512 * i, 512 * i + 512)
                dve.wait_ge(fill_ready, n + 1)
                dve.tensor_tensor(xn[:, t, cols], proj[n % PBANKS][:, :], row2[:, cols], ALU.mult).then_inc(dve_out, 1)
                dve.wait_ge(dve_out, emptied(n)[1])
                dve.tensor_tensor(x_nat[:, t, cols], x_nat[:, t, cols], xn[:, t, cols], ALU.add).then_inc(x1_ready, 1)
            dve.wait_ge(x1_root, 1)
            link(dve.reciprocal(stat[:, 0:NT], stat[:, 0:NT]))
            for t in range(NT):
                dve.tensor_scalar(xn[:, t, :], x_nat[:, t, :], stat[:, t:t + 1], None, ALU.mult).then_inc(xn_ready, 1)
            for q in range(4):
                n = shared_no("fT", q)
                ps = shared_wait(n)
                for c in range(2):
                    k = 2 * q + c
                    ins = dve.tensor_scalar(fT[:, k, :], ps[:, c * L:(c + 1) * L], A_ffn[:, k:k + 1],
                                            mod[:, 3 * KD + k, 0:1], ALU.mult, ALU.add)
                ins.then_inc(shared_out, 1)

            def wide(v, n):
                return v.unsqueeze(2).broadcast_to([P, NT, n])

            def first_best(dst, x, best, weight, tmp, tmp_max, n):
                link(dve.tensor_tensor(tmp, x, wide(best, n), ALU.is_equal))
                link(dve.tensor_tensor(tmp, tmp, weight.unsqueeze(1).broadcast_to([P, NT, n]), ALU.mult))
                link(dve.tensor_reduce(tmp_max, tmp, AX.X, ALU.max))
                link(dve.tensor_tensor(dst, tmp, wide(tmp_max, n), ALU.is_equal))

            ps = shared_wait(shared_no("rT"))
            parts = ps[:, 0:L].rearrange("p (t q n) -> p t n q", t=NT, q=4)[:, :, 0:ROUTES, :]
            dve.tensor_reduce(r_all, parts, AX.X, ALU.add).then_inc(shared_out, 1)
            dve.wait_ge(shared_out, shared_no("rT") + 1)
            link(dve.tensor_tensor(r_all, r_all, sm("router_b").unsqueeze(1).broadcast_to([P, NT, ROUTES]), ALU.add))
            dve.tensor_copy(r_g, r_all[:, :, 0:NG])
            link(dve.tensor_copy(r_e, r_all[:, :, NG:ROUTES]))
            link(dve.tensor_reduce(r_gm, r_g, AX.X, ALU.max))
            dve.tensor_tensor(r_eg, r_g, wide(r_gm, NG), ALU.subtract).then_inc(gexp_in, 1)
            first_best(r_sel, r_g, r_gm, sm("rank")[:, NE - NG:NE], r_t, r_sm, NG)
            sel = r_sel.rearrange("p t g -> p (t g)").unsqueeze(2).broadcast_to([P, NT * NG, EPG])
            em = r_em.rearrange("p t (g e) -> p (t g) e", g=NG)
            link(dve.tensor_tensor(em, r_e.rearrange("p t (g e) -> p (t g) e", g=NG), sel, ALU.mult))
            link(dve.tensor_scalar(r_t, r_sel, -1.0, -NEG, ALU.add, ALU.mult))
            outside = r_t.rearrange("p t g -> p (t g)").unsqueeze(2).broadcast_to([P, NT * NG, EPG])
            link(dve.tensor_tensor(em, em, outside, ALU.add))
            link(dve.tensor_reduce(r_m1, r_em, AX.X, ALU.max))
            first_best(oh1, r_em, r_m1, sm("rank"), r_et, r_sm, NE)
            link(dve.scalar_tensor_tensor(out=r_em, in0=oh1, scalar=3 * NEG, in1=r_em, op0=ALU.mult, op1=ALU.add))
            link(dve.tensor_reduce(r_m2, r_em, AX.X, ALU.max))
            dve.tensor_tensor(r_d, r_m2, r_m1, ALU.subtract).then_inc(gexp_in, 1)
            first_best(oh2, r_em, r_m2, sm("rank"), r_et, r_sm, NE)
            dve.tensor_tensor(member, oh1, oh2, ALU.add).then_inc(member_ready, 1)
            dve.wait_ge(gexp_out, 2)
            link(dve.tensor_reduce(r_gs, r_eg, AX.X, ALU.add))
            link(dve.tensor_scalar(r_w1, r_d, 1.0, None, ALU.add))
            link(dve.tensor_tensor(r_w1, r_w1, r_gs, ALU.mult))
            link(dve.reciprocal(r_w1, r_w1))
            link(dve.tensor_tensor(r_w2, r_w1, r_d, ALU.mult))
            dve.tensor_tensor(oh1, oh1, wide(r_w1, NE), ALU.mult)
            link(dve.tensor_tensor(oh2, oh2, wide(r_w2, NE), ALU.mult))
            link(dve.tensor_tensor(comb, oh1, oh2, ALU.add))
            dve.wait_ge(pos_ready, 1)
            link(dve.tensor_copy(posm, pv_bank[:, 0:32].rearrange("p (t n) -> p t n", t=NT)))
            link(dve.tensor_copy(first_sum, pv_bank[:, 32:48]))
            link(dve.tensor_tensor(posm[:, 1, :], posm[:, 1, :], first_sum, ALU.add))
            dve.wait_ge(member_ready, 1)
            link(dve.scalar_tensor_tensor(out=posm, in0=posm, scalar=1.0, in1=member, op0=ALU.add, op1=ALU.mult))
            link(dve.tensor_scalar(posm, posm, -1.0, None, ALU.add))
            def build_slots(p):
                for t in range(NT):
                    s = S_all[:, t, :].rearrange("p (e c) -> p e c", c=CAP)
                    ins = dve.tensor_tensor(s, slots_iota.unsqueeze(1).broadcast_to([P, NE, CAP]),
                                            posm[:, t, :].unsqueeze(2).broadcast_to([P, NE, CAP]), ALU.is_equal)
                ins.then_inc(slots_ready, 1)
                dve.wait_ge(slots_ready, p + 1)
                for t in range(NT):
                    s = S_all[:, t, :].rearrange("p (e c) -> p e c", c=CAP)
                    w = SW[:, t, :].rearrange("p (e c) -> p e c", c=CAP)
                    ins = dve.tensor_tensor(w, s, comb[:, t, :].unsqueeze(2).broadcast_to([P, NE, CAP]), ALU.mult)
                ins.then_inc(weighted, 1)

            build_slots(0)
            link(dve.tensor_tensor(first_sum, first_sum, pv_bank[:, 48:64], ALU.add))
            link(dve.tensor_reduce(count, first_sum, AX.X, ALU.max))
            link(dve.tensor_scalar(over, sm("limits"), count, None, ALU.is_lt))
            link(dve.tensor_reduce(passes_f, over, AX.X, ALU.add))
            dve.tensor_scalar(passes[0:1, 0:1], passes_f[0:1, :], 1.0, None, ALU.add).then_inc(passes_ready, 2)
            dve.memset(yacc, 0.0)

            def spread(v):
                return v.unsqueeze(2).broadcast_to([P, 4, P])

            def modulate(n):
                dve.wait_ge(gather_ready, n + 1)
                if not isinstance(n, int) or n:
                    dve.wait_ge(up_ready, n)
                for i in range(2):
                    ps = banks[i][:, :].rearrange("p (a b) -> p a b", b=P)
                    dve.tensor_tensor(h_sb[:, 4 * i:4 * i + 4, :], ps, spread(A_ffn[:, 4 * i:4 * i + 4]), ALU.mult)
                dve.drain()
                for i in range(2):
                    hh = h_sb[:, 4 * i:4 * i + 4, :]
                    dve.tensor_tensor(hh, hh, spread(mod[:, 3 * KD + 4 * i:3 * KD + 4 * i + 4, 0]), ALU.add)\
                       .then_inc(h_out, 1)

            def gated(before, first=False):
                n = before + 1
                dve.wait_ge(silu_ready, n + 1)
                dve.wait_ge(up_ready, n + 1)
                if not first:
                    dve.wait_ge(turned, before + 1)
                dve.tensor_tensor(he, sl, banks[3][:, :], ALU.mult).then_inc(he_ready, 1)

            def scattered(n):
                for q in range(4):
                    t, i = q // 2, q % 2
                    dve.wait_ge(scat_ready, 4 * n + q + 1)
                    y = yacc[:, t, 512 * i:512 * i + 512]
                    dve.tensor_tensor(y, y, banks[6 + i][:, :], ALU.add).then_inc(scat_out, 1)

            def slots_out(p):
                for q in range(4):
                    dve.wait_ge(shared_ready, shared_no("sT") + p * 4 + q + 1)
                    dve.tensor_copy(ST_all[:, 2 * q:2 * q + 2, :].rearrange("p a b -> p (a b)"),
                                    shared[(shared_no("sT") + q) % 2][:, :]).then_inc(shared_out, 1)
                dve.wait_ge(shared_out, shared_no("sT") + p * 4 + 4)
                dve.sem_inc(turned_slots, 1)

            def one_pass(p):
                first = isinstance(p, int)
                n0 = p * PAIRS
                modulate(n0)
                slots_out(p)
                gated(n0 - 1, first)
                modulate(n0 + 1)
                with dve.Fori(0, PAIRS - 2) as j:
                    before = n0 + j
                    gated(before)
                    modulate(before + 2)
                    scattered(before)
                before = n0 + PAIRS - 2
                gated(before)
                scattered(before)
                scattered(before + 1)

            one_pass(0)
            n_pass = dve.value_load(passes[0:1, 0:1], min_val=1, max_val=MAXPASS)
            with dve.If(n_pass > 1):
                with dve.Fori(1, n_pass) as p:
                    dve.tensor_scalar(posm, posm, -float(CAP), None, ALU.add)
                    dve.drain()
                    build_slots(p)
                    one_pass(p)
            dve.drain()

            dve.wait_ge(glast_in, 16)
            for t in range(NT):
                link(dve.tensor_tensor(yacc[:, t, :], yacc[:, t, :], row5, ALU.mult))
                dve.tensor_tensor(x_nat[:, t, :], x_nat[:, t, :], yacc[:, t, :], ALU.add).then_inc(fin_sum, 1)
            dve.wait_ge(fin_root, 1)
            link(dve.reciprocal(stat[:, 2:4], stat[:, 2:4]))
            for t in range(NT):
                dve.scalar_tensor_tensor(out=yacc[:, t, :], in0=x_nat[:, t, :], scalar=stat[:, 2 + t:3 + t],
                                         in1=g_last, op0=ALU.mult, op1=ALU.mult).then_inc(fin_ready, 1)


SM = {}
SMALL = 0
for _name, *_dims in (("ident", P), ("ones", P), ("below", P), ("stream0", P), ("iota", CAP), ("eps", 1), ("limits", MAXPASS - 1),
                      ("rank", NE), ("b_ada", 48), ("g_mix", KD), ("g_ffn", KD), ("lb", 8), ("hg_g", 1),
                      ("gqn", HD), ("gqn_swapped", HD), ("gkn", HD), ("gkn_swapped", HD),
                      ("router_b", ROUTES), ("router", KD, 32), ("cos", NT, HD), ("sin", NT, HD)):
    SM[_name] = (SMALL, _dims)
    SMALL += int(np.prod(_dims))


def columns(v):
    return v.reshape(-1, P).T


def shape_constants():
    f = np.float32
    i = np.arange(P)
    rank = np.arange(NE, 0, -1, dtype=f)
    t = np.arange(L)
    pos = np.stack([t // GRID, t % GRID], axis=-1).astype(f)
    n_freq = HD // 4
    inv = np.power(f(10000.0), -np.arange(n_freq, dtype=f) / f(n_freq)).astype(f)
    ang = (pos[:, :, None] * inv).astype(f)
    cos = np.concatenate([np.cos(ang)] * 2, axis=-1).reshape(NT, P, HD).transpose(1, 0, 2)
    sin = np.concatenate([-np.sin(ang), np.sin(ang)], axis=-1).reshape(NT, P, HD).transpose(1, 0, 2)
    return {
        "ident": np.eye(P, dtype=f), "ones": np.ones((P, P), f),
        "below": (i[:, None] < i[None, :]).astype(f),
        "stream0": np.tile((i[:, None] % 32 == 0).astype(f), (1, P)),
        "iota": np.tile(np.arange(CAP, dtype=f), (P, 1)),
        "eps": np.full((P, 1), EPS, f),
        "limits": np.tile(np.arange(1, MAXPASS, dtype=f) * CAP, (P, 1)),
        "rank": np.tile(rank, (P, 1)), "cos": cos.astype(f), "sin": sin.astype(f),
    }


def level_masks():
    i = np.arange(P)
    out = np.zeros((P, 2 * (LEVELS - 1), P), np.float32)
    for v in range(LEVELS - 1):
        m = 1 << v
        same = (i[:, None] // (2 * m)) == (i[None, :] // (2 * m))
        right = (i // m) % 2 == 1
        out[:, v, :] = same & ~right[:, None] & right[None, :]
        out[:, LEVELS - 1 + v, :] = same & right[:, None] & ~right[None, :]
    return out


def bias_layout(rpb):
    col = np.arange(GRID)
    c0 = np.clip(col - WC // 2, 0, GRID - WC)
    inside = (col[None, :] >= c0[:, None]) & (col[None, :] < c0[:, None] + WC)
    dc = np.where(inside, col[None, :] - col[:, None] + WC - 1, 0)
    out = np.full((P, NH, RB, GRID), NEG, np.float32)
    for half in range(2):
        for i in range(RB):
            dr = i - 2 - half + WR - 1
            rows = rpb[:, dr][:, dc]
            out[half * GRID:(half + 1) * GRID, :, i, :] = np.where(inside[:, None, :], rows.transpose(1, 0, 2), np.float32(NEG))
    return out.reshape(P, NH, RB * GRID)


def weight_slots(w, width=512):
    k, n = w.shape
    s = w.reshape(k // P, P, n // width, width).transpose(2, 1, 0, 3)
    return s.reshape(n // width, P, -1)


def kernel(**inputs):
    import concourse.bacc as bacc
    from concourse.bass_utils import run_bass_kernel_spmd

    a = {k: np.asarray(v) for k, v in inputs.items()}
    x, ctx_ = a["x"][0], a["ctx"][0]
    xc = np.concatenate([x, ctx_], axis=0)
    w_in = a["w_in"][0]
    part = {}
    at_ = 0
    for name, n in (("nq", 512), ("nk", 512), ("nv", 512), ("hq", 512), ("ff", 512), ("fb", 512), ("hi", 512),
                    ("hg", 512), ("gq", 512), ("gkv", 256), ("gate", 3 * D)):
        part[name] = w_in[:, at_:at_ + n]
        at_ += n
    part["gq"] = part["gq"].reshape(D, 2, NH // 2, HD).transpose(0, 2, 1, 3).reshape(D, NH * HD)
    ada = weight_slots(a["w_ada"][0])
    gate = weight_slots(part["gate"])
    front = []
    for name in FRONT:
        if name[:3] == "ada":
            s = ada[int(name[3:])]
        elif name[:4] == "gate":
            s = gate[int(name[4:])]
        elif name == "gkv":
            s = np.zeros((P, SLOT), np.float32)
            s[:, 0:SLOT // 2] = weight_slots(part["gkv"], 256)[0]
        elif name[:2] == "br":
            wb = a["w_branch"][0, int(name[2])]
            if name == "br2":
                wb = wb.reshape(2, NH // 2, HD, D).transpose(1, 0, 2, 3).reshape(BW, D)
            s = weight_slots(wb, D)[0]
        elif name[:3] == "out":
            s = weight_slots(a["w_out"][0])[int(name[3])]
        else:
            s = weight_slots(part[name])[0]
        front.append(s)
    experts = []
    for e in range(NE):
        experts += [weight_slots(a["w_exp_gate"][0, e])[0], weight_slots(a["w_exp_up"][0, e])[0],
                    weight_slots(a["w_exp_down"][0, e], D)[0]]
    small = dict(shape_constants())

    def swapped(g):
        return g.reshape(2, 2, HD // 4)[:, ::-1].reshape(HD)

    small.update({
        "b_ada": columns(a["b_ada"][0]), "g_mix": columns(a["g_mix"][0]), "g_ffn": columns(a["g_ffn"][0]),
        "lb": columns(a["hg_lb_logits"][0].reshape(-1)), "hg_g": columns(a["hg_norm_g"][0]),
        "gqn": np.tile(a["gqa_qnorm_g"][0], (P, 1)), "gqn_swapped": np.tile(swapped(a["gqa_qnorm_g"][0]), (P, 1)),
        "gkn": np.tile(a["gqa_knorm_g"][0], (P, 1)), "gkn_swapped": np.tile(swapped(a["gqa_knorm_g"][0]), (P, 1)),
        "router_b": np.tile(np.concatenate([a["b_group_router"][0], a["b_expert_router"][0]]), (P, 1)),
        "router": np.pad(np.concatenate([a["w_group_router"][0], a["w_expert_router"][0]], axis=1)
                         .reshape(KD, P, ROUTES).transpose(1, 0, 2), ((0, 0), (0, 0), (0, 32 - ROUTES))),
    })
    arrays = {
        "xcT": xc.T.reshape(KD, P, 2 * L).transpose(1, 0, 2),
        "x_nat": x.reshape(NT, P, D).transpose(1, 0, 2),
        "cvec": np.pad(np.stack([a["c"][0], a["c_ctx"]], axis=-1).reshape(KD, P, 2).transpose(1, 0, 2),
                       ((0, 0), (0, 0), (0, 30))),
        "b_rows": np.tile(a["b_ada"][0].reshape(12, 512)[list(ROW_GROUPS)], (P, 1, 1)),
        "front_w": np.stack(front), "expert_w": np.stack(experts),
        "na_bias": bias_layout(a["na_rpb"][0]),
        "small_w": np.concatenate([small[n].reshape(P, -1) for n in SM], axis=1),
        "level_masks": level_masks(),
        "g_last": np.tile(a["g_final"], (P, 1)),
    }
    arrays = {k: np.ascontiguousarray(v) for k, v in arrays.items()}
    nc = bacc.Bacc("TRN2", target_bir_lowering=False, num_devices=1)
    d = {n: nc.dram_tensor(n, v.shape, mybir.dt.from_np(v.dtype), kind="ExternalInput").ap() for n, v in arrays.items()}
    d["out"] = nc.dram_tensor("out", (L, D), F32, kind="ExternalOutput").ap()
    build(nc, d)
    r = run_bass_kernel_spmd(nc, [arrays], core_ids=[0])
    return r.results[0]["out"].reshape(1, L, D)
```

```python
import numpy as np
import concourse.bass as bass
from concourse import mybir
from concourse.alu_op_type import AluOpType as ALU
from contextlib import ExitStack

F32 = mybir.dt.float32
I32 = mybir.dt.int32
I8 = mybir.dt.int8
ACT = mybir.ActivationFunctionType
AX = mybir.AxisListType

P = 128
D = 1024
KD = D // P
L = 256
NT = L // P
GRID = 64
ROWS = L // GRID
WR, WC = 8, 16
HD = 64
NH = 8
HGH = 4
NE = 16
NG = 4
EPG = NE // NG
EH = 512
KH = EH // P
BW = NH * HD
CAP = 64
PAIRS = NE // 2
MAXPASS = L // CAP
EPS = 1e-6
QSCALE = HD ** -0.5
NEG = -1e30
RB = ROWS + 2
ROUTES = NG + NE

FRONT = ["ada0", "ada2", "ff", "ada1", "ada3", "fb", "hq", "hg", "hi", "nk", "nq", "nv", "gq", "gkv"]
FRONT += ["gate0", "ada4", "gate1", "ada5", "gate2", "ada6", "gate3", "ada7", "gate4", "ada8", "ada9", "gate5",
          "ada10", "ada11"]
FRONT += ["br0", "br1", "br2", "out0", "out1"]
FSLOTS = 3
SLOTS = 8
LOWER = 6
SLOT = 4096
SLOT_OF = [0, 1, 2, 0, 1] + [n % FSLOTS for n in range(len(FRONT) - 5)]
USES = [SLOT_OF.count(s) for s in range(FSLOTS)]
GROUPS = ["ada0", "ada2", "ada1", "ada3", "ff"] + FRONT[5:]


def taken(n):
    return GROUPS.index(FRONT[n]) + 1


def earlier(n):
    return [m for m in range(n) if SLOT_OF[m] == SLOT_OF[n]]




def group_fills(name):
    if name[:3] == "ada":
        n = 1
    elif name in ("ff", "fb", "hi", "nk", "nv"):
        n = 4
    elif name[:2] in ("br",):
        n = 4
    else:
        n = 2
    return [(name, i, "dve" if name[:2] in ("br", "ou") else "act") for i in range(n)]


FILLS = [f for g in GROUPS for f in group_fills(g)]
PBANKS = 3
BANK_OF = [5 if f[0] == "ada1" else 6 if f[0] == "ada3" else n % PBANKS for n, f in enumerate(FILLS)]
ROW_GROUPS = (4, 5, 10, 11)


def fill_no(name, i=0):
    return [f[:2] for f in FILLS].index((name, i))


def emptied(n):
    who = FILLS[n][2]
    return who, sum(f[2] == who for f in FILLS[:n + 1])


UNITS = [(k, t, c) for k in ("na", "gq") for t in range(NT) for c in range(4)]
STEPS = len(UNITS)
FILLER = [n for n in range(fill_no("gq"), fill_no("br0"))]


def cost(n):
    return 1 if FILLS[n][0][:3] == "ada" else 4


FILLER_AT = {i: [] for i in range(STEPS)}
_spent = 0
for _n in FILLER:
    FILLER_AT[_spent * STEPS // sum(cost(n) for n in FILLER)].append(_n)
    _spent += cost(_n)
G_STEP = [i for i in range(STEPS) if fill_no("gkv", 1) in FILLER_AT[i]][0]
GATE_FILLS = fill_no("gate5", 1)

LEVELS = 8
SHARED = [("ada", g) for g in (0, 2, 1, 3)] + [("kc", i) for i in range(4)]
SHARED += [(f"lev{v}", i) for v in range(LEVELS) for i in range(4)] + [("s0", i) for i in range(2)]
SHARED += [("lev8", i) for i in range(2)] + [("o", i) for i in range(2)] + [("osq", i) for i in range(2)]


def ada_in_step(i):
    return [int(FILLS[n][0][3:]) for n in FILLER_AT.get(i, []) if FILLS[n][0][:3] == "ada"]


for _i in range(STEPS + 1):
    SHARED += [("ada", g) for g in ada_in_step(_i - 1)]
    if _i == 2 * 4:
        SHARED += [("gqT", 0), ("gqT", 1), ("gkT", 0)]
    if _i < STEPS:
        SHARED += [("pT", 2 * _i), ("pT", 2 * _i + 1)]
SHARED += [("fT", i) for i in range(4)] + [("rT", 0)]


def shared_no(name, i=0):
    return SHARED.index((name, i))


def build(nc, d):
    ctx = ExitStack()
    with ctx:
        TOTAL = 52740
        sb = ctx.enter_context(nc.sbuf_tensor("sb", [P, TOTAL], F32))
        banks = [ctx.enter_context(nc.psum_tensor(f"bank{i}", [P, 512], F32)) for i in range(8)]
        proj = banks[0:3]
        shared = banks[3:5]
        score = banks[5:7]
        pv_bank = banks[7]

        def at(start, *dims):
            n = int(np.prod(dims))
            v = sb[:, start:start + n]
            if len(dims) == 2:
                v = v.rearrange("p (a b) -> p a b", b=dims[1])
            if len(dims) == 3:
                v = v.rearrange("p (a b c) -> p a b c", b=dims[1], c=dims[2])
            return v

        slot = [at(i * SLOT, SLOT) for i in range(LOWER)]
        A0 = FSLOTS * SLOT
        na_k = at(A0, 4, 2 * L)
        na_v = at(A0 + 2048, 4, 512)
        sig_q, sig_g = at(A0 + 2048, 4, L), at(A0 + 3072, 4, L)
        na_bias = at(A0 + 4096, NH, RB * GRID)
        X = at(A0 + 7168, 8, L)
        Y = at(A0 + 9216, 8, L)
        sq = at(A0 + 7168, KD, 512)
        probs = at(A0 + 7168, 2, 512)
        probsT = at(A0 + 8192, 2, 512)
        ada_late = at(A0 + 9216, 2, 512)
        ada_early = at(A0, 2, 512)
        gkv = at(A0 + 11264, 4, 256)
        B0 = A0 + (LOWER - FSLOTS) * SLOT
        hT = at(B0, KD, 2 * L)
        xn, fT = at(B0, NT, D), at(B0 + 2048, KD, L)
        F0 = B0 + 4096
        T_lat = at(F0, 8, L)
        masks_wide = at(F0, 2 * (LEVELS - 1), P)
        forget = at(F0, 2, 8, L)
        F_ctx = at(F0 + 2048, 8, L)
        Kc = at(F0 + 4096, 8, L)
        kcn = at(F0 + 6144, 8, L)
        gates = at(F0 + 2048, 3 * KD, L)
        o_sb, o_tmp = at(F0, 4, L), at(F0 + 1024, 4, L)
        b_rows = at(F0, 4, 512)
        slot.append(at(B0 + 2048, SLOT))
        SW = at(F0 + 2048, NT, NE * CAP)
        S_all = at(F0 + 4096, NT, NE * CAP)
        ST_all = at(F0 + 6144, PAIRS, NT * P)
        C0 = F0 + 8192
        rstd_row = at(C0, 512)
        QR = at(C0 + 1024, 4, L)
        row5 = at(C0 + 1024, D)
        v_hg = at(C0 + 2048, 4, 512)
        x_nat = at(C0 + 2048, NT, D)
        AT = at(C0 + 4096, 6, 512)
        yT = at(C0 + 4096, KD, L)
        g_sq = at(C0 + 4096, 1536)
        g_rot = at(C0 + 5632, NT, 512)
        k_rot = at(C0 + 6656, NT, 128)
        h_sb = at(C0, KD, P)
        g_last = at(C0 + 4096, D)
        he = at(C0 + 5120, EH)
        sl = at(C0 + 5632, EH)
        logits_sb = at(C0 + 6144, L)
        heT = at(C0 + 6656, KH, P)
        y_sb = at(C0 + 7168, D)
        S0 = at(C0 + 7168, 8, P)
        row2 = at(C0 + 7168, D)
        bT = at(C0 + 8192, 4, L)
        na_q = at(C0 + 9216, 4, L)
        aT = na_q
        slot.append(at(C0 + 8192, SLOT))
        gq = at(C0 + 10240, NT, 512)
        gqT = at(C0 + 11264, 4, L)
        cT = gqT
        gkT = at(C0 + 12288, 512)
        S_now, ST_now = at(C0 + 12288, NT, P), at(C0 + 12544, NT, P)
        normed = at(0, NT, D)
        E0 = C0 + 12800
        consts = {}
        pos = [E0]

        def keep(n, *dims):
            v = at(pos[0], *dims) if dims else at(pos[0], n)
            pos[0] += n
            assert pos[0] <= TOTAL, pos[0]
            return v

        small = keep(SMALL)
        def sm(name):
            o, dims = SM[name]
            return small[:, o:o + int(np.prod(dims))] if len(dims) == 1 else at(E0 + o, *dims)
        ident, ones, below, slots_iota = sm("ident"), sm("ones"), sm("below"), sm("iota")
        cvec = keep(KD * 32, KD, 32)
        mod = keep(96, 48, 2)
        A_mix, A_ffn = keep(16, KD, 2), keep(8)
        lower, span = keep(8), keep(8)
        lb_e, lb_p = keep(8), keep(8)
        g_ms = keep(24)
        qcos, qsin = keep(128, NT, HD), keep(128, NT, HD)
        kcos, ksin = keep(128, NT, HD), keep(128, NT, HD)
        nmax = keep(32)
        sums = keep(32)
        stat = keep(8)
        zeros = at(C0 + 512, 256)
        ones_now = at(C0 + 768, P)
        r_g, r_e = keep(8, NT, NG), keep(32, NT, NE)
        r_all = keep(2 * ROUTES, NT, ROUTES)
        first_sum = keep(16)
        r_gm, r_gs, r_sm = keep(2), keep(2), keep(2)
        r_m1, r_m2, r_w1, r_w2, r_d = keep(2), keep(2), keep(2), keep(2), keep(2)
        r_t, r_sel, r_eg = keep(8, NT, NG), keep(8, NT, NG), keep(8, NT, NG)
        r_em, r_et = keep(32, NT, NE), keep(32, NT, NE)
        oh1, oh2 = keep(32, NT, NE), keep(32, NT, NE)
        member, comb, posm = keep(32, NT, NE), keep(32, NT, NE), keep(32, NT, NE)
        count, over = keep(1), keep(3)
        passes_f = keep(1)
        masks = ctx.enter_context(nc.sbuf_tensor("masks", [P, 2 * (LEVELS - 1), P], I8))
        passes = ctx.enter_context(nc.sbuf_tensor("passes", [1, 1], I32))

        def sem(name):
            return ctx.enter_context(nc.semaphore(name))

        x_in = [sem("x_in0"), sem("x_in1")]
        c_in, small_in, bias_in, masks_in, xnat_in, glast_in = [sem(n) for n in (
            "c_in", "small_in", "bias_in", "masks_in", "xnat_in", "glast_in")]
        w_in_ = [sem(f"weights_in{i}") for i in range(SLOTS)]
        w_used = sem("weights_used")
        fill_ready = sem("fill_ready")
        out_by = {"act": sem("fill_out_act"), "dve": sem("fill_out_dve")}
        shared_ready, shared_out = sem("shared_ready"), sem("shared_out")
        masks_ready = sem("masks_ready")
        sq_ready, rms_ready, rms_root, c_ready = sem("sq_ready"), sem("rms_ready"), sem("rms_root"), sem("c_ready")
        h_ready = sem("h_ready")
        ones_set = sem("ones_set")
        lb_in, lb_ready = sem("lb_in"), sem("lb_ready")
        silu_hg = sem("silu_hg")
        kc_ready = sem("kc_ready")
        xy_ready = sem("xy_ready")
        o_sq, o_root, b_ready = sem("o_sq"), sem("o_root"), sem("b_ready")
        g_sum, g_root, g_rec, gqa_ready = sem("g_sum"), sem("g_root"), sem("g_rec"), sem("gqa_ready")
        g_tab = sem("g_tab")
        scores_ready, max_ready, exp_ready = sem("scores_ready"), sem("max_ready"), sem("exp_ready")
        norm_ready, pv_ready, pv_out = sem("norm_ready"), sem("pv_ready"), sem("pv_out")
        sig_gates = sem("sig_gates")
        brow_in = sem("brow_in")
        x1_ready, x1_sum, x1_root, xn_ready = sem("x1_ready"), sem("x1_sum"), sem("x1_root"), sem("xn_ready")
        router_ready, gexp_in, gexp_out = sem("router_ready"), sem("gexp_in"), sem("gexp_out")
        member_ready, pos_ready, passes_ready = sem("member_ready"), sem("pos_ready"), sem("passes_ready")
        slots_ready, weighted, turned_slots = sem("slots_ready"), sem("weighted_slots"), sem("turned_slots")
        turn_ready, turn_out = sem("slots_turned"), sem("slots_turned_out")
        cut_ready, cutT_ready = sem("cut_for_gather"), sem("cut_for_scatter")
        gather_ready, h_out = sem("gather_ready"), sem("h_out")
        gate_ready, up_ready, silu_ready = sem("gate_ready"), sem("up_ready"), sem("silu_ready")
        he_ready, turned, heT_ready = sem("he_ready"), sem("hidden_turned"), sem("heT_ready")
        down_ready, y_out = sem("down_ready"), sem("y_out")
        scat_ready, scat_out = sem("scat_ready"), sem("scat_out")
        fin_sum, fin_root, fin_ready, stored = sem("fin_sum"), sem("fin_root"), sem("fin_ready"), sem("stored")
        v_step, p_step, a_step = sem("vector_step"), sem("pool_step"), sem("scalar_step")

        block = ctx.enter_context(nc.Block())

        def wait_emptied(eng, n):
            who, count_ = emptied(n)
            eng.wait_ge(out_by[who], count_)

        def ada_place(g):
            return ada_early[:, g // 2, :] if g < 4 else ada_late[:, g % 2, :]

        def slot_value(s):
            return 16 * USES[s] if s < FSLOTS else 0

        @block.sync
        def _(sp):
            for i in range(2):
                sp.dma_start(hT[:, 4 * i:4 * i + 4, :], d["xcT"][:, 4 * i:4 * i + 4, :]).then_inc(x_in[i], 16)
            for n, name in enumerate(FRONT):
                if earlier(n):
                    sp.wait_ge(w_used, taken(earlier(n)[-1]))
                cols = SLOT // 2 if name == "gkv" else SLOT
                s = SLOT_OF[n]
                sp.dma_start(slot[s][:, 0:cols], d["front_w"][n, :, 0:cols]).then_inc(w_in_[s], 16)
                if name == "nq":
                    sp.dma_start(na_bias, d["na_bias"]).then_inc(bias_in, 16)
                if name == "ada3":
                    sp.dma_start(masks_wide, d["level_masks"]).then_inc(masks_in, 16)
                if name == "gate2":
                    sp.wait_ge(b_ready, 1)
                    sp.dma_start(b_rows, d["b_rows"]).then_inc(brow_in, 16)
                    sp.dma_start(x_nat, d["x_nat"]).then_inc(xnat_in, 16)

            def load(s, row):
                sp.dma_start(slot[s], d["expert_w"][bass.ds(row, 1), :, :].rearrange("a p n -> p (a n)")
                             if not isinstance(row, int) else d["expert_w"][row, :, :]).then_inc(w_in_[s], 16)

            def load_gates(j, odd):
                for e in range(2):
                    load((6 if odd else 0) + e, j * 6 + 3 * e)

            def load_rest(n, j):
                for s in range(2, 6):
                    sp.wait_ge(up_ready if s < 4 else down_ready, n)
                    load(s, j * 6 + (s % 2) * 3 + s // 2)

            def load_pairs(n0):
                def step(n, j, odd, late=False):
                    if late:
                        load_rest(n, j)
                    sp.wait_ge(gate_ready, n)
                    load_gates(j + 1, odd)
                    if not late:
                        load_rest(n, j)

                with sp.Fori(0, (PAIRS - 4) // 2) as i:
                    for u in range(2):
                        step(n0 + i * 2 + (1 + u), i * 2 + (1 + u), u)
                step(n0 + PAIRS - 3, PAIRS - 3, 0)
                step(n0 + PAIRS - 2, PAIRS - 2, 1, late=True)
                load_rest(n0 + PAIRS - 1, PAIRS - 1)

            sp.wait_ge(shared_out, shared_no("pT", 2 * STEPS - 1) + 1)
            sp.wait_ge(pv_out, 4)
            for s in (3, 4, 5, 1, 7, 2, 0, 6):
                if s == 7:
                    load(7, 6 + 3)
                    continue
                if s == 6:
                    sp.wait_ge(router_ready, 1)
                    load(6, 6)
                    continue
                if s < FSLOTS:
                    sp.wait_ge(w_used, taken([n for n in range(len(FRONT)) if SLOT_OF[n] == s][-1]))
                load(s, (s % 2) * 3 + s // 2)
            load_pairs(0)
            sp.wait_ge(passes_ready, 2)
            n_pass = sp.value_load(passes[0:1, 0:1], min_val=1, max_val=MAXPASS)
            with sp.If(n_pass > 1):
                with sp.Fori(0, n_pass - 1) as p:
                    for u in range(2):
                        sp.wait_ge(gate_ready, p * PAIRS + (PAIRS - 1 + u))
                        load_gates(u, u)
                    load_rest(p * PAIRS + PAIRS, 0)
                    load_pairs(p * PAIRS + PAIRS)
            for q in range(2 * NT):
                sp.wait_ge(fin_ready, q + 1)
                rows, cols = slice(q // 2 * P, q // 2 * P + P), slice(q % 2 * 512, q % 2 * 512 + 512)
                sp.dma_start(d["out"][rows, cols], normed[:, q // 2, cols]).then_inc(stored, 16)
            sp.wait_ge(stored, 16 * 2 * NT)

        @block.gpsimd
        def _(pool):
            steps = [0]

            def link(ins):
                steps[0] += 1
                ins.then_inc(p_step, 1)
                pool.wait_ge(p_step, steps[0])

            pool.wait_ge(masks_in, 16)
            pool.tensor_copy(masks[:, :, :], masks_wide).then_inc(masks_ready, 1)
            pool.wait_ge(small_in, 16)
            for c_, s_, g in ((qcos, qsin, "gqn"), (kcos, ksin, "gkn")):
                gn = sm(g).unsqueeze(1).broadcast_to([P, NT, HD])
                gs = sm(g + "_swapped").unsqueeze(1).broadcast_to([P, NT, HD])
                pool.tensor_tensor(c_, sm("cos"), gn, ALU.mult)
                last = pool.tensor_tensor(s_, sm("sin"), gs, ALU.mult)
            last.then_inc(g_tab, 1)

            pool.wait_ge(g_tab, 1)
            pool.wait_ge(g_rec, 1)
            rq = g_ms[:, 0:16].unsqueeze(2).broadcast_to([P, 16, HD])
            rk = g_ms[:, 16:24].rearrange("p (a b) -> p a b", b=2).unsqueeze(3).broadcast_to([P, 4, 2, HD])
            q16 = gq.rearrange("p t (h c) -> p (t h) c", c=HD)
            k4 = gkv[:, :, 0:128].rearrange("p t (h c) -> p t h c", c=HD)
            link(pool.tensor_tensor(q16, q16, rq, ALU.mult))
            link(pool.tensor_tensor(k4, k4, rk, ALU.mult))
            for x, rot, c_, s_, nh in ((gq, g_rot, qcos, qsin, NH), (gkv, k_rot, kcos, ksin, 2)):
                for t in range(NT):
                    xv = x[:, t, 0:nh * HD].rearrange("p (h a f c) -> p h a f c", a=2, f=2, c=16)
                    rv = rot[:, t, :].rearrange("p (h a f c) -> p h a f c", a=2, f=2, c=16)
                    sv = s_[:, t, :].rearrange("p (a f c) -> p a f c", a=2, f=2)
                    for f in range(2):
                        ins = pool.tensor_tensor(rv[:, :, :, f, :], xv[:, :, :, 1 - f, :],
                                                 sv[:, :, f, :].unsqueeze(1).broadcast_to([P, nh, 2, 16]), ALU.mult)
                    link(ins)
                    xh = x[:, t, 0:nh * HD].rearrange("p (h c) -> p h c", c=HD)
                    link(pool.tensor_tensor(xh, xh, c_[:, t, :].unsqueeze(1).broadcast_to([P, nh, HD]), ALU.mult))
                    link(pool.tensor_tensor(x[:, t, 0:nh * HD], x[:, t, 0:nh * HD], rot[:, t, :], ALU.add))
            kx = gkv[:, NT:4, 0:128].rearrange("p t (h c) -> p t h c", c=HD)
            gk = sm("gkn").unsqueeze(1).unsqueeze(1).broadcast_to([P, 2, 2, HD])
            pool.tensor_tensor(kx, kx, gk, ALU.mult).then_inc(gqa_ready, 1)

            def times_one(dst, src):
                return pool.tensor_tensor(dst, src, ones.unsqueeze(1).broadcast_to([P, NT, P]), ALU.mult)

            def cut_gather(n, j, first=False, copy=pool.tensor_copy):
                if not first:
                    pool.wait_ge(gather_ready, n)
                copy(S_now, S_all[:, :, bass.ds(j * P, P)]).then_inc(cut_ready, 1)

            def cut_scatter(n, j, p, first=False, copy=pool.tensor_copy):
                pool.wait_ge(turned_slots, p + 1)
                if not first:
                    pool.wait_ge(scat_ready, 4 * n)
                srcT = ST_all[:, bass.ds(j, 1), :].rearrange("p a (t c) -> p (a t) c", t=NT)
                copy(ST_now, srcT).then_inc(cutT_ready, 1)

            pool.wait_ge(slots_ready, 1)
            cut_gather(0, 0, True)
            pool.wait_ge(slots_ready, 2)
            cut_gather(1, 1)
            cut_scatter(0, 0, 0, True)
            with pool.Fori(1, PAIRS - 1) as j:
                cut_gather(j + 1, j + 1)
                cut_scatter(j, j, 0)
            cut_scatter(PAIRS - 1, PAIRS - 1, 0)
            pool.wait_ge(passes_ready, 2)
            n_pass = pool.value_load(passes[0:1, 0:1], min_val=1, max_val=MAXPASS)
            with pool.If(n_pass > 1):
                with pool.Fori(1, n_pass) as p:
                    n0 = p * PAIRS
                    pool.wait_ge(slots_ready, 2 * p + 2)
                    cut_gather(n0, 0, copy=times_one)
                    with pool.Fori(0, PAIRS - 1) as j:
                        cut_gather(n0 + j + 1, j + 1)
                        cut_scatter(n0 + j, j, p)
                    cut_scatter(n0 + (PAIRS - 1), PAIRS - 1, p, copy=times_one)
            pool.nop()

        @block.scalar
        def _(act):
            act.dma_start(cvec, d["cvec"]).then_inc(c_in, 16)
            act.dma_start(small, d["small_w"]).then_inc(small_in, 16)
            act.wait_ge(c_in, 16)
            act.activation(cvec, cvec, ACT.Silu).then_inc(c_ready, 1)
            for k in range(KD):
                if k % 4 == 0:
                    act.wait_ge(x_in[k // 4], 16)
                act.activation(sq[:, k, :], hT[:, k, :], ACT.Square).then_inc(sq_ready, 1)
            act.wait_ge(rms_ready, 1)
            act.wait_ge(small_in, 16)
            act.activation(rstd_row, pv_bank[:, :], ACT.Sqrt, bias=sm("eps"), scale=1.0 / D).then_inc(rms_root, 1)

            act.wait_ge(lb_in, 1)
            act.activation(lb_e, lb_e, ACT.Exp).then_inc(lb_ready, 1)

            def fill(n):
                name, i, who = FILLS[n]
                assert who == "act"
                ps = banks[BANK_OF[n]]
                act.wait_ge(fill_ready, n + 1)
                two = ps[:, :].rearrange("p (a b) -> p a b", a=2)
                done = out_by["act"]
                if name[:3] == "ada":
                    g = int(name[3:])
                    if g in (1, 3):
                        act.wait_ge(shared_ready, shared_no("ada", g - 1) + 1)
                    elif g > 5:
                        act.wait_ge(shared_ready, shared_no("ada", g - 2) + 1)
                    act.activation(ada_place(g), ps[:, :], ACT.Copy).then_inc(done, 1)
                elif name in ("ff", "fb"):
                    if (name, i) == ("ff", 0):
                        act.wait_ge(masks_ready, 1)
                    act.activation(forget[:, :, 4 * (name == "fb") + i, :], two, ACT.Sigmoid).then_inc(done, 1)
                elif name in ("hq", "hg"):
                    raw, sig = (QR, sig_q) if name == "hq" else (bT, sig_g)
                    act.activation(raw[:, 2 * i:2 * i + 2, :], two, ACT.Copy)
                    act.activation(sig[:, 2 * i:2 * i + 2, :], two, ACT.Sigmoid).then_inc(done, 1)
                elif name == "hi":
                    act.activation(v_hg[:, i, :], ps[:, :], ACT.Copy).then_inc(done, 1)
                elif name == "nk":
                    act.activation(na_k[:, i, :], ps[:, :], ACT.Copy).then_inc(done, 1)
                elif name == "nq":
                    act.activation(na_q[:, 2 * i:2 * i + 2, :], two, ACT.Copy, scale=QSCALE).then_inc(done, 1)
                elif name == "nv":
                    if i == 0:
                        act.wait_ge(silu_hg, 2)
                    act.activation(na_v[:, i, :], ps[:, :], ACT.Copy).then_inc(done, 1)
                elif name == "gq":
                    act.activation(gq[:, i, :], ps[:, :], ACT.Copy).then_inc(done, 1)
                elif name == "gkv":
                    act.activation(gkv[:, 2 * i:2 * i + 2, :], two, ACT.Copy).then_inc(done, 1)
                elif name[:4] == "gate":
                    c = 4 * int(name[4:]) + 2 * i
                    if c == 0:
                        act.wait_ge(shared_out, shared_no("s0", 1) + 1)
                    act.activation(gates[:, c:c + 2, :], two, ACT.Copy).then_inc(done, 1)

            for n in range(fill_no("nv", 2) + 1):
                fill(n)
            act.wait_ge(shared_out, shared_no("o", 1) + 1)
            act.activation(o_tmp, o_sb, ACT.Square).then_inc(o_sq, 1)
            fill(fill_no("nv", 3))
            for i in range(2):
                act.wait_ge(shared_ready, shared_no("osq", i) + 1)
                act.activation(o_tmp[:, 2 * i:2 * i + 2, :],
                               shared[shared_no("osq", i) % 2][:, :].rearrange("p (a b) -> p a b", a=2),
                               ACT.Sqrt, bias=sm("eps"), scale=1.0 / P).then_inc(o_root, 1)
            for i in range(STEPS):
                for e in range(2):
                    act.wait_ge(max_ready, 2 * i + e + 1)
                    if i:
                        act.wait_ge(shared_ready, shared_no("pT", 2 * i - 2 + e) + 1)
                    act.activation(probs[:, e, :], score[e][:, :], ACT.Exp, bias=nmax[:, 2 * i + e:2 * i + e + 1],
                                   accum_out=sums[:, 2 * i + e:2 * i + e + 1]).then_inc(exp_ready, 1)
                for n in FILLER_AT[i]:
                    fill(n)
                if i == G_STEP:
                    act.wait_ge(g_sum, 1)
                    act.activation(g_ms, g_ms, ACT.Sqrt, bias=sm("eps"), scale=1.0 / HD).then_inc(g_root, 1)
            act.wait_ge(out_by["act"], emptied(GATE_FILLS)[1])
            for b in range(3):
                act.activation(gates[:, b * KD:(b + 1) * KD, :], gates[:, b * KD:(b + 1) * KD, :],
                               ACT.Sigmoid).then_inc(sig_gates, 1)
            act.activation(stat[:, 4:5], sm("eps"), ACT.Sqrt)
            for t in range(NT):
                act.wait_ge(x1_ready, NT + t + 1)
                act.activation(xn[:, t, :], x_nat[:, t, :], ACT.Square, accum_out=stat[:, t:t + 1]).then_inc(x1_sum, 1)
            act.wait_ge(x1_sum, NT)
            act.activation(stat[:, 0:NT], stat[:, 0:NT], ACT.Sqrt, bias=sm("eps"), scale=1.0 / D).then_inc(x1_root, 1)
            act.dma_start(g_last, d["g_last"]).then_inc(glast_in, 16)
            act.wait_ge(router_ready, 1)
            act.activation(logits_sb, pv_bank[:, 0:L], ACT.Copy).then_inc(a_step, 1)
            act.wait_ge(gexp_in, 1)
            act.activation(r_eg, r_eg, ACT.Exp).then_inc(gexp_out, 1)
            act.wait_ge(gexp_in, 2)
            act.activation(r_d, r_d, ACT.Exp).then_inc(gexp_out, 1)

            def pair(before, first=False):
                n = before + 1
                act.wait_ge(gate_ready, n + 1)
                if not first:
                    act.wait_ge(he_ready, before + 1)
                act.activation(sl, banks[2][:, :], ACT.Silu).then_inc(silu_ready, 1)
                act.wait_ge(turned, n + 1)
                if not first:
                    act.wait_ge(down_ready, before + 1)
                act.activation(heT, banks[6][:, :].rearrange("p (a b) -> p a b", b=P), ACT.Copy).then_inc(heT_ready, 1)

            pair(-1, True)
            with act.Fori(0, PAIRS - 1) as j:
                pair(j)
            act.wait_ge(passes_ready, 2)
            n_pass = act.value_load(passes[0:1, 0:1], min_val=1, max_val=MAXPASS)
            with act.If(n_pass > 1):
                with act.Fori(PAIRS - 1, n_pass * PAIRS - 1) as j:
                    pair(j)
            act.activation(stat[:, 4:5], sm("eps"), ACT.Sqrt)
            act.wait_ge(fin_sum, 1)
            for t in range(NT):
                act.activation(SW[:, t, :], x_nat[:, t, :], ACT.Square, accum_out=stat[:, 2 + t:3 + t]).then_inc(a_step, 1)
                act.wait_ge(a_step, t + 2)
                act.activation(stat[:, 2 + t:3 + t], stat[:, 2 + t:3 + t], ACT.Sqrt, bias=sm("eps"), scale=1.0 / D)\
                   .then_inc(fin_root, 1)

        @block.tensor
        def _(pe):
            def take_slot(n):
                pe.wait_ge(w_in_[SLOT_OF[n]], 16 * (len(earlier(n)) + 1))

            def lhs(w, k, c, width=512):
                return w[:, k * width + c:k * width + c + P]

            def fill(n, ks=range(KD)):
                name, i, _ = FILLS[n]
                ps = banks[BANK_OF[n]]
                before = [m for m in range(n) if BANK_OF[m] == BANK_OF[n]]
                if before and ks[0] == 0:
                    wait_emptied(pe, before[-1])
                g = FRONT.index(name)
                w = slot[SLOT_OF[g]]
                if i == 0 and ks[0] == 0:
                    take_slot(g)
                if name[:3] == "ada":
                    for k in range(KD):
                        q = 32 * (k % 4)
                        ins = pe.matmul(ps[q:q + 32, :], cvec[:, k, :], w[:, k * 512:(k + 1) * 512],
                                        start=(k < 4), stop=(k >= KD - 4))
                elif name in ("ff", "fb", "nk"):
                    for k in ks:
                        if name == "ff" and i == 0:
                            pe.wait_ge(h_ready, k + 1)
                        ins = pe.matmul(ps[:, :], lhs(w, k, i * P), hT[:, k, :], start=(k == 0), stop=(k == KD - 1))
                    if ks[-1] < KD - 1:
                        return
                elif name in ("hq", "hg", "nq") or name[:4] == "gate":
                    for c in range(2):
                        for k in range(KD):
                            ins = pe.matmul(ps[:, c * L:(c + 1) * L], lhs(w, k, (2 * i + c) * P), hT[:, k, 0:L],
                                            start=(k == 0), stop=(k == KD - 1))
                elif name in ("hi", "nv", "gq"):
                    for k in range(KD):
                        ins = pe.matmul(ps[:, :], hT[:, k, i * P:(i + 1) * P], w[:, k * 512:(k + 1) * 512],
                                        start=(k == 0), stop=(k == KD - 1))
                elif name == "gkv":
                    for c in range(2):
                        for k in range(KD):
                            t = 2 * i + c
                            ins = pe.matmul(ps[:, c * 256:(c + 1) * 256], hT[:, k, t * P:(t + 1) * P],
                                            w[:, k * 256:(k + 1) * 256], start=(k == 0), stop=(k == KD - 1))
                elif name[:2] == "br":
                    b = int(name[2])
                    src = (aT, bT, cT)[b]
                    for c in range(2):
                        for k in range(4):
                            ins = pe.matmul(ps[:, c * L:(c + 1) * L], lhs(w, k, (2 * i + c) * P, D), src[:, k, :],
                                            start=(k == 0), stop=(k == 3))
                elif name[:3] == "out":
                    for k in range(KD):
                        if name == "out0" and i == 0 and k % 2 == 0:
                            pe.wait_ge(out_by["dve"], 8 + k // 2 + 1)
                        ins = pe.matmul(ps[:, :], yT[:, k, i * P:(i + 1) * P], w[:, k * 512:(k + 1) * 512],
                                        start=(k == 0), stop=(k == KD - 1))
                ins.then_inc(fill_ready, 1)
                if n + 1 == len(FILLS) or FILLS[n + 1][0] != name:
                    pe.wait_ge(fill_ready, n + 1)
                    pe.sem_inc(w_used, 1)

            def take_shared(n):
                if n >= 2:
                    pe.wait_ge(shared_out, n - 1)
                return shared[n % 2]

            def level(v):
                pe.wait_ge(xy_ready, v + 1)
                for q in range(4):
                    dr, t = q // 2, q % 2
                    ps = take_shared(shared_no(f"lev{v}", q))
                    for h in range(HGH):
                        j = dr * 4 + h
                        kk = (X if dr else Y)[:, j, t * P:(t + 1) * P]
                        qq = (QR[:, h] if v == 0 else (Y if dr else X)[:, j])[:, t * P:(t + 1) * P]
                        ins = pe.matmul(ps[:, h * P:(h + 1) * P], kk, qq, start=True, stop=True)
                    ins.then_inc(shared_ready, 1)

            def across():
                pe.wait_ge(xy_ready, LEVELS + 1)
                for dr in range(2):
                    ps = take_shared(shared_no("lev8", dr))
                    for h in range(HGH):
                        kk = (X if dr else Y)[:, dr * 4 + h, dr * P:(dr + 1) * P]
                        qq = (Y if dr else X)[:, dr * 4 + h, (1 - dr) * P:(2 - dr) * P]
                        ins = pe.matmul(ps[:, h * P:(h + 1) * P], kk, qq, start=True, stop=True)
                    ins.then_inc(shared_ready, 1)

            def ctx_keys():
                pe.wait_ge(kc_ready, 1)
                for q in range(4):
                    dr, t = q // 2, q % 2
                    ps = take_shared(shared_no("kc", q))
                    for h in range(HGH):
                        ins = pe.transpose(ps[:, h * P:(h + 1) * P], Kc[:, dr * 4 + h, t * P:(t + 1) * P], ident)
                    ins.then_inc(shared_ready, 1)

            def ctx_state():
                pe.wait_ge(shared_out, shared_no("kc", 3) + 1)
                wait_emptied(pe, fill_no("hi", 3))
                for dr in range(2):
                    ps = take_shared(shared_no("s0", dr))
                    for h in range(HGH):
                        for t in range(NT):
                            ins = pe.matmul(ps[:, h * P:(h + 1) * P], kc_tile(dr, t, h), v_hg[:, NT + t, h * P:(h + 1) * P],
                                            start=(t == 0), stop=(t == NT - 1))
                    ins.then_inc(shared_ready, 1)

            def kc_tile(dr, t, h):
                o = F0 + 6144 + ((dr * 2 + t) * HGH + h) * P
                return sb[:, o:o + P]

            def outputs():
                pe.wait_ge(xy_ready, LEVELS + 2)
                pe.wait_ge(shared_out, shared_no("lev8", 1) + 1)
                for i in range(2):
                    ps = take_shared(shared_no("o", i))
                    for hh in range(2):
                        h = 2 * i + hh
                        for t in range(NT):
                            o = ps[:, hh * L + t * P:hh * L + (t + 1) * P]
                            for dr in range(2):
                                cols = slice(h * P, (h + 1) * P)
                                pe.matmul(o, v_hg[:, t, cols], AT[:, dr * 3 + t, cols], start=(dr == 0), stop=False)
                                if t != dr:
                                    pe.matmul(o, v_hg[:, dr, cols], AT[:, dr * 3 + 2, cols], start=False, stop=False)
                                qq = (Y if dr else X)[:, dr * 4 + h, t * P:(t + 1) * P]
                                ins = pe.matmul(o, S0[:, dr * 4 + h, :], qq, start=False, stop=(dr == 1))
                    ins.then_inc(shared_ready, 1)

            def square_sums():
                pe.wait_ge(o_sq, 1)
                for i in range(2):
                    ps = take_shared(shared_no("osq", i))
                    pe.matmul(ps[:, :], ones, o_tmp[:, 2 * i:2 * i + 2, :].rearrange("p a b -> p (a b)"),
                              start=True, stop=True).then_inc(shared_ready, 1)

            def turn_gqa():
                pe.wait_ge(gqa_ready, 1)
                for i in range(2):
                    ps = take_shared(shared_no("gqT", i))
                    for r in range(2):
                        for t in range(NT):
                            src = gq[:, t, (2 * i + r) * P:(2 * i + r + 1) * P]
                            ins = pe.transpose(ps[:, r * L + t * P:r * L + (t + 1) * P], src, ident)
                    ins.then_inc(shared_ready, 1)
                ps = take_shared(shared_no("gkT"))
                for t in range(4):
                    ins = pe.transpose(ps[:, t * P:(t + 1) * P], gkv[:, t, 0:P], ident)
                ins.then_inc(shared_ready, 1)

            def ada_turn(g):
                wait_emptied(pe, fill_no(f"ada{g}"))
                ps = take_shared(shared_no("ada", g))
                src = ada_place(g)
                if g in ROW_GROUPS:
                    ins = pe.matmul(ps[:, :], sm("stream0"), src, start=True, stop=True)
                else:
                    for c in range(4):
                        ins = pe.transpose(ps[:, c * P:(c + 1) * P], src[:, c * P:(c + 1) * P], ident)
                ins.then_inc(shared_ready, 1)

            def scores(i):
                kind, t, c = UNITS[i]
                if i:
                    pe.wait_ge(exp_ready, 2 * i)
                q, k = (na_q[:, c, :], na_k[:, c, :]) if kind == "na" else (gqT[:, c, :], gkT)
                for e in range(2):
                    b = e * HD
                    pe.matmul(score[e][:, :], q[b:b + HD, t * P:(t + 1) * P], k[b:b + HD, :],
                              start=True, stop=True).then_inc(scores_ready, 1)

            def turn_probs(i):
                for e in range(2):
                    pe.wait_ge(norm_ready, 2 * i + e + 1)
                    ps = take_shared(shared_no("pT", 2 * i + e))
                    for c in range(4):
                        ins = pe.transpose(ps[:, c * P:(c + 1) * P], probs[:, e, c * P:(c + 1) * P], ident)
                    ins.then_inc(shared_ready, 1)

            def values(i):
                kind, t, c = UNITS[i]
                pe.wait_ge(shared_out, shared_no("pT", 2 * i + 1) + 1)
                if i >= 4 and c == 0:
                    pe.wait_ge(pv_out, i // 4)
                for j in range(4):
                    for e in range(2):
                        v = na_v[:, j, (2 * c + e) * HD:(2 * c + e + 1) * HD] if kind == "na" else \
                            gkv[:, j, P + e * HD:P + (e + 1) * HD]
                        ins = pe.matmul(pv_bank[e * HD:(e + 1) * HD, c * P:(c + 1) * P], v,
                                        probsT[:, e, j * P:(j + 1) * P], start=(j == 0), stop=(j == 3))
                ins.then_inc(pv_ready, 1)

            pe.wait_ge(ones_set, 1)
            for k in range(KD):
                pe.wait_ge(sq_ready, k + 1)
                ins = pe.matmul(pv_bank[:, :], ones_now, sq[:, k, :], start=(k == 0), stop=(k == KD - 1))
            ins.then_inc(rms_ready, 1)
            pe.wait_ge(c_ready, 1)
            pe.wait_ge(small_in, 16)
            early = range(fill_no("ff"), fill_no("ff") + PBANKS)
            for first, second in ((0, 2), (1, 3)):
                fill(fill_no(f"ada{first}"))
                fill(fill_no(f"ada{second}"))
                ada_turn(first)
                ada_turn(second)
                if first == 0:
                    for n in early:
                        fill(n, range(KD // 2))
            for n in early:
                fill(n, range(KD // 2, KD))
            for n in range(early[-1] + 1, fill_no("hg", 1) + 1):
                fill(n)
            ctx_keys()
            for v in range(4):
                level(v)
                fill(fill_no("hi", v))
            for v in range(4, 8):
                level(v)
                fill(fill_no("nk", v - 4))
            ctx_state()
            fill(fill_no("nq", 0))
            across()
            fill(fill_no("nq", 1))
            fill(fill_no("nv", 0))
            outputs()
            for n in range(fill_no("nv", 1), fill_no("nv", 3) + 1):
                fill(n)
            square_sums()
            wait_emptied(pe, fill_no("nv", 3))
            for i in range(STEPS):
                for g in ada_in_step(i - 1):
                    ada_turn(g)
                if i == 2 * 4:
                    turn_gqa()
                    pe.wait_ge(shared_out, shared_no("gkT") + 1)
                scores(i)
                if i:
                    values(i - 1)
                for n in FILLER_AT[i]:
                    fill(n)
                turn_probs(i)
            for g in ada_in_step(STEPS - 1):
                ada_turn(g)
            values(STEPS - 1)
            for b in range(3):
                if b == 0:
                    pe.wait_ge(pv_out, 2)
                elif b == 1:
                    pe.wait_ge(b_ready, 1)
                else:
                    pe.wait_ge(pv_out, 4)
                for i in range(4):
                    fill(fill_no(f"br{b}", i))
            for n in range(fill_no("out0"), len(FILLS)):
                fill(n)
            def keep_warm(n):
                for _ in range(n):
                    pe.matmul(score[0][:, :], ident, small[:, 0:512], start=True, stop=True)

            keep_warm(5)
            for q in range(4):
                if q == 0:
                    pe.wait_ge(xn_ready, NT)
                elif q > 1:
                    keep_warm(1)
                ps = take_shared(shared_no("fT", q))
                for c in range(2):
                    for t in range(NT):
                        k = 2 * q + c
                        ins = pe.transpose(ps[:, c * L + t * P:c * L + (t + 1) * P], xn[:, t, k * P:(k + 1) * P], ident)
                ins.then_inc(shared_ready, 1)
            keep_warm(1)
            pe.wait_ge(shared_out, shared_no("fT", 3) + 1)
            pe.wait_ge(pv_out, 4)
            for k in range(KD):
                q = 32 * (k % 4)
                ins = pe.matmul(pv_bank[q:q + 32, 0:L], sm("router")[:, k, :], fT[:, k, :],
                                start=(k < 4), stop=(k >= KD - 4))
            ins.then_inc(router_ready, 1)
            keep_warm(2)
            pe.wait_ge(a_step, 1)
            ps = take_shared(shared_no("rT"))
            for t in range(NT):
                ins = pe.transpose(ps[:, t * P:(t + 1) * P], logits_sb[:, t * P:(t + 1) * P], ident)
            ins.then_inc(shared_ready, 1)
            keep_warm(4)
            pe.wait_ge(member_ready, 1)
            both = member.rearrange("p t n -> p (t n)")
            pe.matmul(pv_bank[:, 0:32], below, both, start=True, stop=True)
            pe.matmul(pv_bank[:, 32:64], ones, both, start=True, stop=True).then_inc(pos_ready, 1)

            def turn_slots(p):
                for q in range(4):
                    n = p * 4 + q
                    if q == 0:
                        pe.wait_ge(weighted, p + 1)
                        if isinstance(p, int):
                            pe.wait_ge(passes_ready, 2)
                        else:
                            pe.wait_ge(scat_out, p * (4 * PAIRS))
                    if q > 1:
                        pe.wait_ge(turn_out, n - 1)
                    for c in range(4):
                        pr, t = 2 * q + c // 2, c % 2
                        ins = pe.transpose(banks[6 + q % 2][:, c * P:(c + 1) * P], SW[:, t, pr * P:(pr + 1) * P], ident)
                    ins.then_inc(turn_ready, 1)

            def gather(n):
                pe.wait_ge(cut_ready, n + 1)
                if not isinstance(n, int) or n:
                    pe.wait_ge(h_out, 2 * n)
                for i in range(2):
                    for c in range(4):
                        for t in range(NT):
                            ins = pe.matmul(banks[i][:, c * P:(c + 1) * P], xn[:, t, (4 * i + c) * P:(4 * i + c + 1) * P],
                                            S_now[:, t, :], start=(t == 0), stop=(t == NT - 1))
                    if i == 1:
                        ins.then_inc(gather_ready, 1)

            def two_experts(bank, uses, s, parts, lhsT, cols):
                for e in range(2):
                    pe.wait_ge(w_in_[s + e], slot_value(s + e) + 16 + 16 * uses)
                for k in range(parts):
                    for e in range(2):
                        ins = pe.matmul(bank[e * CAP:(e + 1) * CAP, :], lhsT[:, k, e * CAP:(e + 1) * CAP],
                                        slot[s + e][:, k * cols[0] + cols[1]:k * cols[0] + cols[1] + 512],
                                        start=(k == 0), stop=(k == parts - 1))
                return ins

            def gate_up(before, half, odd, first=False):
                n = before + 1
                pe.wait_ge(h_out, 2 * n + 2)
                if not first:
                    pe.wait_ge(he_ready, before + 1)
                two_experts(banks[2], half, 6 if odd else 0, KD, h_sb, (512, 0)).then_inc(gate_ready, 1)
                two_experts(banks[3], n, 2, KD, h_sb, (512, 0)).then_inc(up_ready, 1)

            def turn_hidden(n):
                pe.wait_ge(he_ready, n + 1)
                if not isinstance(n, int) or n > 1:
                    pe.wait_ge(scat_out, 4 * n - 4)
                for k in range(KH):
                    ins = pe.transpose(banks[6][:, k * P:(k + 1) * P], he[:, k * P:(k + 1) * P], ident)
                ins.then_inc(turned, 1)

            def down(n, first=False):
                pe.wait_ge(heT_ready, n + 1)
                if not first:
                    pe.wait_ge(y_out, 2 * n)
                for i in range(2):
                    ins = two_experts(banks[4 + i], n, 4, KH, heT, (D, 512 * i))
                ins.then_inc(down_ready, 1)

            def scatter(n, last=False):
                pe.wait_ge(y_out, 2 * n + 2)
                pe.wait_ge(cutT_ready, n + 1)
                for q in range(4):
                    t, i = q // 2, q % 2
                    if q == 0:
                        pe.wait_ge(heT_ready, n + (1 if last else 2))
                    if q > 1:
                        pe.wait_ge(scat_out, 4 * n + q - 1)
                    elif not isinstance(n, int) or n:
                        pe.wait_ge(scat_out, 4 * n)
                    pe.matmul(banks[6 + i][:, :], ST_now[:, t, :], y_sb[:, i * 512:(i + 1) * 512],
                              start=True, stop=True).then_inc(scat_ready, 1)

            def one_pass(p):
                first = isinstance(p, int)
                n0, half = p * PAIRS, p * (PAIRS // 2)
                gather(n0)
                gate_up(n0 - 1, half, 0, first)
                gather(n0 + 1)
                turn_slots(p)
                pe.wait_ge(turn_out, p * 4 + 4)
                turn_hidden(n0)
                down(n0, first)
                with pe.Fori(0, (PAIRS - 2) // 2) as j:
                    for u in range(2):
                        before = n0 + j * 2 + u
                        gate_up(before, half + j + u, 1 - u)
                        gather(before + 2)
                        turn_hidden(before + 1)
                        scatter(before)
                        down(before + 1)
                before = n0 + PAIRS - 2
                gate_up(before, half + (PAIRS - 2) // 2, 1)
                turn_hidden(before + 1)
                scatter(before)
                down(before + 1)
                scatter(before + 1, last=True)

            one_pass(0)
            n_pass = pe.value_load(passes[0:1, 0:1], min_val=1, max_val=MAXPASS)
            with pe.If(n_pass > 1):
                with pe.Fori(1, n_pass) as p:
                    one_pass(p)
            pe.nop()

        @block.vector
        def _(dve):
            steps = [0]

            def link(ins):
                steps[0] += 1
                ins.then_inc(v_step, 1)
                dve.wait_ge(v_step, steps[0])

            def shared_wait(n):
                dve.wait_ge(shared_ready, n + 1)
                return shared[n % 2]

            dve.memset(ones_now, 1.0).then_inc(ones_set, 1)
            dve.memset(zeros, 0.0)
            dve.wait_ge(small_in, 16)
            lg = sm("lb")
            dve.tensor_tensor(lb_e, lg, lg, ALU.subtract).then_inc(lb_in, 1)
            dve.wait_ge(rms_root, 1)
            link(dve.reciprocal(rstd_row, rstd_row))
            def add_ada(g):
                n = shared_no("ada", g)
                ps = shared_wait(n)
                if g in ROW_GROUPS:
                    r = ROW_GROUPS.index(g)
                    if r == 0:
                        dve.wait_ge(brow_in, 16)
                    dst = (row2, row5)[r // 2][:, 512 * (r % 2):512 * (r % 2) + 512]
                    dve.tensor_tensor(dst, ps[:, :], b_rows[:, r, :], ALU.add).then_inc(shared_out, 1)
                else:
                    parts = ps[:, :].rearrange("p (c q s) -> p c s q", c=4, q=4)[:, :, 0:2, :]
                    dve.tensor_reduce(mod[:, 4 * g:4 * g + 4, :], parts, AX.X, ALU.add).then_inc(shared_out, 1)

            b_ada = sm("b_ada")
            for half in range(2):
                ks = slice(4 * half, 4 * half + 4)
                for k in range(4 * half, 4 * half + 4):
                    dve.tensor_tensor(hT[:, k, :], hT[:, k, :], rstd_row, ALU.mult)
                add_ada(half)
                add_ada(2 + half)
                dve.wait_ge(shared_out, 2 * half + 2)
                for m in (4 * half, 8 + 4 * half):
                    ins = dve.tensor_tensor(mod[:, m:m + 4, :], mod[:, m:m + 4, :],
                                            b_ada[:, m:m + 4].unsqueeze(2).broadcast_to([P, 4, 2]), ALU.add)
                link(ins)
                link(dve.tensor_scalar(A_mix[:, ks, :], mod[:, 8 + 4 * half:12 + 4 * half, :], 1.0, None, ALU.add))
                link(dve.tensor_tensor(A_mix[:, ks, :], A_mix[:, ks, :],
                                       sm("g_mix")[:, ks].unsqueeze(2).broadcast_to([P, 4, 2]), ALU.mult))
                for k in range(4 * half, 4 * half + 4):
                    for s in range(2):
                        ins = dve.tensor_scalar(hT[:, k, s * L:(s + 1) * L], hT[:, k, s * L:(s + 1) * L],
                                                A_mix[:, k, s:s + 1], mod[:, k, s:s + 1], ALU.mult, ALU.add)
                    ins.then_inc(h_ready, 1)
            dve.wait_ge(lb_ready, 1)
            link(dve.reciprocal(lb_p, lb_e))
            link(dve.tensor_tensor(lb_p, lb_e, lb_p, ALU.mult))
            link(dve.tensor_tensor(lower, lb_p, lb_p, ALU.subtract))
            link(dve.tensor_scalar(span, lower, -1.0, 1.0, ALU.mult, ALU.add))

            for dr in range(2):
                name = ("ff", "fb")[dr]
                for h in range(HGH):
                    j = dr * 4 + h
                    dve.wait_ge(out_by["act"], emptied(fill_no(name, h))[1])
                    ins = dve.tensor_scalar(forget[:, :, j, :], forget[:, :, j, :], span[:, j:j + 1],
                                            lower[:, j:j + 1], ALU.mult, ALU.add)
                link(ins)
                keys = (X if dr else Y)[:, dr * 4:dr * 4 + 4, :]
                link(dve.tensor_scalar(keys, T_lat[:, dr * 4:dr * 4 + 4, :], -1.0, 1.0, ALU.mult, ALU.add))
                dve.tensor_scalar(Kc[:, dr * 4:dr * 4 + 4, :], F_ctx[:, dr * 4:dr * 4 + 4, :], -1.0, 1.0,
                                  ALU.mult, ALU.add)
                for h in range(HGH):
                    j = dr * 4 + h
                    dst = kcn[:, j, :]
                    if dr == 0:
                        dve.memset(dst[:, L - 1:L], 1.0)
                        ins = dve.tensor_tensor_scan(dst[:, 0:L - 1][:, ::-1], F_ctx[:, j, 1:L][:, ::-1],
                                                     zeros[:, 0:L - 1], 1.0, ALU.mult, ALU.add)
                    else:
                        dve.memset(dst[:, 0:1], 1.0)
                        ins = dve.tensor_tensor_scan(dst[:, 1:L], F_ctx[:, j, 0:L - 1],
                                                     zeros[:, 0:L - 1], 1.0, ALU.mult, ALU.add)
                link(ins)
            link(dve.tensor_tensor(Kc, Kc, kcn, ALU.mult))
            dve.sem_inc(kc_ready, 1)
            dve.wait_ge(out_by["act"], emptied(fill_no("hq", 1))[1])
            dve.tensor_tensor(QR, QR, sig_q, ALU.mult).then_inc(silu_hg, 1)
            dve.wait_ge(silu_hg, 1)
            dve.tensor_tensor(X[:, 0:4, :], QR, T_lat[:, 0:4, :], ALU.mult)
            dve.tensor_tensor(Y[:, 4:8, :], QR, T_lat[:, 4:8, :], ALU.mult).then_inc(xy_ready, 2)
            dve.wait_ge(out_by["act"], emptied(fill_no("hg", 1))[1])
            dve.tensor_tensor(bT, bT, sig_g, ALU.mult).then_inc(silu_hg, 1)

            def shared_copy(n, dst):
                dve.tensor_copy(dst, shared_wait(n)[:, :]).then_inc(shared_out, 1)

            for q in range(4):
                o = F0 + 6144 + q * 512
                shared_copy(shared_no("kc", q), sb[:, o:o + 512])

            def products(v):
                for q in range(4):
                    dr, t = q // 2, q % 2
                    n = shared_no(f"lev{v}", q)
                    ps = shared_wait(n)[:, :].rearrange("p (h t) -> p h t", h=HGH)
                    dst = AT[:, dr * 3 + t, :].rearrange("p (h t) -> p h t", h=HGH)
                    if v == 0:
                        m = ident.unsqueeze(1).broadcast_to([P, HGH, P])
                        dve.tensor_tensor(dst, ps, m, ALU.mult).then_inc(shared_out, 1)
                    else:
                        m = masks[:, dr * (LEVELS - 1) + v - 1, :].unsqueeze(1).broadcast_to([P, HGH, P])
                        dve.wait_ge(shared_out, n - 3)
                        dve.copy_predicated(dst, m, ps).then_inc(shared_out, 1)

            def join(v):
                m = 1 << (v - 1)
                t_ = T_of[v - 1]
                pairs = t_.rearrange("p (b s) -> p b s", s=2)
                xv = at(A0 + 7168, 2048).rearrange("p (b s m) -> p b s m", s=2, m=m)
                yv = at(A0 + 9216, 2048).rearrange("p (b s m) -> p b s m", s=2, m=m)
                nb = 2048 // (2 * m)
                left = pairs[:, :, 0:1].broadcast_to([P, nb, m])
                right = pairs[:, :, 1:2].broadcast_to([P, nb, m])
                dve.tensor_tensor(xv[:, :, 1, :], xv[:, :, 1, :], left, ALU.mult)
                ins = dve.tensor_tensor(yv[:, :, 0, :], yv[:, :, 0, :], right, ALU.mult)
                if v < LEVELS:
                    ins.then_inc(xy_ready, 1)
                    dve.tensor_tensor(T_of[v], pairs[:, :, 0], pairs[:, :, 1], ALU.mult).then_inc(v_step, 1)
                    steps[0] += 1
                else:
                    ins.then_inc(xy_ready, 1)

            T_of = [at(F0, 2048)]
            for v in range(1, LEVELS):
                size = 2048 >> v
                T_of.append(at(C0 if v % 2 else F0, size))
            T_of.append(at(C0, 2048 >> LEVELS))

            dve.wait_ge(masks_ready, 1)
            products(0)
            for v in range(1, LEVELS):
                products(v)
                dve.wait_ge(v_step, steps[0])
                dve.wait_ge(xy_ready, v + 1)
                join(v)
            for q in range(2):
                shared_copy(shared_no("s0", q), S0[:, 4 * q:4 * q + 4, :].rearrange("p a b -> p (a b)"))
            for dr in range(2):
                shared_copy(shared_no("lev8", dr), AT[:, dr * 3 + 2, :])
            dve.wait_ge(v_step, steps[0])
            dve.wait_ge(xy_ready, LEVELS + 1)
            join(LEVELS)
            for q in range(2):
                shared_copy(shared_no("o", q), o_sb[:, 2 * q:2 * q + 2, :].rearrange("p a b -> p (a b)"))

            for i in range(2):
                dve.wait_ge(o_root, i + 1)
                dve.reciprocal(o_tmp[:, 2 * i:2 * i + 2, :], o_tmp[:, 2 * i:2 * i + 2, :]).then_inc(shared_out, 1)
            dve.wait_ge(shared_out, shared_no("osq", 1) + 1)
            link(dve.tensor_tensor(o_sb, o_sb, o_tmp, ALU.mult))
            dve.scalar_tensor_tensor(out=bT, in0=o_sb, scalar=sm("hg_g"), in1=bT, op0=ALU.mult, op1=ALU.mult)\
               .then_inc(b_ready, 1)

            def gqa_squares():
                wait_emptied(dve, fill_no("gkv", 1))
                q = gq.rearrange("p t n -> p (t n)")
                dve.tensor_tensor(g_sq[:, 0:1024], q, q, ALU.mult)
                k = gkv[:, :, 0:P]
                link(dve.tensor_tensor(g_sq[:, 1024:1536].rearrange("p (a b) -> p a b", b=P), k, k, ALU.mult))
                dve.tensor_reduce(g_ms, g_sq.rearrange("p (a b) -> p a b", b=HD), AX.X, ALU.add).then_inc(g_sum, 1)

            def gqa_norms():
                dve.wait_ge(g_root, 1)
                link(dve.reciprocal(g_ms, g_ms))
                dve.tensor_scalar(g_ms[:, 0:16], g_ms[:, 0:16], QSCALE, None, ALU.mult).then_inc(g_rec, 1)

            def maxima(i):
                kind, t, c = UNITS[i]
                if i == 0:
                    dve.wait_ge(bias_in, 16)
                for e in range(2):
                    dve.wait_ge(scores_ready, 2 * i + e + 1)
                    s = score[e]
                    if kind == "na":
                        i0 = 2 - 2 * t
                        link(dve.tensor_tensor(s[:, 0:L], s[:, 0:L],
                                               na_bias[:, 2 * c + e, i0 * GRID:(i0 + ROWS) * GRID], ALU.add))
                    u = 2 * i + e
                    dve.tensor_reduce(nmax[:, u:u + 1], s[:, :], AX.X, ALU.max, negate=True).then_inc(max_ready, 1)

            def normalise(i):
                dve.wait_ge(exp_ready, 2 * i + 2)
                r = sums[:, 2 * i:2 * i + 2]
                link(dve.reciprocal(r, r))
                for e in range(2):
                    dve.tensor_scalar(probs[:, e, :], probs[:, e, :], r[:, e:e + 1], None, ALU.mult).then_inc(norm_ready, 1)

            def values_out(k):
                dve.wait_ge(pv_ready, 4 * (k + 1))
                dst = (aT if k < 2 else cT)[:, :, (k % 2) * P:(k % 2 + 1) * P]
                dve.tensor_copy(dst, pv_bank[:, :].rearrange("p (c q) -> p c q", c=4)).then_inc(pv_out, 1)

            for i in range(STEPS):
                for g in ada_in_step(i - 1):
                    add_ada(g)
                if i == G_STEP + 1:
                    gqa_norms()
                if i == 2 * 4:
                    for q in range(2):
                        shared_copy(shared_no("gqT", q), gqT[:, 2 * q:2 * q + 2, :].rearrange("p a b -> p (a b)"))
                    shared_copy(shared_no("gkT"), gkT)
                maxima(i)
                normalise(i)
                if i:
                    if i % 4 == 0:
                        values_out(i // 4 - 1)
                    dve.wait_ge(pv_ready, i)
                for e in range(2):
                    shared_copy(shared_no("pT", 2 * i + e), probsT[:, e, :])
                if i == G_STEP:
                    gqa_squares()
            for g in ada_in_step(STEPS - 1):
                add_ada(g)
            values_out(3)

            dve.wait_ge(shared_out, shared_no("ada", 11) + 1)
            link(dve.tensor_tensor(mod[:, 24:40, 0], mod[:, 24:40, 0], b_ada[:, 24:40], ALU.add))
            link(dve.tensor_scalar(A_ffn, mod[:, 32:40, 0], 1.0, None, ALU.add))
            link(dve.tensor_tensor(A_ffn, A_ffn, sm("g_ffn"), ALU.mult))

            dve_out = out_by["dve"]
            for n in range(fill_no("br0"), fill_no("out0")):
                b, i = int(FILLS[n][0][2]), FILLS[n][1]
                dve.wait_ge(fill_ready, n + 1)
                if i == 0:
                    dve.wait_ge(sig_gates, b + 1)
                ps = banks[BANK_OF[n]][:, :].rearrange("p (a b) -> p a b", a=2)
                g = gates[:, b * KD + 2 * i:b * KD + 2 * i + 2, :]
                y = yT[:, 2 * i:2 * i + 2, :]
                if b == 0:
                    dve.tensor_tensor(y, ps, g, ALU.mult).then_inc(dve_out, 1)
                else:
                    link(dve.tensor_tensor(g, ps, g, ALU.mult))
                    dve.wait_ge(dve_out, 4 * (b - 1) + i + 1)
                    dve.tensor_tensor(y, y, g, ALU.add).then_inc(dve_out, 1)

            dve.wait_ge(xnat_in, 16)
            for n in range(fill_no("out0"), len(FILLS)):
                i, t = int(FILLS[n][0][3]), FILLS[n][1]
                cols = slice(512 * i, 512 * i + 512)
                dve.wait_ge(fill_ready, n + 1)
                dve.tensor_tensor(xn[:, t, cols], banks[BANK_OF[n]][:, :], row2[:, cols], ALU.mult).then_inc(dve_out, 1)
                dve.wait_ge(dve_out, emptied(n)[1])
                dve.tensor_tensor(x_nat[:, t, cols], x_nat[:, t, cols], xn[:, t, cols], ALU.add).then_inc(x1_ready, 1)
            dve.wait_ge(x1_root, 1)
            link(dve.reciprocal(stat[:, 0:NT], stat[:, 0:NT]))
            for t in range(NT):
                dve.tensor_scalar(xn[:, t, :], x_nat[:, t, :], stat[:, t:t + 1], None, ALU.mult).then_inc(xn_ready, 1)
            for q in range(4):
                n = shared_no("fT", q)
                ps = shared_wait(n)
                for c in range(2):
                    k = 2 * q + c
                    ins = dve.tensor_scalar(fT[:, k, :], ps[:, c * L:(c + 1) * L], A_ffn[:, k:k + 1],
                                            mod[:, 3 * KD + k, 0:1], ALU.mult, ALU.add)
                ins.then_inc(shared_out, 1)

            def wide(v, n):
                return v.unsqueeze(2).broadcast_to([P, NT, n])

            def first_best(dst, x, best, weight, tmp, tmp_max, n):
                link(dve.tensor_tensor(tmp, x, wide(best, n), ALU.is_equal))
                link(dve.tensor_tensor(tmp, tmp, weight.unsqueeze(1).broadcast_to([P, NT, n]), ALU.mult))
                link(dve.tensor_reduce(tmp_max, tmp, AX.X, ALU.max))
                link(dve.tensor_tensor(dst, tmp, wide(tmp_max, n), ALU.is_equal))

            ps = shared_wait(shared_no("rT"))
            parts = ps[:, 0:L].rearrange("p (t q n) -> p t n q", t=NT, q=4)[:, :, 0:ROUTES, :]
            dve.tensor_reduce(r_all, parts, AX.X, ALU.add).then_inc(shared_out, 1)
            dve.wait_ge(shared_out, shared_no("rT") + 1)
            link(dve.tensor_tensor(r_all, r_all, sm("router_b").unsqueeze(1).broadcast_to([P, NT, ROUTES]), ALU.add))
            dve.tensor_copy(r_g, r_all[:, :, 0:NG])
            link(dve.tensor_copy(r_e, r_all[:, :, NG:ROUTES]))
            link(dve.tensor_reduce(r_gm, r_g, AX.X, ALU.max))
            dve.tensor_tensor(r_eg, r_g, wide(r_gm, NG), ALU.subtract).then_inc(gexp_in, 1)
            first_best(r_sel, r_g, r_gm, sm("rank")[:, NE - NG:NE], r_t, r_sm, NG)
            sel = r_sel.rearrange("p t g -> p (t g)").unsqueeze(2).broadcast_to([P, NT * NG, EPG])
            em = r_em.rearrange("p t (g e) -> p (t g) e", g=NG)
            link(dve.tensor_tensor(em, r_e.rearrange("p t (g e) -> p (t g) e", g=NG), sel, ALU.mult))
            link(dve.tensor_scalar(r_t, r_sel, -1.0, -NEG, ALU.add, ALU.mult))
            outside = r_t.rearrange("p t g -> p (t g)").unsqueeze(2).broadcast_to([P, NT * NG, EPG])
            link(dve.tensor_tensor(em, em, outside, ALU.add))
            link(dve.tensor_reduce(r_m1, r_em, AX.X, ALU.max))
            first_best(oh1, r_em, r_m1, sm("rank"), r_et, r_sm, NE)
            link(dve.scalar_tensor_tensor(out=r_em, in0=oh1, scalar=3 * NEG, in1=r_em, op0=ALU.mult, op1=ALU.add))
            link(dve.tensor_reduce(r_m2, r_em, AX.X, ALU.max))
            dve.tensor_tensor(r_d, r_m2, r_m1, ALU.subtract).then_inc(gexp_in, 1)
            first_best(oh2, r_em, r_m2, sm("rank"), r_et, r_sm, NE)
            dve.tensor_tensor(member, oh1, oh2, ALU.add).then_inc(member_ready, 1)
            dve.wait_ge(gexp_out, 2)
            link(dve.tensor_reduce(r_gs, r_eg, AX.X, ALU.add))
            link(dve.tensor_scalar(r_w1, r_d, 1.0, None, ALU.add))
            link(dve.tensor_tensor(r_w1, r_w1, r_gs, ALU.mult))
            link(dve.reciprocal(r_w1, r_w1))
            link(dve.tensor_tensor(r_w2, r_w1, r_d, ALU.mult))
            dve.tensor_tensor(oh1, oh1, wide(r_w1, NE), ALU.mult)
            link(dve.tensor_tensor(oh2, oh2, wide(r_w2, NE), ALU.mult))
            link(dve.tensor_tensor(comb, oh1, oh2, ALU.add))
            dve.wait_ge(pos_ready, 1)
            link(dve.tensor_copy(posm, pv_bank[:, 0:32].rearrange("p (t n) -> p t n", t=NT)))
            link(dve.tensor_copy(first_sum, pv_bank[:, 32:48]))
            link(dve.tensor_tensor(posm[:, 1, :], posm[:, 1, :], first_sum, ALU.add))
            dve.wait_ge(member_ready, 1)
            link(dve.scalar_tensor_tensor(out=posm, in0=posm, scalar=1.0, in1=member, op0=ALU.add, op1=ALU.mult))
            link(dve.tensor_scalar(posm, posm, -1.0, None, ALU.add))
            def build_slots(p):
                for e0, e1 in ((0, 2), (2, NE)):
                    for t in range(NT):
                        s = S_all[:, t, e0 * CAP:e1 * CAP].rearrange("p (e c) -> p e c", c=CAP)
                        ins = dve.tensor_tensor(s, slots_iota.unsqueeze(1).broadcast_to([P, e1 - e0, CAP]),
                                                posm[:, t, e0:e1].unsqueeze(2).broadcast_to([P, e1 - e0, CAP]),
                                                ALU.is_equal)
                    ins.then_inc(slots_ready, 1)
                dve.wait_ge(slots_ready, 2 * p + 2)
                for t in range(NT):
                    s = S_all[:, t, :].rearrange("p (e c) -> p e c", c=CAP)
                    w = SW[:, t, :].rearrange("p (e c) -> p e c", c=CAP)
                    ins = dve.tensor_tensor(w, s, comb[:, t, :].unsqueeze(2).broadcast_to([P, NE, CAP]), ALU.mult)
                ins.then_inc(weighted, 1)

            build_slots(0)
            link(dve.tensor_tensor(first_sum, first_sum, pv_bank[:, 48:64], ALU.add))
            link(dve.tensor_reduce(count, first_sum, AX.X, ALU.max))
            link(dve.tensor_scalar(over, sm("limits"), count, None, ALU.is_lt))
            link(dve.tensor_reduce(passes_f, over, AX.X, ALU.add))
            dve.tensor_scalar(passes[0:1, 0:1], passes_f[0:1, :], 1.0, None, ALU.add).then_inc(passes_ready, 2)

            def spread(v):
                return v.unsqueeze(2).broadcast_to([P, 4, P])

            def modulate(n):
                dve.wait_ge(gather_ready, n + 1)
                if not isinstance(n, int) or n:
                    dve.wait_ge(up_ready, n)
                for i in range(2):
                    ps = banks[i][:, :].rearrange("p (a b) -> p a b", b=P)
                    dve.tensor_tensor(h_sb[:, 4 * i:4 * i + 4, :], ps, spread(A_ffn[:, 4 * i:4 * i + 4]), ALU.mult)
                dve.drain()
                for i in range(2):
                    hh = h_sb[:, 4 * i:4 * i + 4, :]
                    dve.tensor_tensor(hh, hh, spread(mod[:, 3 * KD + 4 * i:3 * KD + 4 * i + 4, 0]), ALU.add)\
                       .then_inc(h_out, 1)

            def gated(before, first=False):
                n = before + 1
                dve.wait_ge(silu_ready, n + 1)
                dve.wait_ge(up_ready, n + 1)
                if not first:
                    dve.wait_ge(turned, before + 1)
                dve.tensor_tensor(he, sl, banks[3][:, :], ALU.mult).then_inc(he_ready, 1)

            def scattered(n):
                for q in range(4):
                    t, i = q // 2, q % 2
                    dve.wait_ge(scat_ready, 4 * n + q + 1)
                    y = x_nat[:, t, 512 * i:512 * i + 512]
                    dve.tensor_tensor(y, y, banks[6 + i][:, :], ALU.add).then_inc(scat_out, 1)

            def experts_out(n):
                dve.wait_ge(down_ready, n + 1)
                if not isinstance(n, int) or n:
                    dve.wait_ge(scat_ready, 4 * n)
                for i in range(2):
                    cols = slice(512 * i, 512 * i + 512)
                    dve.tensor_tensor(y_sb[:, cols], banks[4 + i][:, :], row5[:, cols], ALU.mult).then_inc(y_out, 1)

            def slots_out(p):
                for q in range(4):
                    dve.wait_ge(turn_ready, p * 4 + q + 1)
                    dve.tensor_copy(ST_all[:, 2 * q:2 * q + 2, :].rearrange("p a b -> p (a b)"),
                                    banks[6 + q % 2][:, :]).then_inc(turn_out, 1)
                dve.wait_ge(turn_out, p * 4 + 4)
                dve.sem_inc(turned_slots, 1)

            def one_pass(p):
                first = isinstance(p, int)
                n0 = p * PAIRS
                modulate(n0)
                gated(n0 - 1, first)
                slots_out(p)
                modulate(n0 + 1)
                experts_out(n0)
                with dve.Fori(0, PAIRS - 2) as j:
                    before = n0 + j
                    gated(before)
                    modulate(before + 2)
                    scattered(before)
                    experts_out(before + 1)
                before = n0 + PAIRS - 2
                gated(before)
                scattered(before)
                experts_out(before + 1)
                scattered(before + 1)

            one_pass(0)
            n_pass = dve.value_load(passes[0:1, 0:1], min_val=1, max_val=MAXPASS)
            with dve.If(n_pass > 1):
                with dve.Fori(1, n_pass) as p:
                    dve.tensor_scalar(posm, posm, -float(CAP), None, ALU.add)
                    dve.drain()
                    build_slots(p)
                    one_pass(p)
            dve.drain()
            dve.sem_inc(fin_sum, 1)
            dve.wait_ge(glast_in, 16)
            for t in range(NT):
                dve.wait_ge(fin_root, t + 1)
                link(dve.reciprocal(stat[:, 2 + t:3 + t], stat[:, 2 + t:3 + t]))
                for i in range(2):
                    cols = slice(512 * i, 512 * i + 512)
                    dve.scalar_tensor_tensor(out=normed[:, t, cols], in0=x_nat[:, t, cols], scalar=stat[:, 2 + t:3 + t],
                                             in1=g_last[:, cols], op0=ALU.mult, op1=ALU.mult).then_inc(fin_ready, 1)


SM = {}
SMALL = 0
for _name, *_dims in (("ident", P), ("ones", P), ("below", P), ("stream0", P), ("iota", CAP), ("eps", 1), ("limits", MAXPASS - 1),
                      ("rank", NE), ("b_ada", 48), ("g_mix", KD), ("g_ffn", KD), ("lb", 8), ("hg_g", 1),
                      ("gqn", HD), ("gqn_swapped", HD), ("gkn", HD), ("gkn_swapped", HD),
                      ("router_b", ROUTES), ("router", KD, 32), ("cos", NT, HD), ("sin", NT, HD)):
    SM[_name] = (SMALL, _dims)
    SMALL += int(np.prod(_dims))


def columns(v):
    return v.reshape(-1, P).T


def shape_constants():
    f = np.float32
    i = np.arange(P)
    rank = np.arange(NE, 0, -1, dtype=f)
    t = np.arange(L)
    pos = np.stack([t // GRID, t % GRID], axis=-1).astype(f)
    n_freq = HD // 4
    inv = np.power(f(10000.0), -np.arange(n_freq, dtype=f) / f(n_freq)).astype(f)
    ang = (pos[:, :, None] * inv).astype(f)
    cos = np.concatenate([np.cos(ang)] * 2, axis=-1).reshape(NT, P, HD).transpose(1, 0, 2)
    sin = np.concatenate([-np.sin(ang), np.sin(ang)], axis=-1).reshape(NT, P, HD).transpose(1, 0, 2)
    return {
        "ident": np.eye(P, dtype=f), "ones": np.ones((P, P), f),
        "below": (i[:, None] < i[None, :]).astype(f),
        "stream0": np.tile((i[:, None] % 32 == 0).astype(f), (1, P)),
        "iota": np.tile(np.arange(CAP, dtype=f), (P, 1)),
        "eps": np.full((P, 1), EPS, f),
        "limits": np.tile(np.arange(1, MAXPASS, dtype=f) * CAP, (P, 1)),
        "rank": np.tile(rank, (P, 1)), "cos": cos.astype(f), "sin": sin.astype(f),
    }


def level_masks():
    i = np.arange(P)
    out = np.zeros((P, 2 * (LEVELS - 1), P), np.float32)
    for v in range(LEVELS - 1):
        m = 1 << v
        same = (i[:, None] // (2 * m)) == (i[None, :] // (2 * m))
        right = (i // m) % 2 == 1
        out[:, v, :] = same & ~right[:, None] & right[None, :]
        out[:, LEVELS - 1 + v, :] = same & right[:, None] & ~right[None, :]
    return out


def bias_layout(rpb):
    col = np.arange(GRID)
    c0 = np.clip(col - WC // 2, 0, GRID - WC)
    inside = (col[None, :] >= c0[:, None]) & (col[None, :] < c0[:, None] + WC)
    dc = np.where(inside, col[None, :] - col[:, None] + WC - 1, 0)
    out = np.full((P, NH, RB, GRID), NEG, np.float32)
    for half in range(2):
        for i in range(RB):
            dr = i - 2 - half + WR - 1
            rows = rpb[:, dr][:, dc]
            out[half * GRID:(half + 1) * GRID, :, i, :] = np.where(inside[:, None, :], rows.transpose(1, 0, 2), np.float32(NEG))
    return out.reshape(P, NH, RB * GRID)


def weight_slots(w, width=512):
    k, n = w.shape
    s = w.reshape(k // P, P, n // width, width).transpose(2, 1, 0, 3)
    return s.reshape(n // width, P, -1)


def kernel(**inputs):
    import concourse.bacc as bacc
    from concourse.bass_utils import run_bass_kernel_spmd

    a = {k: np.asarray(v) for k, v in inputs.items()}
    x, ctx_ = a["x"][0], a["ctx"][0]
    xc = np.concatenate([x, ctx_], axis=0)
    w_in = a["w_in"][0]
    part = {}
    at_ = 0
    for name, n in (("nq", 512), ("nk", 512), ("nv", 512), ("hq", 512), ("ff", 512), ("fb", 512), ("hi", 512),
                    ("hg", 512), ("gq", 512), ("gkv", 256), ("gate", 3 * D)):
        part[name] = w_in[:, at_:at_ + n]
        at_ += n
    part["gq"] = part["gq"].reshape(D, 2, NH // 2, HD).transpose(0, 2, 1, 3).reshape(D, NH * HD)
    ada = weight_slots(a["w_ada"][0])
    gate = weight_slots(part["gate"])
    front = []
    for name in FRONT:
        if name[:3] == "ada":
            s = ada[int(name[3:])]
        elif name[:4] == "gate":
            s = gate[int(name[4:])]
        elif name == "gkv":
            s = np.zeros((P, SLOT), np.float32)
            s[:, 0:SLOT // 2] = weight_slots(part["gkv"], 256)[0]
        elif name[:2] == "br":
            wb = a["w_branch"][0, int(name[2])]
            if name == "br2":
                wb = wb.reshape(2, NH // 2, HD, D).transpose(1, 0, 2, 3).reshape(BW, D)
            s = weight_slots(wb, D)[0]
        elif name[:3] == "out":
            s = weight_slots(a["w_out"][0])[int(name[3])]
        else:
            s = weight_slots(part[name])[0]
        front.append(s)
    experts = []
    for e in range(NE):
        experts += [weight_slots(a["w_exp_gate"][0, e])[0], weight_slots(a["w_exp_up"][0, e])[0],
                    weight_slots(a["w_exp_down"][0, e], D)[0]]
    small = dict(shape_constants())

    def swapped(g):
        return g.reshape(2, 2, HD // 4)[:, ::-1].reshape(HD)

    small.update({
        "b_ada": columns(a["b_ada"][0]), "g_mix": columns(a["g_mix"][0]), "g_ffn": columns(a["g_ffn"][0]),
        "lb": columns(a["hg_lb_logits"][0].reshape(-1)), "hg_g": columns(a["hg_norm_g"][0]),
        "gqn": np.tile(a["gqa_qnorm_g"][0], (P, 1)), "gqn_swapped": np.tile(swapped(a["gqa_qnorm_g"][0]), (P, 1)),
        "gkn": np.tile(a["gqa_knorm_g"][0], (P, 1)), "gkn_swapped": np.tile(swapped(a["gqa_knorm_g"][0]), (P, 1)),
        "router_b": np.tile(np.concatenate([a["b_group_router"][0], a["b_expert_router"][0]]), (P, 1)),
        "router": np.pad(np.concatenate([a["w_group_router"][0], a["w_expert_router"][0]], axis=1)
                         .reshape(KD, P, ROUTES).transpose(1, 0, 2), ((0, 0), (0, 0), (0, 32 - ROUTES))),
    })
    arrays = {
        "xcT": xc.T.reshape(KD, P, 2 * L).transpose(1, 0, 2),
        "x_nat": x.reshape(NT, P, D).transpose(1, 0, 2),
        "cvec": np.pad(np.stack([a["c"][0], a["c_ctx"]], axis=-1).reshape(KD, P, 2).transpose(1, 0, 2),
                       ((0, 0), (0, 0), (0, 30))),
        "b_rows": np.tile(a["b_ada"][0].reshape(12, 512)[list(ROW_GROUPS)], (P, 1, 1)),
        "front_w": np.stack(front), "expert_w": np.stack(experts),
        "na_bias": bias_layout(a["na_rpb"][0]),
        "small_w": np.concatenate([small[n].reshape(P, -1) for n in SM], axis=1),
        "level_masks": level_masks(),
        "g_last": np.tile(a["g_final"], (P, 1)),
    }
    arrays = {k: np.ascontiguousarray(v) for k, v in arrays.items()}
    nc = bacc.Bacc("TRN2", target_bir_lowering=False, num_devices=1)
    d = {n: nc.dram_tensor(n, v.shape, mybir.dt.from_np(v.dtype), kind="ExternalInput").ap() for n, v in arrays.items()}
    d["out"] = nc.dram_tensor("out", (L, D), F32, kind="ExternalOutput").ap()
    build(nc, d)
    r = run_bass_kernel_spmd(nc, [arrays], core_ids=[0])
    return r.results[0]["out"].reshape(1, L, D)
```
